# Optimizing a Trainium2 kernel written in Bass

```python
import jax, jax.numpy as jnp
from jax import lax
import numpy as np

D_MODEL = 1024
BATCH = 1
SEQ = 128
DEPTH = 1
DEC_BATCH = 1
DEC_SEQ = 512
PAST_LEN = 128

GRID_W = 64
CONV_WIDTH = D_MODEL // 2
DN_HEADS = 4
DN_DK = (D_MODEL // 2) // DN_HEADS
DN_DV = (D_MODEL // 2) // DN_HEADS
DN_KEY = DN_HEADS * DN_DK
DN_VAL = DN_HEADS * DN_DV
CHUNK = 64
D_FF = 2816
N_MOD = 9
EPS = 1e-6
PROJ_DIM = 3 * CONV_WIDTH + 2 * DN_KEY + 2 * DN_VAL + 4 * DN_HEADS
SPLITS = [CONV_WIDTH, 2 * CONV_WIDTH, 3 * CONV_WIDTH,
          3 * CONV_WIDTH + 2 * DN_KEY + DN_VAL,
          3 * CONV_WIDTH + 2 * DN_KEY + 2 * DN_VAL]

kernel_name = "hybrid_conv_gdn_macaron_diffusion_step"

def _rmsnorm(x, g):
    xf = x.astype(jnp.float32)
    y = xf * lax.rsqrt(jnp.mean(xf * xf, axis=-1, keepdims=True) + EPS)
    return (y * g.astype(jnp.float32)).astype(x.dtype)

def _l2norm(x):
    return x * lax.rsqrt(jnp.sum(x * x, axis=-1, keepdims=True) + EPS)

def _conv3(x, w):
    zeros = jnp.zeros_like(x[:, :1])
    prev = jnp.concatenate([zeros, x[:, :-1]], axis=1)
    nxt = jnp.concatenate([x[:, 1:], zeros], axis=1)
    return prev * w[0] + x * w[1] + nxt * w[2]

def _swiglu(h, w_in, w_out):
    a, b = jnp.split(h @ w_in, 2, axis=-1)
    return (jax.nn.silu(a) * b) @ w_out

def _gated_delta(q, k, v, beta, g, s0):
    B, L, H, DK = q.shape
    n = L // CHUNK
    to_c = lambda t: t.reshape(B, n, CHUNK, H, -1).transpose(1, 0, 3, 2, 4)
    to_s = lambda t: t.reshape(B, n, CHUNK, H).transpose(1, 0, 3, 2)
    qc, kc, vc = to_c(q * (DK ** -0.5)), to_c(k), to_c(v)
    bc = to_s(beta)
    gc = jnp.cumsum(to_s(g), axis=-1)
    tril = jnp.tril(jnp.ones((CHUNK, CHUNK), bool))
    strict = jnp.tril(jnp.ones((CHUNK, CHUNK), bool), -1)
    diff = gc[..., :, None] - gc[..., None, :]
    decay = jnp.where(tril, jnp.exp(jnp.where(tril, diff, 0.0)), 0.0)
    kb = kc * bc[..., None]
    lmat = jnp.where(strict, jnp.einsum('nbhcd,nbhed->nbhce', kb, kc) * decay, 0.0)
    eye = jnp.eye(CHUNK, dtype=jnp.float32)
    tmat = lax.linalg.triangular_solve(eye + lmat, jnp.broadcast_to(eye, lmat.shape),
                                       left_side=True, lower=True, unit_diagonal=True)
    u = tmat @ (vc * bc[..., None])
    wk = tmat @ (kb * jnp.exp(gc)[..., None])
    qk = jnp.where(tril, jnp.einsum('nbhcd,nbhed->nbhce', qc, kc) * decay, 0.0)
    qg = qc * jnp.exp(gc)[..., None]
    kg = kc * jnp.exp(gc[..., -1:] - gc)[..., None]
    g_last = jnp.exp(gc[..., -1])

    def step(s, inp):
        qg_i, kg_i, u_i, w_i, qk_i, gl_i = inp
        v_new = u_i - w_i @ s
        o = qg_i @ s + qk_i @ v_new
        s = s * gl_i[..., None, None] + jnp.einsum('bhcd,bhce->bhde', kg_i, v_new)
        return s, o

    s_fin, o = lax.scan(step, s0, (qg, kg, u, wk, qk, g_last))
    o = o.transpose(1, 0, 3, 2, 4).reshape(B, L, H, -1)
    return o, s_fin

def _mixer(h, w_in, conv_w, dn_conv_w, a_log, dt_bias, dn_norm, w_out, s0_fwd, s0_bwd, on_grid):
    B, L, _ = h.shape
    f32 = jnp.float32
    proj = h @ w_in
    cb, cc, ch, qkv, z, ab = jnp.split(proj, SPLITS, axis=-1)
    u = cc * ch
    if on_grid:
        rows = L // GRID_W
        u = _conv3(u.reshape(B, rows, GRID_W, CONV_WIDTH), conv_w).reshape(B, L, CONV_WIDTH)
    else:
        u = _conv3(u, conv_w)
    y_conv = cb * u
    qkv = jax.nn.silu(_conv3(qkv, dn_conv_w))
    q, k, v = jnp.split(qkv, [DN_KEY, 2 * DN_KEY], axis=-1)
    q = _l2norm(q.astype(f32).reshape(B, L, DN_HEADS, DN_DK))
    k = _l2norm(k.astype(f32).reshape(B, L, DN_HEADS, DN_DK))
    v = v.astype(f32).reshape(B, L, DN_HEADS, DN_DV)
    ab = ab.astype(f32).reshape(B, L, 4, DN_HEADS)
    A = jnp.exp(a_log.astype(f32))
    dtb = dt_bias.astype(f32)
    g_f = -A[0] * jax.nn.softplus(ab[:, :, 0] + dtb[0])
    beta_f = jax.nn.sigmoid(ab[:, :, 1])
    g_b = -A[1] * jax.nn.softplus(ab[:, :, 2] + dtb[1])
    beta_b = jax.nn.sigmoid(ab[:, :, 3])
    o_f, s_f = _gated_delta(q, k, v, beta_f, g_f, s0_fwd.astype(f32))
    rev = lambda t: t[:, ::-1]
    o_b, s_b = _gated_delta(rev(q), rev(k), rev(v), rev(beta_b), rev(g_b), s0_bwd.astype(f32))
    o = o_f + rev(o_b)
    o = _rmsnorm(o, dn_norm) * jax.nn.silu(z.astype(f32)).reshape(B, L, DN_HEADS, DN_DV)
    y_dn = o.reshape(B, L, DN_VAL).astype(h.dtype)
    out = jnp.concatenate([y_conv, y_dn], axis=-1) @ w_out
    return out, s_f.astype(h.dtype), s_b.astype(h.dtype)

def _layer(x, mod, s0_fwd, s0_bwd, on_grid, norm_ffn1, w_ffn1_in, w_ffn1_out, norm_mix, w_mix_in, conv_w,
           dn_conv_w, dn_a_log, dn_dt_bias, dn_norm, w_mix_out, norm_ffn2, w_ffn2_in, w_ffn2_out):
    sh1, sc1, gt1, sh2, sc2, gt2, sh3, sc3, gt3 = jnp.split(mod, N_MOD, axis=-1)
    h = _rmsnorm(x, norm_ffn1) * (1 + sc1) + sh1
    x = x + 0.5 * gt1 * _swiglu(h, w_ffn1_in, w_ffn1_out)
    h = _rmsnorm(x, norm_mix) * (1 + sc2) + sh2
    m, s_f, s_b = _mixer(h, w_mix_in, conv_w, dn_conv_w, dn_a_log, dn_dt_bias, dn_norm, w_mix_out,
                         s0_fwd, s0_bwd, on_grid)
    x = x + gt2 * m
    h = _rmsnorm(x, norm_ffn2) * (1 + sc3) + sh3
    x = x + 0.5 * gt3 * _swiglu(h, w_ffn2_in, w_ffn2_out)
    return x, s_f, s_b

def setup_inputs(seed: int = 0) -> dict:
    key = jax.random.key(seed)
    ks = jax.random.split(key, 24)
    nrm = lambda k, shape, s: jax.random.normal(k, shape, jnp.float32) * s
    gain = lambda k, shape: 1.0 + 0.02 * jax.random.normal(k, shape, jnp.float32)
    dt = jnp.exp(jax.random.uniform(ks[15], (DEPTH, 2, DN_HEADS), jnp.float32,
                                    np.log(1e-3), np.log(1e-1)))
    return {
        "x_prompt": nrm(ks[0], (BATCH, SEQ, D_MODEL), 1.0),
        "x_sample": nrm(ks[1], (DEC_BATCH, DEC_SEQ, D_MODEL), 1.0),
        "state_dn_fwd": nrm(ks[2], (DEC_BATCH, DEPTH, DN_HEADS, DN_DK, DN_DV), 1.0),
        "state_dn_bwd": nrm(ks[3], (DEC_BATCH, DEPTH, DN_HEADS, DN_DK, DN_DV), 1.0),
        "c": nrm(ks[4], (DEC_BATCH, D_MODEL), 1.0),
        "c_ctx": nrm(ks[5], (D_MODEL,), 1.0),
        "w_ada": nrm(ks[6], (DEPTH, D_MODEL, N_MOD * D_MODEL), 0.5 * D_MODEL ** -0.5),
        "b_ada": nrm(ks[7], (DEPTH, N_MOD * D_MODEL), 0.02),
        "norm_ffn1": gain(ks[8], (DEPTH, D_MODEL)),
        "w_ffn1_in": nrm(ks[9], (DEPTH, D_MODEL, 2 * D_FF), D_MODEL ** -0.5),
        "w_ffn1_out": nrm(ks[10], (DEPTH, D_FF, D_MODEL), D_FF ** -0.5),
        "norm_mix": gain(ks[11], (DEPTH, D_MODEL)),
        "w_mix_in": nrm(ks[12], (DEPTH, D_MODEL, PROJ_DIM), D_MODEL ** -0.5),
        "conv_w": nrm(ks[13], (DEPTH, 3, CONV_WIDTH), 3 ** -0.5),
        "dn_conv_w": nrm(ks[14], (DEPTH, 3, 2 * DN_KEY + DN_VAL), 3 ** -0.5),
        "dn_a_log": jnp.log(jax.random.uniform(ks[16], (DEPTH, 2, DN_HEADS), jnp.float32, 1.0, 16.0)),
        "dn_dt_bias": dt + jnp.log(-jnp.expm1(-dt)),
        "dn_norm": gain(ks[17], (DEPTH, DN_DV)),
        "w_mix_out": nrm(ks[18], (DEPTH, CONV_WIDTH + DN_VAL, D_MODEL), (CONV_WIDTH + DN_VAL) ** -0.5),
        "norm_ffn2": gain(ks[19], (DEPTH, D_MODEL)),
        "w_ffn2_in": nrm(ks[20], (DEPTH, D_MODEL, 2 * D_FF), D_MODEL ** -0.5),
        "w_ffn2_out": nrm(ks[21], (DEPTH, D_FF, D_MODEL), D_FF ** -0.5),
        "norm_final": gain(ks[22], (D_MODEL,)),
    }

def reference(x_prompt, x_sample, state_dn_fwd, state_dn_bwd, c, c_ctx, w_ada, b_ada, norm_ffn1, w_ffn1_in,
              w_ffn1_out, norm_mix, w_mix_in, conv_w, dn_conv_w, dn_a_log, dn_dt_bias, dn_norm, w_mix_out,
              norm_ffn2, w_ffn2_in, w_ffn2_out, norm_final):
    xp, xs = x_prompt, x_sample
    nb = xp.shape[0]
    zero_state = jnp.zeros((nb, DN_HEADS, DN_DK, DN_DV), jnp.float32)
    new_f, new_b = [], []
    for l in range(DEPTH):
        lw = (norm_ffn1[l], w_ffn1_in[l], w_ffn1_out[l], norm_mix[l], w_mix_in[l], conv_w[l], dn_conv_w[l],
              dn_a_log[l], dn_dt_bias[l], dn_norm[l], w_mix_out[l], norm_ffn2[l], w_ffn2_in[l], w_ffn2_out[l])
        mod_ctx = (jax.nn.silu(c_ctx) @ w_ada[l] + b_ada[l])[None, None, :]
        mod_lat = (jax.nn.silu(c) @ w_ada[l] + b_ada[l])[:, None, :]
        xp, sf, sb = _layer(xp, mod_ctx, zero_state, zero_state, False, *lw)
        new_f.append(sf)
        new_b.append(sb)
        xs, _, _ = _layer(xs, mod_lat, state_dn_fwd[:, l], state_dn_bwd[:, l], True, *lw)
    y_prompt = _rmsnorm(xp, norm_final)
    y_sample = _rmsnorm(xs, norm_final)
    new_state_dn_fwd = jnp.stack(new_f, axis=1)
    new_state_dn_bwd = jnp.stack(new_b, axis=1)
    return (y_prompt, y_sample, new_state_dn_fwd, new_state_dn_bwd)


_drawn_inputs = setup_inputs


def setup_inputs(seed=0):
    import zlib

    import numpy as np

    out = dict(_drawn_inputs(seed))
    spreads = {}
    factors = {'state_dn_bwd': 2.887,
     'norm_ffn1': 8.0,
     'dn_norm': 64.0,
     'norm_ffn2': 21.738,
     'norm_final': 7.935}
    for name, (base, spread) in spreads.items():
        noise = np.random.default_rng([zlib.crc32(name.encode()), seed]).standard_normal(out[name].shape)
        drawn = base * np.exp(spread * noise) if base else spread * noise
        out[name] = __import__('jax').numpy.asarray(drawn.astype(out[name].dtype))
    for name, factor in factors.items():
        out[name] = (out[name] * factor).astype(out[name].dtype)
    return out
```

```python
from contextlib import ExitStack

import numpy as np

import concourse.bass as bass
from concourse import mybir

F32 = mybir.dt.float32
F32R = mybir.dt.float32r
BF16 = mybir.dt.bfloat16
ALU = mybir.AluOpType
ACT = mybir.ActivationFunctionType

P = 128
D = 1024
KD = D // P
TP, TS = 128, 512
T = TP + TS
TH = T // 2
NC = T // P
FF = 2816
KF = FF // P
KH = KF // 2
HEADS = 4
CW = D // 2
QKV0 = 3 * CW
Z0 = QKV0 + 3 * CW
AB0 = Z0 + CW
NAB = 4 * HEADS
LEVELS = 7
GRID_W = 64
EPS = 1e-6
NEG = -1e30

U_F1I = 0
U_F1O = U_F1I + 2 * KF
U_MI = U_F1O + 2 * KD
U_MO = U_MI + 28
U_F2I = U_MO + KD
U_F2O = U_F2I + 2 * KF
U_END = U_F2O + 2 * KD
A_F1I = 0
A_F1O = A_F1I + 2 * KF
A_MI = A_F1O + KD
A_MO = A_MI + 28
A_F2I = A_MO + KD
A_F2O = A_F2I + 2 * KF

R_CTX, R_C, R_N1, R_NM, R_N2, R_NF, R_CONV, R_DNC, R_DNN = 0, 8, 16, 24, 32, 40, 48, 60, 96
NROWS = 97
C_ID, C_TRI, C_LEV, C_NEG = 0, P, 3 * P, 3 * P + 2 * LEVELS * P
NCONST = C_NEG + 2 * P


def constants():
    j, i = np.meshgrid(np.arange(P), np.arange(P), indexing="ij")
    out = np.zeros((P, NCONST), np.float32)
    out[:, C_ID:C_ID + P] = i == j
    for d in range(2):
        a, b = (j, i) if d == 0 else (i, j)
        out[:, C_TRI + d * P:C_TRI + (d + 1) * P] = a <= b
        for s in range(LEVELS):
            joined = (a >> s) + 1 == (b >> s)
            c = C_LEV + (d * LEVELS + s) * P
            out[:, c:c + P] = -1.0 * (joined & ((b >> s) % 2 == 1))
        out[:, C_NEG + d * P:C_NEG + (d + 1) * P] = np.where(a <= b, 0.0, NEG)
    return out


def hybrid_layer(nc, x_prompt, x_sample, state_f, state_b, c, c_ctx, w_ada, b_ada, norm1, w1i, w1o, norm_mix,
                 w_mi, conv_w, dn_conv_w, a_log, dt_bias, dn_norm, w_mo, norm2, w2i, w2o, norm_f, consts,
                 y_prompt, y_sample, s_out_f, s_out_b):
    ctx = ExitStack()
    with ctx:
        sem = lambda name: ctx.enter_context(nc.semaphore(name))
        place = {"at": 16512}

        def sb(name, shape, dt, at=None):
            size = int(np.prod(shape[1:])) * (2 if dt == BF16 else 4)
            if at is None:
                at = place["at"]
                place["at"] += (size + 31) // 32 * 32
            return nc.alloc_sbuf_tensor_at(name, shape, dt, offset=at)

        x = sb("x", [P, KD, T], F32)
        at_h = place["at"]
        h_hi = sb("h_hi", [P, KD, T], F32R)
        h_lo = sb("h_lo", [P, KD, T], F32R)
        at_g = place["at"]
        g_hi = sb("g_hi", [P, KF, T], F32R)
        g_lo = sb("g_lo", [P, KF, T], F32R)
        w_raw = sb("w_raw", [P, 2, KH * P], F32)
        w_hi = sb("w_hi", [P, 2, KH * P], F32R)
        w_lo = sb("w_lo", [P, 2, KH * P], F32R)
        sa = sb("sa", [P, T], F32)
        mod = sb("mod", [P, 9 * KD, 2], F32)
        gain = sb("gain", [P, 3, KD, 2], F32)
        gate = sb("gate", [P, 3, KD, 2], F32)
        vec = sb("vec", [P, NROWS], F32)
        bada = sb("bada", [P, 9 * KD], F32)
        ident = sb("ident", [P, P], F32)
        ones = sb("ones", [P, 1], F32)
        eps = sb("eps", [P, 1], F32)
        assert place["at"] <= 229344, place["at"]
        ones_t = ones[:, 0:1].to_broadcast([P, P])

        KB = 1024
        xin = sb("xin", [P, NC, D], F32, at=at_g)
        vrow = sb("vrow", [NROWS, P], F32, at=at_g + 20 * KB)
        brow = sb("brow", [9 * KD, P], F32, at=at_g + 20 * KB + 512)
        at_ada = at_g + (KF + 8) * 4 * T
        ADA = 4
        ada_w = sb("ada_w", [P, ADA, 2048], F32, at=at_ada)
        ada_r = sb("ada_r", [P, 512], F32, at=at_ada + ADA * 8 * KB)
        ccol = sb("ccol", [P, KD, 32], F32, at=at_ada + ADA * 8 * KB + 2048)
        assert at_ada + ADA * 8 * KB + 2048 + 1024 <= at_g + 2 * KF * 4 * T
        rinv = sb("rinv", [P, T], F32, at=at_g + 20 * KB)
        tn = sb("tn", [P, KD, T], F32, at=at_g)
        hf = sb("hf", [P, KD, T], F32, at=at_g + 24 * KB)
        B = 4 * T
        qkv = sb("qkv", [P, 12, T], F32, at=at_g)
        zs = sb("zs", [P, 4, T], F32, at=at_g + 12 * B)
        yc = sb("yc", [P, 4, T], F32, at=at_g + 16 * B)
        ot = sb("ot", [P, HEADS, T], F32, at=at_g + 20 * B)
        wab = sb("wab", [P, KD, NAB], F32, at=at_g + 20 * B)
        wab_hi = sb("wab_hi", [P, KD, NAB], F32R, at=at_g + 20 * B + 512)
        wab_lo = sb("wab_lo", [P, KD, NAB], F32R, at=at_g + 20 * B + 1024)
        ktok = sb("ktok", [P, NC, CW], F32, at=at_g + 24 * B)
        vtok = sb("vtok", [P, NC, CW], F32, at=at_g + 28 * B)
        ss = sb("ss", [P, 8, T], F32, at=at_g + 32 * B)
        cc = sb("cc", [P, T], F32, at=at_g + 40 * B)
        uu = sb("uu", [P, T], F32, at=at_g + 41 * B)
        cv = sb("cv", [P, T], F32, at=at_g + 42 * B)
        lev = sb("lev", [P, 2 * LEVELS, P], F32, at=at_g + 40 * B)
        tri = sb("tri", [P, 2, P], F32, at=at_g + 43 * B)
        negb = sb("negb", [P, 2, P], BF16, at=at_g + 43 * B + 1024)
        identb = sb("identb", [P, P], BF16, at=at_g + 43 * B + 1536)
        spots = [at_h + 2048 * i for i in range(20)] + [at_g + 32 * B + 2048 * i for i in range(10)] + \
                [at_g + 8 * B + 2048 * i for i in range(5)]
        small = spots.pop(0)
        negf = sb("negf", [P, 2, P], F32, at=small)
        gsm = {}
        off = small + 1024
        for name, width in (("ab", NC * NAB), ("adt", 16)):
            gsm[name] = sb(name, [P, width], F32, at=off)
            off += 4 * width
        off = spots.pop(0)
        for name in ("g", "beta", "gc", "ngc", "eg", "gt", "gl", "kgs", "t1", "t2", "t3"):
            gsm[name] = sb("s_" + name, [P, 2, NC, HEADS], F32, at=off)
            off += 160
        per = lambda name: [sb(f"{name}{d}", [P, HEADS, P], F32, at=spots.pop(0)) for d in range(2)]
        DT = per("DT")
        gtri = DT
        Erow = per("Erow")
        WT = Erow
        LT, NTa, NTb, Tm, Rm, Xm = per("LT"), per("NTa"), per("NTb"), per("Tm"), per("Rm"), per("Xm")
        QK, ke, kg, qg, VN = per("QK"), per("ke"), per("kg"), per("qg"), per("VN")
        Sa, Sb, Sc = per("Sa"), per("Sb"), per("Sc")
        osq = sb("osq", [P, T], F32, at=at_g + 24 * B)
        orr = sb("orr", [P, HEADS, T], F32, at=at_g + 32 * B)

        ssq_h = sb("ssq_h", [P, T], F32, at=at_h)
        ssq_g = sb("ssq_g", [P, T], F32, at=at_g + 38 * B)
        sq_h = sb("sq_h", [P, T], F32, at=at_h + B)
        sq_g = sb("sq_g", [P, T], F32, at=at_g + 39 * B)
        xg = sb("xg", [P, 2, T], F32, at=at_h + 2 * B)
        rfin = sb("rfin", [P, NC], F32, at=at_h + 5 * B)
        yo = sb("yo", [P, NC, D], F32, at=at_h + 8 * B)

        ps = [ctx.enter_context(nc.psum_tensor(f"ps{i}", [P, 512], F32)) for i in range(8)]
        acc = [[ps[2 * s][:, 0:TH], ps[2 * s + 1][:, 0:TH]] for s in range(2)]
        sums = [ps[4][:, 0:TH], ps[5][:, 0:TH]]
        adap, adat = ps[6], ps[7]

        in_x, in_vec, in_b, in_id, in_wab, in_adt, in_tri, in_lev = (sem(n) for n in (
            "in_x", "in_vec", "in_b", "in_id", "in_wab", "in_adt", "in_tri", "in_lev"))
        in_s = [sem(f"in_s{d}") for d in range(2)]
        w_in = [sem(f"w_in{s}") for s in range(2)]
        hi_ready, lo_ready, mm_done = sem("hi_ready"), sem("lo_ready"), sem("mm_done")
        acc_free = [sem(f"acc_free{s}") for s in range(2)]
        ada_in = [sem(f"ada_in{s}") for s in range(ADA)]
        ada_mm, ada_row, ada_tr, mod_rdy = sem("ada_mm"), sem("ada_row"), sem("ada_tr"), sem("mod_rdy")
        misc_set, vec_tr, vec_rdy, c_rdy = sem("misc_set"), sem("vec_tr"), sem("vec_rdy"), sem("c_rdy")
        x_tr, x_evA, x_evB = sem("x_tr"), sem("x_evA"), sem("x_evB")
        sq_rdy, ssq_rdy, sum_mm, rt_rdy, r_rdy = (sem(n) for n in ("sq_rdy", "ssq_rdy", "sum_mm", "rt_rdy", "r_rdy"))
        tn_rdy, tnp_rdy, hh_rdy, hf_rdy, h_rdy = (sem(n) for n in ("tn_rdy", "tnp_rdy", "hh_rdy", "hf_rdy", "h_rdy"))
        sa_rdy, gp_rdy, gh_rdy, g_rdy = sem("sa_rdy"), sem("gp_rdy"), sem("gh_rdy"), sem("g_rdy")
        x_upd = sem("x_upd")
        dve_step = sem("dve_step")
        gain_rdy = sem("gain_rdy")

        def seq(engine):
            count = [0]

            def link(instruction):
                count[0] += 1
                instruction.then_inc(dve_step, 1)
                engine.wait_ge(dve_step, count[0])
            return link

        cv_rdy, qs_rdy, q2_rdy, ssm, ss_rdy, st_rdy, sr_rdy, qn_rdy = (sem(n) for n in (
            "cv_rdy", "qs_rdy", "q2_rdy", "ssm", "ss_rdy", "st_rdy", "sr_rdy", "qn_rdy"))
        cc_rdy, u_rdy, uc_rdy, y_rdy, z_rdy = (sem(n) for n in ("cc_rdy", "u_rdy", "uc_rdy", "y_rdy", "z_rdy"))
        wab_h, wab_rdy, ab_mm, ab_ev, ab_tr, ab_rdy = (sem(n) for n in (
            "wab_h", "wab_rdy", "ab_mm", "ab_ev", "ab_tr", "ab_rdy"))
        tok_tr, tok_evA, tok_evB = sem("tok_tr"), sem("tok_evA"), sem("tok_evB")
        act_g, dve_g, gsum, gates = sem("act_g"), sem("dve_g"), sem("gsum"), sem("gates")
        pair = lambda n: [sem(f"{n}{d}") for d in range(2)]
        gtri_rdy, row_rdy, erow_rdy, rowm, kk_rdy, dt_rdy, lt_rdy, qk_rdy = (pair(n) for n in (
            "gtri_rdy", "row_rdy", "erow_rdy", "rowm", "kk_rdy", "dt_rdy", "lt_rdy", "qk_rdy"))
        nt_rdy, x_mm, xm_rdy, tr_mm, t_rdy, rr_rdy = (pair(n) for n in (
            "nt_rdy", "x_mm", "xm_rdy", "tr_mm", "t_rdy", "rr_rdy"))
        ke_rdy, kg_rdy, qg_rdy, w_mm, wt_rdy, v_mm, vn_rdy, o_mm, o_read, s_mm, s_rdy = (pair(n) for n in (
            "ke_rdy", "kg_rdy", "qg_rdy", "w_mm", "wt_rdy", "v_mm", "vn_rdy", "o_mm", "o_read", "s_mm", "s_rdy"))
        osq_rdy, osum, ort_rdy, orr_rdy, on_rdy, yh_rdy, yf_rdy, yl_rdy = (sem(n) for n in (
            "osq_rdy", "osum", "ort_rdy", "orr_rdy", "on_rdy", "yh_rdy", "yf_rdy", "yl_rdy"))
        xg_rdy, y_tr, y_ev, y_sum, y_rt, y_r, y_fin, out_done, st_done = (sem(n) for n in (
            "xg_rdy", "y_tr", "y_ev", "y_sum", "y_rt", "y_r", "y_fin", "out_done", "st_done"))
        zero_s = sem("zero_s")

        GROUPS = ((0, 0, TP), (1, TP, T))
        PIECES = ((0, 0, TP, 0, 0), (0, TP, TH, 1, TP), (1, 0, TH, 1, TH))

        def tn_wait(m, k):
            if m == 0:
                return (tn_rdy, k // 2 + 1) if k % 2 == 0 else (tnp_rdy, k // 2 + 1)
            return (tn_rdy, KD // 2 + m) if k == 0 else (tnp_rdy, KD // 2 + (KD - 1) * (m - 1) + k)

        def halves(t2):
            return t2.rearrange("p (a b) -> p a b", a=2)

        block = ctx.enter_context(nc.Block())

        @block.sync
        def _(sp):
            sp.dma_start(xin[:, 0, :], x_prompt[0]).then_inc(in_x, 16)
            sp.dma_start(xin[:, 1:NC, :], x_sample[0].rearrange("(c p) f -> p c f", p=P)).then_inc(in_x, 16)

            def load_w(u, slot, src, kt, wait=True):
                if wait:
                    sp.wait_ge(lo_ready, u - 1)
                sp.dma_start(w_raw[:, slot, 0:kt * P].rearrange("p (k f) -> p k f", k=kt),
                             src).then_inc(w_in[slot], 16)

            ada_v = w_ada[0].rearrange("(k p) f -> p k f", p=P)

            def load_ada(n, s, k, col, width):
                if not (isinstance(n, int) and n < ADA):
                    sp.wait_ge(ada_mm, n - ADA + 1)
                sp.dma_start(ada_w[:, s, 0:width], ada_v[:, k, bass.ds(col, width)]).then_inc(ada_in[s], 16)

            w_in_v = [w[0].rearrange("(k p) f -> p k f", p=P) for w in (w1i, w2i)]
            w_out_v = [w[0].rearrange("(k p) f -> p k f", p=P) for w in (w1o, w2o)]
            sp.wait_ge(in_vec, 9 * 16)
            sp.wait_ge(in_b, 16)
            for k in range(KD):
                load_ada(k, k % ADA, k, 0, 2048)
            for u in range(2):
                load_w(u, u, w_in_v[0][:, :, u * FF:u * FF + P], KD, wait=False)

            with sp.Fori(0, 3) as s:
                for half in range(2):
                    for k in range(4):
                        load_ada(8 * s + (8 + 4 * half + k), k, 4 * half + k, 2048 * s + 2048, 2048)
                    i = 2 * s + half + 1
                    for b in range(2):
                        load_w(2 * i + b, b, w_in_v[0][:, :, bass.ds(P * i + b * FF, P)], KD)
            for half in range(2):
                for k in range(4):
                    load_ada(32 + 4 * half + k, k, 4 * half + k, 8192, 1024)
                i = 7 + half
                for b in range(2):
                    load_w(2 * i + b, b, w_in_v[0][:, :, P * i + b * FF:P * i + b * FF + P], KD)
            with sp.Fori(9, KF) as i:
                for b in range(2):
                    load_w(2 * i + b, b, w_in_v[0][:, :, bass.ds(P * i + b * FF, P)], KD)
            with sp.Fori(0, KD) as j:
                for b in range(2):
                    load_w(U_F1O + 2 * j + b, b, w_out_v[0][:, KH * b:KH * b + KH, bass.ds(P * j, P)], KH)

            w_mi_v = w_mi[0].rearrange("(k p) f -> p k f", p=P)
            with sp.Fori(0, 8) as i:
                for b in range(2):
                    load_w(U_MI + 2 * i + b, b, w_mi_v[:, :, bass.ds(QKV0 + 2 * P * i + b * P, P)], KD)
            sp.wait_ge(mm_done, U_MI)
            sp.dma_start(wab[:, :, :], w_mi_v[:, :, AB0:AB0 + NAB]).then_inc(in_wab, 16)
            sp.dma_start(tri[:, :, :], consts[:, C_TRI:C_TRI + 2 * P].rearrange("p (a b) -> p a b", a=2)
                         ).then_inc(in_tri, 16)
            for n in range(12):
                col = {0: CW, 1: 2 * CW, 2: 0}[n % 3] + P * (n // 3)
                load_w(U_MI + 16 + n, n % 2, w_mi_v[:, :, col:col + P], KD)
            sp.wait_ge(y_rdy, 4)
            sp.dma_start(lev[:, :, :], consts[:, C_LEV:C_LEV + 2 * LEVELS * P].rearrange("p (a b) -> p a b", b=P)
                         ).then_inc(in_lev, 16)
            sp.wait_ge(ab_mm, 1)
            sp.dma_start(negf[:, :, :], consts[:, C_NEG:C_NEG + 2 * P].rearrange("p (a b) -> p a b", a=2)
                         ).then_inc(in_lev, 16)
            sp.dma_start(gsm["adt"][:, 0:8], a_log.rearrange("a b h -> a (b h)").to_broadcast([P, 8])
                         ).then_inc(in_adt, 16)
            sp.dma_start(gsm["adt"][:, 8:16], dt_bias.rearrange("a b h -> a (b h)").to_broadcast([P, 8])
                         ).then_inc(in_adt, 16)
            sp.wait_ge(qn_rdy, 8)
            sp.wait_ge(tok_tr, 10)
            for d, state in enumerate((state_f, state_b)):
                sp.dma_start(Sc[d][:, :, :], state[0, 0].rearrange("h k v -> k h v")).then_inc(in_s[d], 16)
            w_mo_v = w_mo[0].rearrange("(k p) f -> p k f", p=P)
            for j in range(KD):
                load_w(U_MO + j, j % 2, w_mo_v[:, :, P * j:P * j + P], KD)
            with sp.Fori(0, KF) as i:
                for b in range(2):
                    load_w(U_F2I + 2 * i + b, b, w_in_v[1][:, :, bass.ds(P * i + b * FF, P)], KD)
            with sp.Fori(0, KD) as j:
                for b in range(2):
                    load_w(U_F2O + 2 * j + b, b, w_out_v[1][:, KH * b:KH * b + KH, bass.ds(P * j, P)], KH)
            for t in range(NC):
                sp.wait_ge(y_fin, t + 1)
                dst = y_prompt[0] if t == 0 else y_sample[0, (t - 1) * P:t * P, :]
                sp.dma_start(dst, yo[:, t, :]).then_inc(out_done, 16)
            sp.wait_ge(out_done, 16 * NC)
            sp.wait_ge(st_done, 32)

        @block.tensor
        def _(pe):
            def unit(u, slot, kt, hi, lo, a_slot, start=True, stop=True, k0=0, h_wait=None, ready=True):
                pe.wait_ge(lo_ready, u + 1)
                for k in range(kt):
                    if h_wait is not None:
                        pe.wait_ge(*h_wait(k))
                    wh = w_hi[:, slot, k * P:k * P + P]
                    wl = w_lo[:, slot, k * P:k * P + P]
                    for n, (w, m) in enumerate(((wh, hi), (wh, lo), (wl, hi))):
                        for b in range(2):
                            last = pe.matmul(acc[a_slot][b], w, m[:, k0 + k, b * TH:b * TH + TH],
                                             start=start and k == 0 and n == 0,
                                             stop=stop and k == kt - 1 and n == 2)
                last.then_inc(mm_done, 1)

            def acc_wait(a_half, slot):
                if not (isinstance(a_half, int) and a_half == 0):
                    pe.wait_ge(acc_free[slot], a_half)

            def sum_squares(m, src):
                pe.wait_ge(ssq_rdy, KD * (m + 1))
                for b in range(2):
                    last = pe.matmul(sums[b], ones_t, src[:, b * TH:b * TH + TH], start=True, stop=True)
                last.then_inc(sum_mm, 1)

            pe.wait_ge(in_id, 16)
            pe.wait_ge(in_vec, 9 * 16)
            pe.wait_ge(in_b, 16)
            pe.transpose(ps[0][:, 0:NROWS], vrow[:, :], ident[0:NROWS, 0:NROWS])
            pe.transpose(ps[0][:, P:P + 9 * KD], brow[:, :], ident[0:9 * KD, 0:9 * KD]).then_inc(vec_tr, 1)
            pe.wait_ge(in_x, 32)
            for n in range(10):
                if n >= 2:
                    pe.wait_ge((x_evA, x_evB)[n % 2], n // 2)
                for m in range(4):
                    k, t = divmod(4 * n + m, NC)
                    last = pe.transpose(ps[2 + n % 2][:, m * P:m * P + P], xin[:, t, k * P:k * P + P], ident[:, :])
                last.then_inc(x_tr, 1)

            def ada_step(n, s, k, width):
                pe.wait_ge(ada_in[s], 16 * (n // ADA + 1) if isinstance(n, int) else n)
                for g in range(4):
                    last = pe.matmul(adap[32 * g:32 * g + 32, 0:width], ccol[:, k, :],
                                     ada_w[:, s, g * width:(g + 1) * width], start=k == 0, stop=k == KD - 1)
                last.then_inc(ada_mm, 1)

            def ada_turn(n, blocks):
                pe.wait_ge(ada_row, n + 1)
                if not (isinstance(n, int) and n == 0):
                    pe.wait_ge(mod_rdy, n)
                for b in range(blocks):
                    last = pe.transpose(adat[:, b * P:b * P + P], ada_r[:, b * P:b * P + P], ident[:, :])
                last.then_inc(ada_tr, 1)

            pe.wait_ge(c_rdy, 1)
            for k in range(KD):
                ada_step(k, k % ADA, k, 512)
                if k == 3:
                    sum_squares(0, ssq_h)
            ada_turn(0, 4)

            def first_pair(u0, a0, h0):
                for b in range(2):
                    acc_wait(a0 // 2, b)
                    pe.wait_ge(lo_ready, u0 + b + 1)
                for k in range(KD):
                    pe.wait_ge(h_rdy, h0 + k + 1)
                    for s in range(2):
                        wh, wl = (w[:, s, k * P:k * P + P] for w in (w_hi, w_lo))
                        for n, (w, m) in enumerate(((wh, h_hi), (wh, h_lo), (wl, h_hi))):
                            for b in range(2):
                                last = pe.matmul(acc[s][b], w, m[:, k, b * TH:b * TH + TH],
                                                 start=k == 0 and n == 0, stop=k == KD - 1 and n == 2)
                        if k == KD - 1:
                            last.then_inc(mm_done, 1)

            def swiglu_in(i, u0, a0, kt_next=None, extra=(), h_wait=None):
                if h_wait is not None:
                    first_pair(u0, a0, h_wait)
                    for step in extra:
                        step()
                    return
                for b in range(2):
                    acc_wait(a0 // 2 + i, b)
                    unit(u0 + 2 * i + b, b, KD, h_hi, h_lo, b)
                    for step in extra[2 * b:2 * b + 2]:
                        step()

            def with_ada(i, s, half, n_of, width, first_wait=None):
                steps = []
                for k in range(4):
                    kk = 4 * half + k
                    steps.append(lambda kk=kk, k=k: ada_step(n_of(kk), k, kk, width))
                swiglu_in(i, U_F1I, A_F1I, extra=steps, h_wait=first_wait)

            def slab(s, first=False):
                for half in range(2):
                    with_ada(2 * s + half, s, half,
                             (lambda kk: 8 * (s + 1) + kk) if isinstance(s, int) else
                             (lambda kk: 16 * (2 * s + 3 + kk // 4)), 512 if not isinstance(s, int) or s < 3 else 256,
                             0 if first and half == 0 else None)
            slab(0, first=True)
            ada_turn(1, 4)
            with pe.Fori(1, 3) as s:
                slab(s)
                ada_turn(s + 1, 4)
            slab(3)
            ada_turn(4, 2)
            with pe.Fori(8, KF) as i:
                swiglu_in(i, U_F1I, A_F1I)

            def swiglu_out(u0, a0, g0, after=lambda j: None):
                for j in range(KD):
                    s = j % 2
                    acc_wait(a0 // 2 + j // 2, s)
                    for b in range(2):
                        unit(u0 + 2 * j + b, b, KH, g_hi, g_lo, s, start=b == 0, stop=b == 1, k0=KH * b,
                             h_wait=(lambda k, b=b: (g_rdy, g0 + KH * b + k + 1)) if j == 0 else None)
                    after(j)

            swiglu_out(U_F1O, A_F1O, 0)
            sum_squares(1, ssq_h)

            first_pair(U_MI, A_MI, KD)
            for n in range(1, 28):
                if n > 1:
                    acc_wait(A_MI // 2 + n // 2, n % 2)
                    unit(U_MI + n, n % 2, KD, h_hi, h_lo, n % 2)
                if 1 <= n <= 8:
                    pe.wait_ge(q2_rdy, n)
                    if n > 1:
                        pe.wait_ge(ss_rdy, n - 1)
                    for b in range(2):
                        last = pe.matmul(sums[b], ones_t, sa[:, b * TH:b * TH + TH], start=True, stop=True)
                    last.then_inc(ssm, 1)
            pe.wait_ge(wab_rdy, 1)
            pe.wait_ge(ss_rdy, 8)
            for k in range(KD):
                for n, (w, m) in enumerate(((wab_hi, h_hi), (wab_hi, h_lo), (wab_lo, h_hi))):
                    for b in range(2):
                        last = pe.matmul(sums[b][0:NAB, :], w[:, k, :], m[:, k, b * TH:b * TH + TH],
                                         start=k == 0 and n == 0, stop=k == KD - 1 and n == 2)
            last.then_inc(ab_mm, 1)
            pe.wait_ge(ab_ev, 1)
            for t in range(NC):
                last = pe.transpose(ps[6][:, t * NAB:(t + 1) * NAB], sa[0:NAB, t * P:t * P + P], ident[0:NAB, 0:NAB])
            last.then_inc(ab_tr, 1)
            for n in range(10):
                t, isv = divmod(n, 2)
                if not isv and t == 0:
                    pe.wait_ge(qn_rdy, 8)
                if n == 0:
                    pe.wait_ge(qs_rdy, 12)
                if n < 2:
                    acc_wait(A_MO // 2, 0)
                else:
                    pe.wait_ge((tok_evA, tok_evB)[n % 2], n // 2)
                for h in range(HEADS):
                    last = pe.transpose(ps[n % 2][:, h * P:h * P + P],
                                        qkv[:, (8 if isv else 4) + h, t * P:t * P + P], ident[:, :])
                last.then_inc(tok_tr, 1)
            pe.wait_ge(dve_g, 1)
            pe.wait_ge(in_tri, 16)
            for d in range(2):
                gv = gsm["g"][:, d].rearrange("p c h -> p (c h)")
                pe.matmul(ps[7][:, 32 * d:32 * d + 20], tri[:, d, :], gv, start=True, stop=True)
                last = pe.matmul(ps[7][:, 64 + 32 * d:64 + 32 * d + 20], ones_t, gv, start=True, stop=True)
            last.then_inc(gsum, 1)

            acc_wait(A_MO // 2, 1)
            pe.wait_ge(tok_evA, 5)
            pe.wait_ge(tok_evB, 5)
            pe.wait_ge(gates, 1)
            pe.wait_ge(in_lev, 32)
            bank = [[ps[4 * d + i] for i in range(4)] for d in range(2)]
            hs = lambda t, h: t[:, h * P:h * P + P]

            def chunk(n, d):
                return n if n == 0 or d == 0 else NC - n

            def row(n, d):
                pe.wait_ge(gtri_rdy[d], n + 1)
                if n == 1:
                    pe.wait_ge(t_rdy[d], 6)
                elif n > 1:
                    pe.wait_ge(wt_rdy[d], n - 1)
                pe.matmul(bank[d][0][:, :], ones_t, gtri[d][:, :, :], start=True, stop=True).then_inc(row_rdy[d], 1)

            def products(n, d):
                t = chunk(n, d) * P
                if n > 0:
                    pe.wait_ge(vn_rdy[d], n)
                    pe.wait_ge(o_read[d], n)
                for h in range(HEADS):
                    kt = qkv[:, 4 + h, t:t + P]
                    pe.matmul(hs(bank[d][1], h), kt, kt, start=True, stop=True)
                    last = pe.matmul(hs(bank[d][2], h), kt, qkv[:, h, t:t + P], start=True, stop=True)
                last.then_inc(kk_rdy[d], 1)

            def mask_row(n, d):
                pe.wait_ge(erow_rdy[d], n + 1)
                pe.matmul(bank[d][0][:, :], identb[:, :], negb[:, d:d + 1, :].to_broadcast([P, HEADS, P]),
                          start=False, stop=True, skip_group_check=True).then_inc(rowm[d], 1)

            def level0(n, d):
                pe.wait_ge(nt_rdy[d], 7 * n + 1)
                if n > 0:
                    pe.wait_ge(s_rdy[d], n)
                for h in range(HEADS):
                    last = pe.matmul(hs(bank[d][3], h), NTa[d][:, h, :], ident[:, :], start=True, stop=True)
                last.then_inc(x_mm[d], 1)

            def level_x(n, d, s):
                pe.wait_ge(nt_rdy[d], 7 * n + s + 1)
                pe.wait_ge(t_rdy[d], 6 * n + s)
                if s == 1:
                    pe.wait_ge(lt_rdy[d], n + 1)
                nt = (NTa, NTb)[s % 2][d]
                for h in range(HEADS):
                    last = pe.matmul(hs(bank[d][1], h), nt[:, h, :], Tm[d][:, h, :], start=True, stop=True)
                last.then_inc(x_mm[d], 1)

            def level_tr(n, d, s):
                pe.wait_ge(xm_rdy[d], 6 * n + s)
                pe.wait_ge(rr_rdy[d], 7 * n + s)
                if s == 1:
                    pe.wait_ge(dt_rdy[d], n + 1)
                    pe.wait_ge(qk_rdy[d], n + 1)
                for h in range(HEADS):
                    if s < LEVELS - 1:
                        pe.matmul(hs(bank[d][0], h), Rm[d][:, h, :], Xm[d][:, h, :], start=True, stop=True)
                    last = pe.matmul(hs(bank[d][2], h), Xm[d][:, h, :], Rm[d][:, h, :], start=True, stop=True)
                last.then_inc(tr_mm[d], 1)

            def w_product(n, d):
                pe.wait_ge(rr_rdy[d], 7 * n + 7)
                pe.wait_ge(ke_rdy[d], n)
                pe.wait_ge(t_rdy[d], 6 * n + 6)
                for h in range(HEADS):
                    last = pe.matmul(hs(bank[d][0], h), ke[d][:, h, :], Rm[d][:, h, :], start=True, stop=True)
                last.then_inc(w_mm[d], 1)

            def v_product(n, d, s_in):
                c0 = chunk(n, d)
                pe.wait_ge(rr_rdy[d], 7 * n + 7)
                pe.wait_ge(xm_rdy[d], 6 * n + 6)
                for h in range(HEADS):
                    last = pe.matmul(hs(bank[d][1], h), Rm[d][:, h, :], hs(vtok[:, c0, :], h),
                                     start=True, stop=n == 0)
                    if n > 0:
                        if h == 0:
                            pe.wait_ge(wt_rdy[d], n)
                            if n == 1:
                                pe.wait_ge(in_s[d], 16)
                            else:
                                pe.wait_ge(s_rdy[d], n)
                        last = pe.matmul(hs(bank[d][1], h), WT[d][:, h, :], s_in[:, h, :], start=False, stop=True)
                last.then_inc(v_mm[d], 1)

            def s_product(n, d):
                pe.wait_ge(vn_rdy[d], n + 1)
                pe.wait_ge(kg_rdy[d], n + 1)
                pe.wait_ge(t_rdy[d], 6 * n + 1)
                for h in range(HEADS):
                    last = pe.matmul(hs(bank[d][3], h), kg[d][:, h, :], VN[d][:, h, :], start=True, stop=True)
                last.then_inc(s_mm[d], 1)

            def o_product(n, d, s_in):
                pe.wait_ge(vn_rdy[d], n + 1)
                pe.wait_ge(rr_rdy[d], 7 * n + 7)
                if n > 0:
                    pe.wait_ge(qg_rdy[d], n)
                for h in range(HEADS):
                    last = pe.matmul(hs(bank[d][2], h), VN[d][:, h, :], QK[d][:, h, :], start=True, stop=n == 0)
                    if n > 0:
                        last = pe.matmul(hs(bank[d][2], h), s_in[:, h, :], qg[d][:, h, :], start=False, stop=True)
                last.then_inc(o_mm[d], 1)

            s_of = lambda n, d: {0: None, 1: Sc[d], 2: Sa[d], 3: Sc[d], 4: Sa[d]}[n]
            for n in range(NC):
                for step in (row, products, mask_row, level0):
                    for d in range(2):
                        step(n, d)
                for s in range(1, LEVELS):
                    for d in range(2):
                        level_x(n, d, s)
                    for d in range(2):
                        level_tr(n, d, s)
                for d in range(2):
                    if n > 0:
                        w_product(n, d)
                for d in range(2):
                    v_product(n, d, s_of(n, d))
                for d in range(2):
                    if n < NC - 1:
                        s_product(n, d)
                    o_product(n, d, s_of(n, d))

            for h in range(HEADS):
                pe.wait_ge(osq_rdy, h + 1)
                if h > 0:
                    pe.wait_ge(ort_rdy, h)
                else:
                    pe.wait_ge(o_read[0], NC)
                    pe.wait_ge(o_read[1], NC)
                for b in range(2):
                    last = pe.matmul(sums[b], ones_t, osq[:, b * TH:b * TH + TH], start=True, stop=True)
                last.then_inc(osum, 1)

            for j in range(KD):
                if j == 0:
                    pe.wait_ge(o_read[0], NC)
                acc_wait(A_MO // 2 + j // 2, j % 2)
                unit(U_MO + j, j % 2, KD, h_hi, h_lo, j % 2, h_wait=(lambda k: (yl_rdy, k + 1)) if j == 0 else None)
            sum_squares(2, ssq_g)

            swiglu_in(0, U_F2I, A_F2I, h_wait=2 * KD)
            with pe.Fori(1, KF) as i:
                swiglu_in(i, U_F2I, A_F2I)

            def turn_y(j):
                pe.wait_ge(xg_rdy, j + 1)
                if j > 0:
                    pe.wait_ge(y_ev, j)
                for t in range(NC):
                    last = pe.transpose(ps[6 + t // 4][:, t % 4 * P:t % 4 * P + P], xg[:, j % 2, t * P:t * P + P],
                                        ident[:, :])
                last.then_inc(y_tr, 1)

            swiglu_out(U_F2O, A_F2O, KF, after=lambda j: turn_y(j - 1) if j > 0 else None)
            turn_y(KD - 1)
            pe.wait_ge(ssq_rdy, 4 * KD)
            for t in range(NC):
                last = pe.matmul(ps[4][:, t:t + 1], ssq_h[:, t * P:t * P + P], ones[:, :], start=True, stop=True)
            last.then_inc(y_sum, 1)

        @block.scalar
        def _(act):
            def split_hi(u, slot, kt, u_half, first=False):
                act.wait_ge(w_in[slot], 16 * u_half + 16)
                if not first:
                    act.wait_ge(mm_done, u - 1)
                nc.scalar.activation(w_hi[:, slot, 0:kt * P], w_raw[:, slot, 0:kt * P], ACT.Copy
                                     ).then_inc(hi_ready, 1)

            act.dma_start(vrow[R_CTX:R_CTX + 8, :], c_ctx.rearrange("(k p) -> k p", p=P)).then_inc(in_vec, 16)
            act.dma_start(vrow[R_C:R_C + 8, :], c[0].rearrange("(k p) -> k p", p=P)).then_inc(in_vec, 16)
            for row, v in ((R_N1, norm1[0]), (R_NM, norm_mix[0]), (R_N2, norm2[0]), (R_NF, norm_f)):
                act.dma_start(vrow[row:row + 8, :], v.rearrange("(k p) -> k p", p=P)).then_inc(in_vec, 16)
            act.dma_start(vrow[R_CONV:R_CONV + 12, :],
                         conv_w[0].rearrange("w (k p) -> (w k) p", p=P)).then_inc(in_vec, 16)
            act.dma_start(vrow[R_DNC:R_DNC + 36, :],
                         dn_conv_w[0].rearrange("w (k p) -> (w k) p", p=P)).then_inc(in_vec, 16)
            act.dma_start(vrow[R_DNN:R_DNN + 1, :], dn_norm).then_inc(in_vec, 16)
            act.dma_start(brow[:, :], b_ada[0].rearrange("(k p) -> k p", p=P)).then_inc(in_b, 16)
            act.dma_start(ident[:, :], consts[:, C_ID:C_ID + P]).then_inc(in_id, 16)
            act.wait_ge(vec_tr, 1)
            nc.scalar.activation(vec[:, :], ps[0][:, 0:NROWS], ACT.Copy).then_inc(vec_rdy, 1)
            nc.scalar.activation(bada[:, :], ps[0][:, P:P + 9 * KD], ACT.Copy).then_inc(vec_rdy, 1)
            act.wait_ge(misc_set, 3)
            act.wait_ge(vec_rdy, 2)
            nc.scalar.activation(ccol[:, :, 0:2], vec[:, 0:16].rearrange("p (i k) -> p k i", i=2), ACT.Silu
                                 ).then_inc(c_rdy, 1)
            xf = x[:, :, :].rearrange("p k t -> p (k t)")
            for n in range(0, 10, 2):
                act.wait_ge(x_tr, n + 1)
                nc.scalar.activation(xf[:, n * 512:n * 512 + 512], ps[2][:, :], ACT.Copy).then_inc(x_evA, 1)

            def square(n, k, wait, odd=sq_h):
                act.wait_ge(*wait)
                if n > 1:
                    act.wait_ge(ssq_rdy, n - 1)
                nc.scalar.activation((sa, odd)[k % 2][:, :], x[:, k, :], ACT.Square).then_inc(sq_rdy, 1)

            def ada_out(n, width):
                act.wait_ge(ada_mm, 8 * n + 8)
                if not (isinstance(n, int) and n == 0):
                    act.wait_ge(ada_tr, n)
                nc.scalar.activation(ada_r[:, 0:width], adap[:, 0:width], ACT.Copy).then_inc(ada_row, 1)

            for k in range(KD):
                act.wait_ge(x_evA, 5)
                square(k, k, (x_evB, 5))

            def norm(m, kt_next=None, n_sum=0):
                act.wait_ge(sum_mm, m + 1)
                nc.scalar.activation(halves(rinv[:, :])[:, 0, :], sums[0], ACT.Sqrt, bias=eps[:, :], scale=1.0 / D)
                nc.scalar.activation(halves(rinv[:, :])[:, 1, :], sums[1], ACT.Sqrt, bias=eps[:, :], scale=1.0 / D
                                     ).then_inc(rt_rdy, 1)
                if m == 0:
                    ada_out(0, 512)
                    for u in range(2):
                        split_hi(u, u, KD, 0, first=True)
                act.wait_ge(gain_rdy, 1 if m == 0 else 2)
                for k in range(KD):
                    act.wait_ge(*tn_wait(m, k))
                    for i, t0, t1 in GROUPS:
                        last = nc.scalar.activation(h_hi[:, k, t0:t1], tn[:, k, t0:t1], ACT.Identity,
                                                    bias=mod[:, 3 * m * KD + k, i:i + 1],
                                                    scale=gain[:, m, k, i:i + 1])
                    last.then_inc(hh_rdy, 1)

            norm(0)

            def gate_in(i, u0, i0):
                act.wait_ge(mm_done, u0 + 2 * i + 1)
                if not (isinstance(i, int) and i0 + i == 0):
                    act.wait_ge(g_rdy, i + i0)
                for b in range(2):
                    last = nc.scalar.activation(sa[:, b * TH:b * TH + TH], acc[0][b], ACT.Silu)
                last.then_inc(sa_rdy, 1)

            def swiglu_in(i, u0, i0, kt_next=KD, last=False):
                if not (isinstance(i, int) and i == 0):
                    split_hi(u0 + 2 * i + 1, 1, KD, u0 // 2 + i)
                gate_in(i, u0, i0)
                act.wait_ge(sa_rdy, i + i0 + 1)
                act_free(0)
                split_hi(u0 + 2 * i + 2, 0, kt_next, u0 // 2 + i + 1)

            def act_free(slot):
                act.sem_inc(acc_free[slot], 1)

            def slab(s, width=512):
                for half in range(2):
                    swiglu_in(2 * s + half, U_F1I, 0)
                ada_out(s + 1, width)
            slab(0)
            with act.Fori(1, 3) as s:
                slab(s)
            slab(3, 256)
            with act.Fori(8, KF - 1) as i:
                swiglu_in(i, U_F1I, 0)
            swiglu_in(KF - 1, U_F1I, 0, kt_next=KH)

            def swiglu_out(u0, n0, kt_next, x0, after=lambda j: None):
                for j in range(KD):
                    split_hi(u0 + 2 * j + 1, 1, KH, u0 // 2 + j)
                    if j > 0:
                        square(n0 + j - 1, j - 1, (x_upd, x0 + j))
                        after(j - 1)
                    if j < KD - 1:
                        split_hi(u0 + 2 * j + 2, 0, KH, u0 // 2 + j + 1)
                    elif kt_next:
                        split_hi(u0 + 2 * j + 2, 0, kt_next, u0 // 2 + j + 1)
                square(n0 + KD - 1, KD - 1, (x_upd, x0 + KD))

            swiglu_out(U_F1O, KD, KD, 0)
            split_hi(U_MI + 1, 1, KD, U_MI // 2)
            norm(1)

            for n in range(28):
                u = U_MI + n + 1
                if n == 24:
                    act.wait_ge(in_wab, 16)
                    nc.scalar.activation(wab_hi[:, :, :], wab[:, :, :], ACT.Copy).then_inc(wab_h, 1)
                if 0 < n < 27:
                    split_hi(u, (n + 1) % 2, KD, u // 2)
                if 1 <= n <= 8:
                    act.wait_ge(ssm, n)
                    for b in range(2):
                        last = nc.scalar.activation(ss[:, n - 1, b * TH:b * TH + TH], sums[b], ACT.Copy)
                    last.then_inc(ss_rdy, 1)
                if n < 12:
                    act.wait_ge(mm_done, U_MI + n + 1)
                    if n > 0:
                        act.wait_ge(qs_rdy, n)
                    tap = vec[:, R_DNC + 12 + n:R_DNC + 13 + n]
                    for b in range(2):
                        last = nc.scalar.activation(cv[:, b * TH:b * TH + TH], acc[n % 2][b], ACT.Identity, scale=tap)
                    last.then_inc(cv_rdy, 1)
                    act.wait_ge(uc_rdy, n + 1)
                    nc.scalar.activation(qkv[:, n, :], cv[:, :], ACT.Silu).then_inc(qs_rdy, 1)
                    if n < 8:
                        act.wait_ge(qs_rdy, n + 1)
                        if n > 0:
                            act.wait_ge(ssm, n)
                        nc.scalar.activation(sa[:, :], qkv[:, n, :], ACT.Square).then_inc(q2_rdy, 1)
                elif n < 16:
                    act.wait_ge(mm_done, U_MI + n + 1)
                    for b in range(2):
                        last = nc.scalar.activation(zs[:, n - 12, b * TH:b * TH + TH], acc[n % 2][b], ACT.Silu)
                    last.then_inc(z_rdy, 1)
                    act.wait_ge(z_rdy, n - 11)
                    act_free(n % 2)
                elif n % 3 == 1:
                    act.wait_ge(mm_done, U_MI + n + 1)
                    if n > 16:
                        act.wait_ge(u_rdy, (n - 16) // 3)
                    for b in range(2):
                        last = nc.scalar.activation(cc[:, b * TH:b * TH + TH], acc[n % 2][b], ACT.Copy)
                    last.then_inc(cc_rdy, 1)
                    act.wait_ge(cc_rdy, (n - 16) // 3 + 1)
                    act_free(n % 2)
                if 16 <= n < 24:
                    act.wait_ge(ss_rdy, 8)
                    nc.scalar.activation(ss[:, n - 16, :], ss[:, n - 16, :], ACT.Sqrt, bias=eps[:, :]
                                         ).then_inc(st_rdy, 1)
            act.wait_ge(ab_mm, 1)
            act.wait_ge(ssm, 8)
            for b in range(2):
                last = nc.scalar.activation(sa[0:NAB, b * TH:b * TH + TH], sums[b][0:NAB, :], ACT.Copy)
            last.then_inc(ab_ev, 1)

            def tok(t):
                act.wait_ge(tok_tr, 2 * t + 1)
                nc.scalar.activation(ktok[:, t, :], ps[0][:, :], ACT.Copy).then_inc(tok_evA, 1)
            for t in range(NC):
                tok(t)

            act.wait_ge(ab_rdy, 3)
            nc.scalar.activation(gsm["t1"][:, :, :, :], gsm["t1"][:, :, :, :], ACT.Exp).then_inc(act_g, 1)
            nc.scalar.activation(gsm["beta"][:, :, :, :], gsm["t3"][:, :, :, :], ACT.Exp).then_inc(act_g, 1)
            act.wait_ge(in_adt, 32)
            nc.scalar.activation(gsm["adt"][:, 0:8], gsm["adt"][:, 0:8], ACT.Exp).then_inc(act_g, 1)
            act.wait_ge(act_g, 3)
            nc.scalar.activation(gsm["t1"][:, :, :, :], gsm["t1"][:, :, :, :], ACT.Ln, bias=1.0).then_inc(act_g, 1)
            act.wait_ge(dve_g, 2)
            nc.scalar.activation(gsm["eg"][:, :, :, :], gsm["gc"][:, :, :, :], ACT.Exp)
            nc.scalar.activation(gsm["gl"][:, :, :, :], gsm["gt"][:, :, :, :], ACT.Exp)
            nc.scalar.activation(gsm["kgs"][:, :, :, :], gsm["t2"][:, :, :, :], ACT.Exp).then_inc(gates, 1)

            bank = [[ps[4 * d + i] for i in range(4)] for d in range(2)]

            def chunk(n, d):
                return n if n == 0 or d == 0 else NC - n

            flat = lambda t: t[:, :, :].rearrange("p h j -> p (h j)")
            for n in range(NC):
                for d in range(2):
                    act.wait_ge(row_rdy[d], n + 1)
                    if n > 0:
                        act.wait_ge(v_mm[d], n)
                    nc.scalar.activation(flat(Erow[d]), bank[d][0][:, :], ACT.Exp).then_inc(erow_rdy[d], 1)
                for d in range(2):
                    act.wait_ge(rowm[d], n + 1)
                    for h in range(HEADS):
                        last = nc.scalar.activation(DT[d][:, h, :], bank[d][0][:, h * P:h * P + P], ACT.Exp,
                                                    bias=gsm["ngc"][:, d, chunk(n, d), h:h + 1])
                    last.then_inc(dt_rdy[d], 1)
                for s in range(1, LEVELS):
                    for d in range(2):
                        act.wait_ge(x_mm[d], 7 * n + s + 1)
                        if 6 * n + s > 1:
                            act.wait_ge(tr_mm[d], 6 * n + s - 1)
                        nc.scalar.activation(flat(Xm[d]), bank[d][1][:, :], ACT.Copy).then_inc(xm_rdy[d], 1)
                for d in range(2):
                    if n > 0:
                        act.wait_ge(w_mm[d], n)
                        act.wait_ge(qg_rdy[d], n)
                        nc.scalar.activation(flat(WT[d]), bank[d][0][:, :], ACT.Copy, scale=-1.0
                                             ).then_inc(wt_rdy[d], 1)
                if n == 0:
                    for d, out in enumerate((s_out_f, s_out_b)):
                        act.wait_ge(s_rdy[d], 1)
                        act.dma_start(out[0, 0].rearrange("h k v -> k h v"), Sb[d][:, :, :]).then_inc(st_done, 16)

            act.wait_ge(st_done, 32)
            for h in range(HEADS):
                if h == 0:
                    act.wait_ge(o_read[0], NC)
                    act.wait_ge(o_read[1], NC)
                else:
                    act.wait_ge(osum, h)
                nc.scalar.activation(osq[:, :], ot[:, h, :], ACT.Square).then_inc(osq_rdy, 1)
                act.wait_ge(osum, h + 1)
                for b in range(2):
                    last = nc.scalar.activation(orr[:, h, b * TH:b * TH + TH], sums[b], ACT.Sqrt, bias=eps[:, :],
                                                scale=1.0 / P)
                last.then_inc(ort_rdy, 1)
            act.wait_ge(o_mm[0], NC)
            act.wait_ge(o_mm[1], NC)
            for k in range(KD):
                if k < 4:
                    act.wait_ge(y_rdy, k + 1)
                    src = yc[:, k, :]
                else:
                    act.wait_ge(on_rdy, k - 3)
                    src = ot[:, k - 4, :]
                nc.scalar.activation(h_hi[:, k, :], src, ACT.Copy).then_inc(yh_rdy, 1)
            split_hi(U_MO, 0, KD, U_MO // 2)
            for j in range(KD):
                u = U_MO + j + 1
                split_hi(u, u % 2, KD, u // 2)
                if j > 0:
                    square(2 * KD + j - 1, j - 1, (x_upd, KD + j), sq_g)
            square(3 * KD - 1, KD - 1, (x_upd, 2 * KD), sq_g)
            split_hi(U_F2I + 1, 1, KD, U_F2I // 2)
            norm(2)
            swiglu_in(0, U_F2I, KF)
            with act.Fori(1, KF - 1) as i:
                swiglu_in(i, U_F2I, KF)
            swiglu_in(KF - 1, U_F2I, KF, kt_next=KH)

            def scale_x(j):
                if j > 1:
                    act.wait_ge(y_tr, j - 1)
                nc.scalar.activation(xg[:, j % 2, :], x[:, j, :], ACT.Identity, scale=vec[:, R_NF + j:R_NF + j + 1]
                                     ).then_inc(xg_rdy, 1)

            def copy_y(j):
                act.wait_ge(y_tr, j + 1)
                nc.scalar.activation(yo[:, 0:4, j * P:j * P + P], ps[6][:, :].rearrange("p (t f) -> p t f", t=4), ACT.Copy)
                nc.scalar.activation(yo[:, 4, j * P:j * P + P], ps[7][:, 0:P], ACT.Copy).then_inc(y_ev, 1)

            def after(j):
                scale_x(j)
                if j > 0:
                    copy_y(j - 1)
            swiglu_out(U_F2O, 3 * KD, None, 2 * KD, after)
            after(KD - 1)
            copy_y(KD - 1)
            act.wait_ge(y_sum, 1)
            nc.scalar.activation(rfin[:, :], ps[4][:, 0:NC], ACT.Sqrt, bias=eps[:, :], scale=1.0 / D).then_inc(y_rt, 1)

        @block.vector
        def _(dve):
            link = seq(dve)

            def split_lo(u, slot, kt):
                dve.wait_ge(hi_ready, u + 1)
                nc.vector.tensor_tensor(w_lo[:, slot, 0:kt * P], w_raw[:, slot, 0:kt * P],
                                        w_hi[:, slot, 0:kt * P].bitcast(F32), ALU.subtract).then_inc(lo_ready, 1)

            nc.vector.memset(ones[:, :], 1.0).then_inc(misc_set, 1)
            nc.vector.memset(eps[:, :], EPS).then_inc(misc_set, 1)
            nc.vector.memset(ccol[:, :, :], 0.0).then_inc(misc_set, 1)
            xf = x[:, :, :].rearrange("p k t -> p (k t)")
            for n in range(1, 10, 2):
                dve.wait_ge(x_tr, n + 1)
                nc.vector.tensor_copy(xf[:, n * 512:n * 512 + 512], ps[3][:, :]).then_inc(x_evB, 1)

            def ada_cols(n, blocks):
                dve.wait_ge(ada_tr, n + 1)
                if isinstance(n, int) and n == 0:
                    dve.wait_ge(vec_rdy, 2)
                for b in range(blocks):
                    src = adat[:, b * P:b * P + P].rearrange("p (g i) -> p g i", i=32)
                    for i in range(2):
                        lo = 16 * n + b
                        last = nc.vector.tensor_tensor(
                            mod[:, bass.ds(lo, 4, blocks), i], src[:, :, i], bada[:, bass.ds(lo, 4, blocks)], ALU.add)
                last.then_inc(mod_rdy, 1)

            def gains(m, first):
                for i in range(2):
                    last = nc.vector.scalar_tensor_tensor(
                        out=gain[:, m, :, i], in0=mod[:, (3 * m + 1) * KD:(3 * m + 2) * KD, i], scalar=1.0,
                        in1=vec[:, (R_N1, R_NM, R_N2)[m]:(R_N1, R_NM, R_N2)[m] + 8], op0=ALU.add, op1=ALU.mult)
                return last

            def add_squares(m, k, dst, odd=sq_h):
                dve.wait_ge(sq_rdy, KD * m + k + 1)
                src = (sa, odd)[k % 2]
                if k == 0:
                    nc.vector.tensor_copy(dst[:, :], src[:, :]).then_inc(ssq_rdy, 1)
                else:
                    dve.wait_ge(ssq_rdy, KD * m + k)
                    nc.vector.tensor_tensor(dst[:, :], dst[:, :], src[:, :], ALU.add).then_inc(ssq_rdy, 1)

            for k in range(KD):
                add_squares(0, k, ssq_h)

            def norm(m):
                dve.wait_ge(rt_rdy, m + 1)
                nc.vector.reciprocal(rinv[:, :], rinv[:, :]).then_inc(r_rdy, 1)
                dve.wait_ge(r_rdy, m + 1)
                for k in range(0, KD, 2 if m == 0 else KD):
                    nc.vector.tensor_tensor(tn[:, k, :], x[:, k, :], rinv[:, :], ALU.mult).then_inc(tn_rdy, 1)
                if m == 0:
                    ada_cols(0, 4)
                    dve.wait_ge(mod_rdy, 1)
                    gains(0, True).then_inc(gain_rdy, 1)
                    for u in range(2):
                        split_lo(u, u, KD)
                    dve.wait_ge(gain_rdy, 1)

                def low(k):
                    dve.wait_ge(hf_rdy, KD * m + k + 1)
                    dve.wait_ge(hh_rdy, KD * m + k + 1)
                    nc.vector.tensor_tensor(h_lo[:, k, :], hf[:, k, :], h_hi[:, k, :].bitcast(F32), ALU.subtract
                                            ).then_inc(h_rdy, 1)
                for k in range(KD):
                    if k > 0:
                        low(k - 1)
                    dve.wait_ge(*tn_wait(m, k))
                    for i, t0, t1 in GROUPS:
                        last = nc.vector.tensor_scalar(hf[:, k, t0:t1], tn[:, k, t0:t1], gain[:, m, k, i:i + 1],
                                                       mod[:, 3 * m * KD + k, i:i + 1], ALU.mult, ALU.add)
                    last.then_inc(hf_rdy, 1)
                low(KD - 1)

            norm(0)

            def gate_out(i, u0, i0):
                dve.wait_ge(mm_done, u0 + 2 * i + 2)
                dve.wait_ge(sa_rdy, i + i0 + 1)
                for b in range(2):
                    last = nc.vector.tensor_tensor(sa[:, b * TH:b * TH + TH], sa[:, b * TH:b * TH + TH], acc[1][b],
                                                   ALU.mult)
                last.then_inc(gp_rdy, 1)
                dve.wait_ge(gp_rdy, i + i0 + 1)
                dve.sem_inc(acc_free[1], 1)
                gh = g_hi[:, bass.ds(i, 1), :].rearrange("p a t -> p (a t)")
                gl = g_lo[:, bass.ds(i, 1), :].rearrange("p a t -> p (a t)")
                nc.vector.tensor_copy(gh, sa[:, :]).then_inc(gh_rdy, 1)
                dve.wait_ge(gh_rdy, i + i0 + 1)
                nc.vector.tensor_tensor(gl, sa[:, :], gh.bitcast(F32), ALU.subtract).then_inc(g_rdy, 1)

            def swiglu_in(i, u0, i0, kt_next=KD):
                if not (isinstance(i, int) and i == 0):
                    split_lo(u0 + 2 * i + 1, 1, KD)
                split_lo(u0 + 2 * i + 2, 0, kt_next)
                gate_out(i, u0, i0)

            def slab(s, blocks=4):
                for half in range(2):
                    swiglu_in(2 * s + half, U_F1I, 0)
                ada_cols(s + 1, blocks)
            slab(0)
            with dve.Fori(1, 3) as s:
                slab(s)
            slab(3, 2)
            dve.wait_ge(mod_rdy, 5)
            gains(1, False)
            gains(2, False)
            for m in range(3):
                last = nc.vector.tensor_scalar(gate[:, m, :, :], mod[:, (3 * m + 2) * KD:(3 * m + 3) * KD, :],
                                               1.0 if m == 1 else 0.5, None, ALU.mult)
            last.then_inc(gain_rdy, 1)
            with dve.Fori(8, KF - 1) as i:
                swiglu_in(i, U_F1I, 0)
            swiglu_in(KF - 1, U_F1I, 0, kt_next=KH)

            def residual(m, j, done, a_slot, n):
                dve.wait_ge(mm_done, done)
                if j == 0:
                    dve.wait_ge(gain_rdy, 2)
                for bnk, b0, b1, i, t0 in PIECES:
                    last = nc.vector.scalar_tensor_tensor(
                        out=x[:, j, t0:t0 + b1 - b0], in0=acc[a_slot][bnk][:, b0:b1], scalar=gate[:, m, j, i:i + 1],
                        in1=x[:, j, t0:t0 + b1 - b0], op0=ALU.mult, op1=ALU.add)
                last.then_inc(x_upd, 1)
                dve.wait_ge(x_upd, n + 1)
                dve.sem_inc(acc_free[a_slot], 1)

            def swiglu_out(u0, m, x0, kt_next, norm_m):
                for j in range(KD):
                    split_lo(u0 + 2 * j + 1, 1, KH)
                    if j < KD - 1:
                        split_lo(u0 + 2 * j + 2, 0, KH)
                    elif kt_next:
                        split_lo(u0 + 2 * j + 2, 0, kt_next)
                    if j > 0:
                        add_squares(norm_m, j - 1, ssq_h)
                    residual(m, j, u0 + 2 * j + 2, j % 2, x0 + j)
                add_squares(norm_m, KD - 1, ssq_h)

            swiglu_out(U_F1O, 0, 0, KD, 1)
            split_lo(U_MI + 1, 1, KD)
            norm(1)

            def taps(n, a_slot):
                dve.wait_ge(cv_rdy, n + 1)
                a = acc[a_slot]
                before, after = (vec[:, R_DNC + 12 * w + n:R_DNC + 12 * w + n + 1] for w in (0, 2))
                for step, (bnk, b0, b1, t0, tap) in enumerate((
                        (0, 0, TP - 1, 1, before), (0, TP, TH, TP + 1, before), (1, 0, TH - 1, TH + 1, before),
                        (0, 1, TP, 0, after), (0, TP + 1, TH, TP, after), (1, 0, TH, TH - 1, after))):
                    ins = nc.vector.scalar_tensor_tensor(out=cv[:, t0:t0 + b1 - b0], in0=a[bnk][:, b0:b1], scalar=tap,
                                                         in1=cv[:, t0:t0 + b1 - b0], op0=ALU.mult, op1=ALU.add)
                    if step in (2, 5):
                        link(ins)
                dve.sem_inc(acc_free[a_slot], 1)
                dve.sem_inc(uc_rdy, 1)

            for n in range(28):
                u = U_MI + n + 1
                if n == 24:
                    dve.wait_ge(wab_h, 1)
                    nc.vector.tensor_tensor(wab_lo[:, :, :], wab[:, :, :], wab_hi[:, :, :].bitcast(F32), ALU.subtract
                                            ).then_inc(wab_rdy, 1)
                if 0 < n < 27:
                    split_lo(u, (n + 1) % 2, KD)
                a_slot = n % 2
                if n < 12:
                    taps(n, a_slot)
                elif n < 16:
                    pass
                elif n % 3 == 2:
                    m = (n - 16) // 3
                    dve.wait_ge(mm_done, U_MI + n + 1)
                    dve.wait_ge(cc_rdy, m + 1)
                    for b in range(2):
                        last = nc.vector.tensor_tensor(uu[:, b * TH:b * TH + TH], cc[:, b * TH:b * TH + TH],
                                                       acc[a_slot][b], ALU.mult)
                    last.then_inc(u_rdy, 1)
                    dve.wait_ge(u_rdy, m + 1)
                    dve.sem_inc(acc_free[a_slot], 1)
                    if m == 0:
                        dve.wait_ge(qs_rdy, 12)
                    tap = [vec[:, R_CONV + 4 * w + m:R_CONV + 4 * w + m + 1] for w in range(3)]
                    link(nc.vector.tensor_scalar(cv[:, :], uu[:, :], tap[1], None, ALU.mult))
                    for w in (0, 2):
                        for t0, t1, far in ((0, TP, 1), (TP, T, GRID_W)):
                            o = slice(t0 + far, t1) if w == 0 else slice(t0, t1 - far)
                            i = slice(t0, t1 - far) if w == 0 else slice(t0 + far, t1)
                            ins = nc.vector.scalar_tensor_tensor(out=cv[:, o], in0=uu[:, i], scalar=tap[w],
                                                                 in1=cv[:, o], op0=ALU.mult, op1=ALU.add)
                        link(ins)
                elif n % 3 == 0:
                    m = (n - 16) // 3
                    dve.wait_ge(mm_done, U_MI + n + 1)
                    for b in range(2):
                        last = nc.vector.tensor_tensor(yc[:, m, b * TH:b * TH + TH], cv[:, b * TH:b * TH + TH],
                                                       acc[a_slot][b], ALU.mult)
                    last.then_inc(y_rdy, 1)
                    dve.wait_ge(y_rdy, m + 1)
                    dve.sem_inc(acc_free[a_slot], 1)
                if 16 <= n < 24:
                    k = n - 16
                    dve.wait_ge(st_rdy, k + 1)
                    nc.vector.reciprocal(ss[:, k, :], ss[:, k, :]).then_inc(sr_rdy, 1)
                    dve.wait_ge(sr_rdy, k + 1)
                    nc.vector.scalar_tensor_tensor(out=qkv[:, k, :], in0=qkv[:, k, :],
                                                   scalar=float(P) ** -0.5 if k < 4 else 1.0, in1=ss[:, k, :],
                                                   op0=ALU.mult, op1=ALU.mult).then_inc(qn_rdy, 1)
            for t in range(NC):
                dve.wait_ge(tok_tr, 2 * t + 2)
                nc.vector.tensor_copy(vtok[:, t, :], ps[1][:, :]).then_inc(tok_evB, 1)

            G = gsm
            dve.wait_ge(ab_tr, 1)
            dve.wait_ge(ab_mm, 1)
            dve.wait_ge(in_adt, 32)
            ab4 = G["ab"][:, :].rearrange("p (c a h) -> p a c h", c=NC, a=4)
            link(nc.vector.tensor_copy(G["ab"][:, :], ps[6][:, 0:NC * NAB]))
            for d in range(2):
                dtb = G["adt"][:, 8 + 4 * d:12 + 4 * d].rearrange("p (a h) -> p a h", a=1).to_broadcast([P, NC, HEADS])
                last = nc.vector.tensor_tensor(G["g"][:, d], ab4[:, 2 * d], dtb, ALU.add)
            link(last)
            link(nc.vector.tensor_scalar(G["t2"][:, :, :, :], G["g"][:, :, :, :], -1.0, None, ALU.mult))
            nc.vector.tensor_tensor(G["t1"][:, :, :, :], G["g"][:, :, :, :], G["t2"][:, :, :, :], ALU.min
                                    ).then_inc(ab_rdy, 1)
            for d in range(2):
                nc.vector.tensor_scalar(G["t3"][:, d], ab4[:, 2 * d + 1], -1.0, None, ALU.mult).then_inc(ab_rdy, 1)
            dve.wait_ge(ab_rdy, 3)
            link(nc.vector.tensor_scalar(G["t2"][:, :, :, :], G["g"][:, :, :, :], 0.0, None, ALU.max))
            dve.wait_ge(act_g, 4)
            link(nc.vector.tensor_tensor(G["t2"][:, :, :, :], G["t2"][:, :, :, :], G["t1"][:, :, :, :], ALU.add))
            for d in range(2):
                A = G["adt"][:, 4 * d:4 * d + 4].rearrange("p (a h) -> p a h", a=1).to_broadcast([P, NC, HEADS])
                last = nc.vector.tensor_tensor(G["g"][:, d], G["t2"][:, d], A, ALU.mult)
            link(last)
            nc.vector.tensor_scalar(G["g"][:, :, :, :], G["g"][:, :, :, :], -1.0, None, ALU.mult
                                    ).then_inc(dve_g, 1)
            link(nc.vector.tensor_scalar(G["t3"][:, :, :, :], G["beta"][:, :, :, :], 1.0, None, ALU.add))
            link(nc.vector.reciprocal(G["beta"][:, :, :, :], G["t3"][:, :, :, :]))
            dve.wait_ge(in_lev, 32)
            link(nc.vector.tensor_copy(negb[:, :, :], negf[:, :, :]))
            link(nc.vector.tensor_copy(identb[:, :], ident[:, :]))
            dve.wait_ge(gsum, 1)
            flat2 = lambda t, d: t[:, d].rearrange("p c h -> p (c h)")
            for d in range(2):
                nc.vector.tensor_copy(flat2(G["gc"], d), ps[7][:, 32 * d:32 * d + 20])
                last = nc.vector.tensor_copy(flat2(G["gt"], d), ps[7][:, 64 + 32 * d:64 + 32 * d + 20])
            link(last)
            nc.vector.tensor_scalar(G["ngc"][:, :, :, :], G["gc"][:, :, :, :], -1.0, None, ALU.mult)
            link(nc.vector.tensor_tensor(G["t2"][:, :, :, :], G["gt"][:, :, :, :], G["gc"][:, :, :, :], ALU.subtract))
            dve.sem_inc(dve_g, 1)

            bank = [[ps[4 * d + i] for i in range(4)] for d in range(2)]

            def chunk(n, d):
                return n if n == 0 or d == 0 else NC - n

            flat = lambda t: t[:, :, :].rearrange("p h j -> p (h j)")
            ident4 = ident[:, :].rearrange("p (a j) -> p a j", a=1).to_broadcast([P, HEADS, P])
            b3 = lambda t: t[:, :].rearrange("p (h j) -> p h j", h=HEADS)
            s_of = lambda n, d: {0: None, 1: Sc[d], 2: Sa[d], 3: Sc[d], 4: Sa[d]}[n]
            for n in range(NC):
                for d in range(2):
                    c0 = chunk(n, d)
                    dve.wait_ge(kk_rdy[d], n + 1)
                    dve.wait_ge(dt_rdy[d], n + 1)
                    if n == 0:
                        dve.wait_ge(gates, 1)
                    else:
                        dve.wait_ge(nt_rdy[d], 7 * n)
                    for h in range(HEADS):
                        last = nc.vector.scalar_tensor_tensor(
                            out=LT[d][:, h, :], in0=bank[d][1][:, h * P:h * P + P], scalar=G["beta"][:, d, c0, h:h + 1],
                            in1=DT[d][:, h, :], op0=ALU.mult, op1=ALU.mult)
                    last.then_inc(lt_rdy[d], 1)
                    nc.vector.tensor_tensor(flat(QK[d]), bank[d][2][:, :], flat(DT[d]), ALU.mult
                                            ).then_inc(qk_rdy[d], 1)
                for d in range(2):
                    dve.wait_ge(x_mm[d], 7 * n + 1)
                    nc.vector.tensor_tensor(Tm[d][:, :, :], b3(bank[d][3]), ident4, ALU.add).then_inc(t_rdy[d], 1)
                for s in range(1, LEVELS):
                    for d in range(2):
                        dve.wait_ge(tr_mm[d], 6 * n + s)
                        if s < LEVELS - 1:
                            nc.vector.tensor_tensor(flat(Tm[d]), flat(Tm[d]), bank[d][0][:, :], ALU.add
                                                    ).then_inc(t_rdy[d], 1)
                        dve.wait_ge(rr_rdy[d], 7 * n + s)
                        nc.vector.tensor_tensor(flat(Rm[d]), flat(Rm[d]), bank[d][2][:, :], ALU.add
                                                ).then_inc(rr_rdy[d], 1)
                for d in range(2):
                    dve.wait_ge(v_mm[d], n + 1)
                    beta4 = G["beta"][:, d, chunk(n, d), :].rearrange("p (h a) -> p h a", a=1).to_broadcast([P, HEADS, P])
                    nc.vector.tensor_tensor(VN[d][:, :, :], b3(bank[d][1]), beta4, ALU.mult).then_inc(vn_rdy[d], 1)
                for d in range(2):
                    c0 = chunk(n, d)
                    if n < NC - 1:
                        dve.wait_ge(s_mm[d], n + 1)
                        s_in, s_new = s_of(n, d), (Sb if n == 0 else Sa if n in (1, 3) else Sc)[d]
                        if n == 0:
                            nc.vector.tensor_copy(flat(s_new), bank[d][3][:, :]).then_inc(s_rdy[d], 1)
                        else:
                            for h in range(HEADS):
                                last = nc.vector.scalar_tensor_tensor(
                                    out=s_new[:, h, :], in0=s_in[:, h, :], scalar=G["gl"][:, d, c0, h:h + 1],
                                    in1=bank[d][3][:, h * P:h * P + P], op0=ALU.mult, op1=ALU.add)
                            last.then_inc(s_rdy[d], 1)
                    dve.wait_ge(o_mm[d], n + 1)
                    dst = ot[:, :, c0 * P:c0 * P + P]
                    first = d == 0 if c0 == 0 or chunk(n, 0) == chunk(n, 1) else n < (c0 if d else NC - c0)
                    if first:
                        nc.vector.tensor_copy(dst, b3(bank[d][2])).then_inc(o_read[d], 1)
                    else:
                        if c0 == 0:
                            dve.wait_ge(o_read[0], 1)
                        else:
                            dve.wait_ge(o_read[1 - d], (NC - c0 if d == 0 else c0) + 1)
                        nc.vector.tensor_tensor(dst, dst, b3(bank[d][2]), ALU.add).then_inc(o_read[d], 1)

            for h in range(HEADS):
                dve.wait_ge(ort_rdy, h + 1)
                dve.wait_ge(osq_rdy, h + 1)
                nc.vector.reciprocal(orr[:, h, :], orr[:, h, :]).then_inc(orr_rdy, 1)
                dve.wait_ge(orr_rdy, h + 1)
                dve.wait_ge(z_rdy, h + 1)
                link(nc.vector.scalar_tensor_tensor(out=orr[:, h, :], in0=zs[:, h, :],
                                                    scalar=vec[:, R_DNN:R_DNN + 1], in1=orr[:, h, :],
                                                    op0=ALU.mult, op1=ALU.mult))
                nc.vector.tensor_tensor(ot[:, h, :], ot[:, h, :], orr[:, h, :], ALU.mult).then_inc(on_rdy, 1)
            dve.wait_ge(o_mm[0], NC)
            dve.wait_ge(o_mm[1], NC)
            for k in range(KD):
                dve.wait_ge(yh_rdy, k + 1)
                src = yc[:, k, :] if k < 4 else ot[:, k - 4, :]
                if k >= 4:
                    dve.wait_ge(on_rdy, k - 3)
                nc.vector.tensor_tensor(h_lo[:, k, :], src, h_hi[:, k, :].bitcast(F32), ALU.subtract
                                        ).then_inc(yl_rdy, 1)
            split_lo(U_MO, 0, KD)
            for j in range(KD):
                u = U_MO + j + 1
                split_lo(u, u % 2, KD)
                if j > 0:
                    add_squares(2, j - 1, ssq_g, sq_g)
                residual(1, j, U_MO + j + 1, j % 2, KD + j)
            add_squares(2, KD - 1, ssq_g, sq_g)
            split_lo(U_F2I + 1, 1, KD)
            norm(2)
            swiglu_in(0, U_F2I, KF)
            with dve.Fori(1, KF - 1) as i:
                swiglu_in(i, U_F2I, KF)
            swiglu_in(KF - 1, U_F2I, KF, kt_next=KH)
            swiglu_out(U_F2O, 2, 2 * KD, None, 3)
            dve.wait_ge(y_rt, 1)
            nc.vector.reciprocal(rfin[:, :], rfin[:, :]).then_inc(y_r, 1)
            dve.wait_ge(y_r, 1)
            dve.wait_ge(y_ev, KD)
            for t in range(NC):
                nc.vector.tensor_scalar(yo[:, t, :], yo[:, t, :], rfin[:, t:t + 1], None, ALU.mult).then_inc(y_fin, 1)

        @block.gpsimd
        def _(pool):
            def chunk(n, d):
                return n if n == 0 or d == 0 else NC - n

            def norm(m):
                pool.wait_ge(r_rdy, m + 1)
                for k in range(1, KD, 2 if m == 0 else 1):
                    nc.gpsimd.tensor_tensor(tn[:, k, :], x[:, k, :], rinv[:, :], ALU.mult).then_inc(tnp_rdy, 1)

            norm(0)
            norm(1)
            G = gsm
            pool.wait_ge(dve_g, 2)
            pool.wait_ge(gates, 1)
            pool.wait_ge(in_tri, 16)
            pool.wait_ge(in_lev, 32)
            pool.wait_ge(tok_evA, NC)
            pool.wait_ge(qn_rdy, 8)
            bc = lambda t, d, c0: t[:, d, c0, :].rearrange("p (h a) -> p h a", a=1).to_broadcast([P, HEADS, P])
            rep = lambda m: m.rearrange("p (a j) -> p a j", a=1).to_broadcast([P, HEADS, P])
            for n in range(NC):
                for d in range(2):
                    c0 = chunk(n, d)
                    if n > 0:
                        pool.wait_ge(lt_rdy[d], n)
                        pool.wait_ge(qk_rdy[d], n)
                    nc.gpsimd.tensor_tensor(gtri[d][:, :, :], rep(tri[:, d, :]), bc(G["g"], d, c0), ALU.mult
                                            ).then_inc(gtri_rdy[d], 1)

                def mask(s, d):
                    nt = (NTa, NTb)[s % 2][d]
                    if s == 0:
                        pool.wait_ge(lt_rdy[d], n + 1)
                    if s == 2:
                        pool.wait_ge(rr_rdy[d], 7 * n + 1)
                    used = 7 * n + (0, -1)[s] if s < 2 else 7 * n + s - 1
                    if used > 0:
                        pool.wait_ge(x_mm[d], used)
                    nc.gpsimd.tensor_tensor(nt[:, :, :], LT[d][:, :, :], rep(lev[:, LEVELS * d + s, :]), ALU.mult
                                            ).then_inc(nt_rdy[d], 1)

                for d in range(2):
                    mask(0, d)
                    pool.wait_ge(nt_rdy[d], 7 * n + 1)
                    if n > 0:
                        pool.wait_ge(v_mm[d], n)
                    nc.gpsimd.tensor_tensor(Rm[d][:, :, :], NTa[d][:, :, :], rep(ident[:, :]), ALU.add
                                            ).then_inc(rr_rdy[d], 1)
                    mask(1, d)
                for s in range(2, LEVELS):
                    for d in range(2):
                        mask(s, d)
                    d = s % 2
                    c0 = chunk(n, d)
                    kt = ktok[:, c0, :].rearrange("p (h j) -> p h j", h=HEADS)
                    if s < 4:
                        if n > 0:
                            pool.wait_ge(s_mm[d], n)
                        if n < NC - 1:
                            nc.gpsimd.tensor_tensor(kg[d][:, :, :], kt, bc(G["kgs"], d, c0), ALU.mult
                                                    ).then_inc(kg_rdy[d], 1)
                    elif s < 6 and n > 0:
                        if n > 1:
                            pool.wait_ge(w_mm[d], n - 1)
                        nc.gpsimd.tensor_tensor(ke[d][:, :, :], kt, bc(G["eg"], d, c0), ALU.mult
                                                ).then_inc(ke_rdy[d], 1)
                for d in range(2):
                    if n > 0:
                        c0 = chunk(n, d)
                        pool.wait_ge(erow_rdy[d], n + 1)
                        if n > 1:
                            pool.wait_ge(o_mm[d], n)
                        nc.gpsimd.tensor_tensor(qg[d][:, :, :], qkv[:, 0:4, c0 * P:c0 * P + P], Erow[d][:, :, :], ALU.mult
                                                ).then_inc(qg_rdy[d], 1)
            norm(2)


_INS = ["x_prompt", "x_sample", "state_dn_fwd", "state_dn_bwd", "c", "c_ctx", "w_ada", "b_ada", "norm_ffn1",
        "w_ffn1_in", "w_ffn1_out", "norm_mix", "w_mix_in", "conv_w", "dn_conv_w", "dn_a_log", "dn_dt_bias", "dn_norm",
        "w_mix_out", "norm_ffn2", "w_ffn2_in", "w_ffn2_out", "norm_final"]
_OUTS = [(1, TP, D), (1, TS, D), (1, 1, HEADS, P, P), (1, 1, HEADS, P, P)]


def kernel(**inputs):
    import concourse.bacc as bacc
    from concourse.bass_utils import run_bass_kernel_spmd

    nc = bacc.Bacc("TRN2", target_bir_lowering=False, num_devices=1)
    arrays, args = {}, []
    for name in _INS:
        a = np.ascontiguousarray(inputs[name])
        arrays[f"in_{name}"] = a
        args.append(nc.dram_tensor(f"in_{name}", a.shape, mybir.dt.from_np(a.dtype), kind="ExternalInput").ap())
    arrays["in_consts"] = constants()
    args.append(nc.dram_tensor("in_consts", (P, NCONST), F32, kind="ExternalInput").ap())
    for i, shape in enumerate(_OUTS):
        args.append(nc.dram_tensor(f"out_{i}", shape, F32, kind="ExternalOutput").ap())
    hybrid_layer(nc, *args)
    r = run_bass_kernel_spmd(nc, [arrays], core_ids=[0])
    return tuple(r.results[0][f"out_{i}"] for i in range(len(_OUTS)))
```

```python
from contextlib import ExitStack

import numpy as np

import concourse.bass as bass
from concourse import mybir

F32 = mybir.dt.float32
F32R = mybir.dt.float32r
BF16 = mybir.dt.bfloat16
ALU = mybir.AluOpType
ACT = mybir.ActivationFunctionType

P = 128
D = 1024
KD = D // P
TP, TS = 128, 512
T = TP + TS
TH = T // 2
NC = T // P
FF = 2816
KF = FF // P
KH = KF // 2
HEADS = 4
CW = D // 2
QKV0 = 3 * CW
Z0 = QKV0 + 3 * CW
AB0 = Z0 + CW
NAB = 4 * HEADS
BS = 16
LEV0 = 4
LEVELS = 3
BPC = P // BS
GROUPS_DN = 2 * NC
HPL = BPC * (BS * P + BS)
PREP0 = 15
GRID_W = 64
EPS = 1e-6
NEG = -1e30

U_F1I = 0
U_F1O = U_F1I + 2 * KF
U_MI = U_F1O + 2 * KD
U_MO = U_MI + 28
U_F2I = U_MO + KD
U_F2O = U_F2I + 2 * KF
U_END = U_F2O + 2 * KD
A_F1I = 0
A_F1O = A_F1I + 2 * KF
A_MI = A_F1O + KD
A_MO = A_MI + 28
A_F2I = A_MO + KD
A_F2O = A_F2I + 2 * KF

R_CTX, R_C, R_N1, R_NM, R_N2, R_NF, R_CONV, R_DNC, R_DNN = 0, 8, 16, 24, 32, 40, 48, 60, 96
NROWS = 97
C_ID, C_TRI, C_LEV, C_BLK = 0, P, 3 * P, 3 * P + 2 * LEVELS * P
C_NEG = C_BLK + P
C_SUB = C_NEG + 2 * P
NCONST = C_SUB + BS * BS


def constants():
    j, i = np.meshgrid(np.arange(P), np.arange(P), indexing="ij")
    out = np.zeros((P, NCONST), np.float32)
    out[:, C_ID:C_ID + P] = i == j
    for d in range(2):
        a, b = (j, i) if d == 0 else (i, j)
        out[:, C_TRI + d * P:C_TRI + (d + 1) * P] = a <= b
        for m in range(LEVELS):
            s = LEV0 + m
            joined = (a >> s) + 1 == (b >> s)
            c = C_LEV + (d * LEVELS + m) * P
            out[:, c:c + P] = -1.0 * (joined & ((b >> s) % 2 == 1))
        out[:, C_NEG + d * P:C_NEG + (d + 1) * P] = np.where(a <= b, 0.0, NEG)
    out[:, C_BLK:C_BLK + P] = j // BS == i // BS
    out[:, C_SUB:] = (np.eye(BS) - np.triu(np.ones((BS, BS)), 1)).reshape(1, -1)
    return out


def hybrid_layer(nc, x_prompt, x_sample, state_f, state_b, c, c_ctx, w_ada, b_ada, norm1, w1i, w1o, norm_mix,
                 w_mi, conv_w, dn_conv_w, a_log, dt_bias, dn_norm, w_mo, norm2, w2i, w2o, norm_f, consts,
                 y_prompt, y_sample, s_out_f, s_out_b):
    ctx = ExitStack()
    with ctx:
        sem = lambda name: ctx.enter_context(nc.semaphore(name))
        place = {"at": 16512}

        def sb(name, shape, dt, at=None):
            size = int(np.prod(shape[1:])) * (2 if dt == BF16 else 4)
            if at is None:
                at = place["at"]
                place["at"] += (size + 31) // 32 * 32
            return nc.alloc_sbuf_tensor_at(name, shape, dt, offset=at)

        x = sb("x", [P, KD, T], F32)
        at_h = place["at"]
        h_hi = sb("h_hi", [P, KD, T], F32R)
        h_lo = sb("h_lo", [P, KD, T], F32R)
        at_g = place["at"]
        g_hi = sb("g_hi", [P, KF, T], F32R)
        g_lo = sb("g_lo", [P, KF, T], F32R)
        w_raw = sb("w_raw", [P, 2, KH * P], F32)
        w_hi = sb("w_hi", [P, 2, KH * P], F32R)
        w_lo = sb("w_lo", [P, 2, KH * P], F32R)
        at_sa = place["at"]
        sa = sb("sa", [P, T], F32)
        mod = sb("mod", [P, 9 * KD, 2], F32)
        gain = sb("gain", [P, 3, KD, 2], F32)
        gate = sb("gate", [P, 3, KD, 2], F32)
        vec = sb("vec", [P, NROWS], F32)
        bada = sb("bada", [P, 9 * KD], F32)
        ident = sb("ident", [P, P], F32)
        ones = sb("ones", [P, 1], F32)
        eps = sb("eps", [P, 1], F32)
        eps_o = sb("eps_o", [P, 1], F32)
        assert place["at"] <= 229344, place["at"]
        ones_t = ones[:, 0:1].to_broadcast([P, P])

        KB = 1024
        xin = sb("xin", [P, NC, D], F32, at=at_g)
        vrow = sb("vrow", [NROWS, P], F32, at=at_g + 20 * KB)
        brow = sb("brow", [9 * KD, P], F32, at=at_g + 20 * KB + 512)
        at_ada = at_g + (KF + 8) * 4 * T
        ADA = 4
        ada_w = sb("ada_w", [P, ADA, 2048], F32, at=at_ada)
        ada_r = sb("ada_r", [P, 512], F32, at=at_ada + ADA * 8 * KB)
        ccol = sb("ccol", [P, KD, 32], F32, at=at_ada + ADA * 8 * KB + 2048)
        assert at_ada + ADA * 8 * KB + 2048 + 1024 <= at_g + 2 * KF * 4 * T
        rinv = sb("rinv", [P, T], F32, at=at_g + 20 * KB)
        tn = sb("tn", [P, KD, T], F32, at=at_g)
        hf = sb("hf", [P, KD, T], F32, at=at_g + 24 * KB)
        B = 4 * T
        qkv = sb("qkv", [P, 12, T], F32, at=at_g)
        zs = sb("zs", [P, 4, T], F32, at=at_g + 12 * B)
        yc = sb("yc", [P, 4, T], F32, at=at_g + 16 * B)
        ot = sb("ot", [P, HEADS, T], F32, at=at_g + 20 * B)
        wab = sb("wab", [P, KD, NAB], F32, at=at_g + 20 * B)
        wab_hi = sb("wab_hi", [P, KD, NAB], F32R, at=at_g + 20 * B + 512)
        wab_lo = sb("wab_lo", [P, KD, NAB], F32R, at=at_g + 20 * B + 1024)
        abt = sb("abt", [NAB, T], F32, at=at_g + 20 * B + 1536)
        negf = sb("negf", [P, 2, P], F32, at=at_g + 22 * B)
        ktok = sb("ktok", [P, NC, CW], F32, at=at_g + 24 * B)
        vtok = sb("vtok", [P, NC, CW], F32, at=at_g + 28 * B)
        ss = sb("ss", [P, 4, T], F32, at=at_g + 36 * B)
        cc = sb("cc", [P, T], F32, at=at_g + 40 * B)
        uu = sb("uu", [P, T], F32, at=at_g + 41 * B)
        cv = sb("cv", [P, T], F32, at=at_g + 42 * B)
        tri = sb("tri", [P, 2, P], F32, at=at_g + 43 * B)
        negb = sb("negb", [P, 2, P], BF16, at=at_g + 43 * B + 1024)
        identb = sb("identb", [P, P], BF16, at=at_g + 43 * B + 1536)
        lev = sb("lev", [P, 2 * LEVELS, P], F32, at=at_g + 40 * B)
        blk = sb("blk", [P, P], F32, at=at_g + 40 * B + 3072)
        rt16 = [sb(f"rt16_{d}", [P, 2, 2, HEADS * BS], F32, at=at_g + 40 * B + 3584 + 1024 * d) for d in range(2)]
        gsm = {}
        off = at_sa
        for name in ("g", "beta", "gc", "ngc", "eg", "gt", "gl", "kgs", "t1", "t2", "t3"):
            gsm[name] = sb("s_" + name, [P, 2, NC, HEADS], F32, at=off)
            off += 160
        off = at_g + 22 * B + 1024
        for name, width in (("ab", NC * NAB), ("adt", 16)):
            gsm[name] = sb(name, [P, width], F32, at=off)
            off += 4 * width
        spots = [at_g + 24 * B + 2048 * i for i in range(10)]
        per = lambda name: [sb(f"{name}{d}", [P, HEADS, P], F32, at=spots.pop(0)) for d in range(2)]
        DT = per("DT")
        gtri = DT
        Erow, LTp, QKp, qgp = per("Erow"), per("LTp"), per("QKp"), per("qgp")
        sub = {name: sb("sub_" + name, [P, BS, BS], F32, at=at_g + 32 * B + 1024 * i)
               for i, name in enumerate(("u", "n", "x", "xt", "tmp", "mask"))}
        spots = [at_h + 2048 * i for i in range(20)] + [at_g + 36 * B + 2048 * i for i in range(5)] + \
                [at_g + 32 * B + 6144 + 2048 * i for i in range(2)] + [at_g + 8 * B + 2048 * i for i in range(5)]
        NTa, NTb, Tm, Xm, LT, QK, qg, ke = (per(n) for n in ("NTa", "NTb", "Tm", "Xm", "LT", "QK", "qg", "ke"))
        Rm = [per("Rm0_"), per("Rm1_")]
        kg, VN, WT, Sa, Sb, Sc = (per(n) for n in ("kg", "VN", "WT", "Sa", "Sb", "Sc"))
        keep = lambda name, n: nc.dram_tensor(name, [NC, 2, n], F32).ap()
        d_lt, d_qk, d_qg = keep("d_lt", HEADS * HPL), keep("d_qk", P * CW), keep("d_qg", P * CW)
        d_rt = nc.dram_tensor("d_rt", [NC, 2, 2, P * HEADS * BS], F32).ap()

        def view(t, dims):
            return bass.AP(tensor=t.tensor, offset=t.offset, ap=dims)

        osq = sb("osq", [P, T], F32, at=at_g + 24 * B)
        oq = sb("oq", [P, HEADS, T], F32, at=at_g + 28 * B)
        orr = sb("orr", [P, HEADS, T], F32, at=at_g + 32 * B)

        ssq_h = sb("ssq_h", [P, T], F32, at=at_h)
        ssq_g = sb("ssq_g", [P, T], F32, at=at_g + 38 * B)
        sq_h = sb("sq_h", [P, T], F32, at=at_h + B)
        sq_g = sb("sq_g", [P, T], F32, at=at_g + 39 * B)
        xg = sb("xg", [P, 2, T], F32, at=at_h + 2 * B)
        rfin = sb("rfin", [P, NC], F32, at=at_h + 5 * B)
        yo = sb("yo", [P, NC, D], F32, at=at_h + 8 * B)

        ps = [ctx.enter_context(nc.psum_tensor(f"ps{i}", [P, 512], F32)) for i in range(8)]
        acc = [[ps[2 * s][:, 0:TH], ps[2 * s + 1][:, 0:TH]] for s in range(2)]
        sums = [ps[4][:, 0:TH], ps[5][:, 0:TH]]
        adap, adat = ps[6], ps[7]

        in_x, in_vec, in_id, in_wab, in_adt, in_tri, in_lev = (sem(n) for n in (
            "in_x", "in_vec", "in_id", "in_wab", "in_adt", "in_tri", "in_lev"))
        pk_in, solved = sem("pk_in"), sem("solved")
        in_s = [sem(f"in_s{d}") for d in range(2)]
        w_in = [sem(f"w_in{s}") for s in range(2)]
        hi_ready, lo_ready, mm_done = sem("hi_ready"), sem("lo_ready"), sem("mm_done")
        acc_free = [sem(f"acc_free{s}") for s in range(2)]
        ada_in = [sem(f"ada_in{s}") for s in range(ADA)]
        ada_mm, ada_row, ada_tr, mod_rdy = sem("ada_mm"), sem("ada_row"), sem("ada_tr"), sem("mod_rdy")
        misc_set, vec_tr, vec_rdy, c_rdy = sem("misc_set"), sem("vec_tr"), sem("vec_rdy"), sem("c_rdy")
        x_tr, x_evA, x_evB = sem("x_tr"), sem("x_evA"), sem("x_evB")
        sq_rdy, ssq_rdy, sum_mm, rt_rdy, r_rdy = (sem(n) for n in ("sq_rdy", "ssq_rdy", "sum_mm", "rt_rdy", "r_rdy"))
        tn_rdy, tnp_rdy, hh_rdy, hf_rdy, h_rdy = (sem(n) for n in ("tn_rdy", "tnp_rdy", "hh_rdy", "hf_rdy", "h_rdy"))
        sa_rdy, gp_rdy, gh_rdy, g_rdy = sem("sa_rdy"), sem("gp_rdy"), sem("gh_rdy"), sem("g_rdy")
        x_upd = sem("x_upd")
        dve_step = sem("dve_step")
        gain_rdy = sem("gain_rdy")

        def seq(engine):
            count = [0]

            def link(instruction):
                count[0] += 1
                instruction.then_inc(dve_step, 1)
                engine.wait_ge(dve_step, count[0])
            return link

        cv_rdy, qs_rdy, q2_rdy, ssm, ss_rdy, st_rdy, qn_rdy = (sem(n) for n in (
            "cv_rdy", "qs_rdy", "q2_rdy", "ssm", "ss_rdy", "st_rdy", "qn_rdy"))
        cc_rdy, u_rdy, uc_rdy, y_rdy, z_rdy = (sem(n) for n in ("cc_rdy", "u_rdy", "uc_rdy", "y_rdy", "z_rdy"))
        wab_h, wab_rdy, ab_mm, ab_ev, ab_tr, ab_rdy = (sem(n) for n in (
            "wab_h", "wab_rdy", "ab_mm", "ab_ev", "ab_tr", "ab_rdy"))
        tok_tr, tok_evA, tok_evB = sem("tok_tr"), sem("tok_evA"), sem("tok_evB")
        act_g, dve_g, gsum, gates = sem("act_g"), sem("dve_g"), sem("gsum"), sem("gates")
        pair = lambda n: [sem(f"{n}{d}") for d in range(2)]
        gtri_rdy, row_rdy, erow_rdy, rowm, kk_rdy, dt_rdy, lt_rdy, qk_rdy = (pair(n) for n in (
            "gtri_rdy", "row_rdy", "erow_rdy", "rowm", "kk_rdy", "dt_rdy", "lt_rdy", "qk_rdy"))
        nt_rdy, x_mm, xm_rdy, tr_mm, t_rdy, rr_rdy = (pair(n) for n in (
            "nt_rdy", "x_mm", "xm_rdy", "tr_mm", "t_rdy", "rr_rdy"))
        in_rt = [pair("in_rt_even"), pair("in_rt_odd")]
        st_lt, st_qk, st_rt, in_lt, in_qk = (pair(n) for n in (
            "st_lt", "st_qk", "st_rt", "in_lt", "in_qk"))
        ke_rdy, kg_rdy, qg_rdy, w_mm, wt_rdy, v_mm, vn_rdy, o_mm, o_read, s_mm, s_rdy = (pair(n) for n in (
            "ke_rdy", "kg_rdy", "qg_rdy", "w_mm", "wt_rdy", "v_mm", "vn_rdy", "o_mm", "o_read", "s_mm", "s_rdy"))
        osq_rdy, oq_rdy, osum, ort_rdy, orr_rdy, on_rdy, yh_rdy, yl_rdy = (sem(n) for n in (
            "osq_rdy", "oq_rdy", "osum", "ort_rdy", "orr_rdy", "on_rdy", "yh_rdy", "yl_rdy"))
        xg_rdy, y_tr, y_ev, y_sum, y_rt, y_r, y_fin, out_done, st_done = (sem(n) for n in (
            "xg_rdy", "y_tr", "y_ev", "y_sum", "y_rt", "y_r", "y_fin", "out_done", "st_done"))

        GROUPS = ((0, 0, TP), (1, TP, T))
        PIECES = ((0, 0, TP, 0, 0), (0, TP, TH, 1, TP), (1, 0, TH, 1, TH))

        def strip_col(n):
            if n < 16:
                return QKV0 + P * qkv_tile(n)
            return (CW, 2 * CW, 0)[(n - 16) % 3] + P * ((n - 16) // 3)

        def qkv_tile(n):
            return n + 4 if n < 4 else n - 4 if n < 8 else n

        def chunk(n, d):
            return n if n == 0 or d == 0 else NC - n

        def tn_wait(m, k):
            if m == 0:
                return (tn_rdy, k // 2 + 1) if k % 2 == 0 else (tnp_rdy, k // 2 + 1)
            return (tn_rdy, KD // 2 + m) if k == 0 else (tnp_rdy, KD // 2 + (KD - 1) * (m - 1) + k)

        def halves(t2):
            return t2.rearrange("p (a b) -> p a b", a=2)

        block = ctx.enter_context(nc.Block())

        @block.sync
        def _(sp):
            sp.dma_start(xin[:, 0, :], x_prompt[0]).then_inc(in_x, 16)
            sp.dma_start(xin[:, 1:NC, :], x_sample[0].rearrange("(c p) f -> p c f", p=P)).then_inc(in_x, 16)

            def load_w(u, slot, src, kt, wait=True):
                if wait:
                    sp.wait_ge(lo_ready, u - 1)
                sp.dma_start(w_raw[:, slot, 0:kt * P].rearrange("p (k f) -> p k f", k=kt),
                             src).then_inc(w_in[slot], 16)

            ada_v = w_ada[0].rearrange("(k p) f -> p k f", p=P)

            def load_ada(n, s, k, col, width):
                if not (isinstance(n, int) and n < ADA):
                    sp.wait_ge(ada_mm, n - ADA + 1)
                sp.dma_start(ada_w[:, s, 0:width], ada_v[:, k, bass.ds(col, width)]).then_inc(ada_in[s], 16)

            w_in_v = [w[0].rearrange("(k p) f -> p k f", p=P) for w in (w1i, w2i)]
            w_out_v = [w[0].rearrange("(k p) f -> p k f", p=P) for w in (w1o, w2o)]
            sp.wait_ge(in_vec, 10 * 16)
            for k in range(KD):
                load_ada(k, k % ADA, k, 0, 2048)
            for u in range(2):
                load_w(u, u, w_in_v[0][:, :, u * FF:u * FF + P], KD, wait=False)

            with sp.Fori(0, 3) as s:
                for half in range(2):
                    for k in range(4):
                        load_ada(8 * s + (8 + 4 * half + k), k, 4 * half + k, 2048 * s + 2048, 2048)
                    i = 2 * s + half + 1
                    for b in range(2):
                        load_w(2 * i + b, b, w_in_v[0][:, :, bass.ds(P * i + b * FF, P)], KD)
            for half in range(2):
                for k in range(4):
                    load_ada(32 + 4 * half + k, k, 4 * half + k, 8192, 1024)
                i = 7 + half
                for b in range(2):
                    load_w(2 * i + b, b, w_in_v[0][:, :, P * i + b * FF:P * i + b * FF + P], KD)
            with sp.Fori(9, KF) as i:
                for b in range(2):
                    load_w(2 * i + b, b, w_in_v[0][:, :, bass.ds(P * i + b * FF, P)], KD)
            with sp.Fori(0, KD) as j:
                for b in range(2):
                    load_w(U_F1O + 2 * j + b, b, w_out_v[0][:, KH * b:KH * b + KH, bass.ds(P * j, P)], KH)

            w_mi_v = w_mi[0].rearrange("(k p) f -> p k f", p=P)

            def prep_store(g):
                n, d = divmod(g, 2)
                sp.wait_ge(lt_rdy[d], n + 1)
                sp.dma_start(view(d_lt[n, d], [[P, P], [HPL, HEADS], [1, P]]), LTp[d][:, :, :]).then_inc(st_lt[d], 16)
                sp.wait_ge(qk_rdy[d], n + 1)
                sp.dma_start(view(d_qk[n, d], [[CW, P], [1, CW]]), QKp[d][:, :, :]).then_inc(st_qk[d], 16)
                if n > 0:
                    sp.wait_ge(qg_rdy[d], n)
                    sp.dma_start(view(d_qg[n, d], [[CW, P], [1, CW]]), qgp[d][:, :, :]).then_inc(st_qk[d], 16)

            def batch(b):
                return [(n, d, 64 * d + 32 * (n % 2)) for n in range(2 * b, min(2 * b + 2, NC)) for d in range(2)]

            def pack(b):
                if b > 0:
                    sp.wait_ge(solved, b)
                for n, d, p0 in batch(b):
                    sp.wait_ge(st_lt[d], 16 * (n + 1))
                    sp.dma_start(sub["u"][p0:p0 + 32, :, :], view(d_lt[n, d], [[BS * P + BS, 32], [P, BS], [1, BS]])
                                 ).then_inc(pk_in, 16)

            def unpack(b):
                sp.wait_ge(solved, b + 1)
                for n, d, p0 in batch(b):
                    for kind in range(2):
                        src = sub["x" if kind == d else "xt"]
                        sp.dma_start(view(d_rt[n, d, kind], [[BS * BS, 32], [1, BS * BS]]), src[p0:p0 + 32, :, :]
                                     ).then_inc(st_rt[d], 16)

            for n in range(28):
                col = strip_col(n)
                load_w(U_MI + n, n % 2, w_mi_v[:, :, col:col + P], KD)
                if n == 1:
                    sp.wait_ge(mm_done, U_MI)
                    sp.dma_start(wab[:, :, :], w_mi_v[:, :, AB0:AB0 + NAB]).then_inc(in_wab, 16)
                    sp.dma_start(tri[:, :, :], consts[:, C_TRI:C_TRI + 2 * P].rearrange("p (a b) -> p a b", a=2)
                                 ).then_inc(in_tri, 16)
                    sp.dma_start(negf[:, :, :], consts[:, C_NEG:C_NEG + 2 * P].rearrange("p (a b) -> p a b", a=2)
                                 ).then_inc(in_tri, 16)
                    sp.dma_start(sub["mask"][:, :, :], consts[:, C_SUB:C_SUB + BS * BS].rearrange(
                        "p (a b) -> p a b", a=BS)).then_inc(in_tri, 16)
                    sp.dma_start(gsm["adt"][:, 0:8], a_log.rearrange("a b h -> a (b h)").to_broadcast([P, 8])
                                 ).then_inc(in_adt, 16)
                    sp.dma_start(gsm["adt"][:, 8:16], dt_bias.rearrange("a b h -> a (b h)").to_broadcast([P, 8])
                                 ).then_inc(in_adt, 16)
                g = n - PREP0 - 4
                if g >= 0:
                    prep_store(g)
                if g == 3:
                    pack(0)
                if g == 6:
                    unpack(0)
                if g == 7:
                    pack(1)
            prep_store(9)
            w_mo_v = w_mo[0].rearrange("(k p) f -> p k f", p=P)
            for j in range(2):
                load_w(U_MO + j, j % 2, w_mo_v[:, :, P * j:P * j + P], KD)
            unpack(1)
            pack(2)
            sp.wait_ge(y_rdy, 4)
            sp.dma_start(lev[:, :, :], consts[:, C_LEV:C_LEV + 2 * LEVELS * P].rearrange("p (a b) -> p a b", b=P)
                         ).then_inc(in_lev, 16)
            sp.dma_start(blk[:, :], consts[:, C_BLK:C_BLK + P]).then_inc(in_lev, 16)
            sp.wait_ge(mm_done, U_MO)

            def dn_load(n):
                for d in range(2):
                    if n > 1:
                        sp.wait_ge(t_rdy[d], 3 * (n - 2) + 1)
                        sp.wait_ge(rr_rdy[d], 4 * (n - 2) + 1)
                    sp.wait_ge(st_rt[d], 32 * (n + 1))
                    for kind in range(2):
                        sp.dma_start(rt16[d][:, n % 2, kind, :].rearrange("p (h c) -> p h c", h=HEADS),
                                     view(d_rt[n, d, kind], [[BS, P], [P * BS, HEADS], [1, BS]])
                                     ).then_inc(in_rt[n % 2][d], 16)
                    if n > 0:
                        sp.wait_ge(nt_rdy[d], 3 * n)
                    sp.wait_ge(st_lt[d], 16 * (n + 1))
                    sp.dma_start(LT[d][:, :, :], view(d_lt[n, d], [[P, P], [HPL, HEADS], [1, P]])
                                 ).then_inc(in_lt[d], 16)
                for d in range(2):
                    if n > 0:
                        sp.wait_ge(o_mm[d], n)
                    sp.wait_ge(st_qk[d], 16 * (2 * n + 1))
                    sp.dma_start(QK[d][:, :, :], view(d_qk[n, d], [[CW, P], [1, CW]])).then_inc(in_qk[d], 16)
                    if n > 0:
                        sp.dma_start(qg[d][:, :, :], view(d_qg[n, d], [[CW, P], [1, CW]])).then_inc(in_qk[d], 16)

            dn_load(0)
            sp.wait_ge(tok_tr, 10)
            for d, state in enumerate((state_f, state_b)):
                sp.dma_start(Sc[d][:, :, :], state[0, 0].rearrange("h k v -> k h v")).then_inc(in_s[d], 16)
            dn_load(1)
            unpack(2)
            for n in range(2, NC):
                dn_load(n)
            for j in range(2, KD):
                load_w(U_MO + j, j % 2, w_mo_v[:, :, P * j:P * j + P], KD)
            with sp.Fori(0, KF) as i:
                for b in range(2):
                    load_w(U_F2I + 2 * i + b, b, w_in_v[1][:, :, bass.ds(P * i + b * FF, P)], KD)
            with sp.Fori(0, KD) as j:
                for b in range(2):
                    load_w(U_F2O + 2 * j + b, b, w_out_v[1][:, KH * b:KH * b + KH, bass.ds(P * j, P)], KH)
            for t in range(NC):
                sp.wait_ge(y_fin, t + 1)
                dst = y_prompt[0] if t == 0 else y_sample[0, (t - 1) * P:t * P, :]
                sp.dma_start(dst, yo[:, t, :]).then_inc(out_done, 16)
            sp.wait_ge(out_done, 16 * NC)
            sp.wait_ge(st_done, 32)

        @block.tensor
        def _(pe):
            def unit(u, slot, kt, hi, lo, a_slot, start=True, stop=True, k0=0, h_wait=None, ready=True):
                pe.wait_ge(lo_ready, u + 1)
                for k in range(kt):
                    if h_wait is not None:
                        pe.wait_ge(*h_wait(k))
                    wh = w_hi[:, slot, k * P:k * P + P]
                    wl = w_lo[:, slot, k * P:k * P + P]
                    for n, (w, m) in enumerate(((wh, hi), (wh, lo), (wl, hi))):
                        for b in range(2):
                            last = pe.matmul(acc[a_slot][b], w, m[:, k0 + k, b * TH:b * TH + TH],
                                             start=start and k == 0 and n == 0,
                                             stop=stop and k == kt - 1 and n == 2)
                last.then_inc(mm_done, 1)

            def acc_wait(a_half, slot):
                if not (isinstance(a_half, int) and a_half == 0):
                    pe.wait_ge(acc_free[slot], a_half)

            def sum_squares(m, src):
                pe.wait_ge(ssq_rdy, KD * (m + 1))
                for b in range(2):
                    last = pe.matmul(sums[b], ones_t, src[:, b * TH:b * TH + TH], start=True, stop=True)
                last.then_inc(sum_mm, 1)

            pe.wait_ge(in_id, 16)
            pe.wait_ge(in_vec, 10 * 16)
            pe.transpose(ps[0][:, 0:NROWS], vrow[:, :], ident[0:NROWS, 0:NROWS])
            pe.transpose(ps[0][:, P:P + 9 * KD], brow[:, :], ident[0:9 * KD, 0:9 * KD]).then_inc(vec_tr, 1)
            pe.wait_ge(in_x, 32)
            for n in range(10):
                if n >= 2:
                    pe.wait_ge((x_evA, x_evB)[n % 2], n // 2)
                for m in range(4):
                    k, t = divmod(4 * n + m, NC)
                    last = pe.transpose(ps[2 + n % 2][:, m * P:m * P + P], xin[:, t, k * P:k * P + P], ident[:, :])
                last.then_inc(x_tr, 1)

            def ada_step(n, s, k, width):
                pe.wait_ge(ada_in[s], 16 * (n // ADA + 1) if isinstance(n, int) else n)
                for g in range(4):
                    last = pe.matmul(adap[32 * g:32 * g + 32, 0:width], ccol[:, k, :],
                                     ada_w[:, s, g * width:(g + 1) * width], start=k == 0, stop=k == KD - 1)
                last.then_inc(ada_mm, 1)

            def ada_turn(n, blocks):
                pe.wait_ge(ada_row, n + 1)
                if not (isinstance(n, int) and n == 0):
                    pe.wait_ge(mod_rdy, n)
                for b in range(blocks):
                    last = pe.transpose(adat[:, b * P:b * P + P], ada_r[:, b * P:b * P + P], ident[:, :])
                last.then_inc(ada_tr, 1)

            pe.wait_ge(c_rdy, 1)
            for k in range(KD):
                ada_step(k, k % ADA, k, 512)
                if k == 3:
                    sum_squares(0, ssq_h)
            ada_turn(0, 4)

            def first_pair(u0, a0, h0):
                for b in range(2):
                    acc_wait(a0 // 2, b)
                    pe.wait_ge(lo_ready, u0 + b + 1)
                for k in range(KD):
                    pe.wait_ge(h_rdy, h0 + k + 1)
                    for s in range(2):
                        wh, wl = (w[:, s, k * P:k * P + P] for w in (w_hi, w_lo))
                        for n, (w, m) in enumerate(((wh, h_hi), (wh, h_lo), (wl, h_hi))):
                            for b in range(2):
                                last = pe.matmul(acc[s][b], w, m[:, k, b * TH:b * TH + TH],
                                                 start=k == 0 and n == 0, stop=k == KD - 1 and n == 2)
                        if k == KD - 1:
                            last.then_inc(mm_done, 1)

            def swiglu_in(i, u0, a0, kt_next=None, extra=(), h_wait=None):
                if h_wait is not None:
                    first_pair(u0, a0, h_wait)
                    for step in extra:
                        step()
                    return
                for b in range(2):
                    acc_wait(a0 // 2 + i, b)
                    unit(u0 + 2 * i + b, b, KD, h_hi, h_lo, b)
                    for step in extra[2 * b:2 * b + 2]:
                        step()

            def with_ada(i, s, half, n_of, width, first_wait=None):
                steps = []
                for k in range(4):
                    kk = 4 * half + k
                    steps.append(lambda kk=kk, k=k: ada_step(n_of(kk), k, kk, width))
                swiglu_in(i, U_F1I, A_F1I, extra=steps, h_wait=first_wait)

            def slab(s, first=False):
                for half in range(2):
                    with_ada(2 * s + half, s, half,
                             (lambda kk: 8 * (s + 1) + kk) if isinstance(s, int) else
                             (lambda kk: 16 * (2 * s + 3 + kk // 4)), 512 if not isinstance(s, int) or s < 3 else 256,
                             0 if first and half == 0 else None)
            slab(0, first=True)
            ada_turn(1, 4)
            with pe.Fori(1, 3) as s:
                slab(s)
                ada_turn(s + 1, 4)
            slab(3)
            ada_turn(4, 2)
            with pe.Fori(8, KF) as i:
                swiglu_in(i, U_F1I, A_F1I)

            def swiglu_out(u0, a0, g0, after=lambda j: None):
                for j in range(KD):
                    s = j % 2
                    acc_wait(a0 // 2 + j // 2, s)
                    for b in range(2):
                        unit(u0 + 2 * j + b, b, KH, g_hi, g_lo, s, start=b == 0, stop=b == 1, k0=KH * b,
                             h_wait=(lambda k, b=b: (g_rdy, g0 + KH * b + k + 1)) if j == 0 else None)
                    after(j)

            swiglu_out(U_F1O, A_F1O, 0)
            sum_squares(1, ssq_h)

            hs = lambda t, h: t[:, h * P:h * P + P]

            def row(n, d):
                pe.wait_ge(gtri_rdy[d], n + 1)
                if n > 0:
                    pe.wait_ge(dt_rdy[d], n)
                pe.matmul(ps[4 + d][:, :], ones_t, gtri[d][:, :, :], start=True, stop=True).then_inc(row_rdy[d], 1)

            def mask_row(n, d):
                if n > 0:
                    pe.wait_ge(erow_rdy[d], n)
                pe.matmul(ps[4 + d][:, :], identb[:, :], negb[:, d:d + 1, :].to_broadcast([P, HEADS, P]),
                          start=False, stop=True, skip_group_check=True).then_inc(rowm[d], 1)

            def products(n, d):
                t = chunk(n, d) * P
                if n == 0 and d == 0:
                    pe.wait_ge(qn_rdy, 4)
                else:
                    pe.wait_ge(lt_rdy[1 - d], n + d)
                    pe.wait_ge(qk_rdy[1 - d], n + d)
                for h in range(HEADS):
                    kt = qkv[:, 4 + h, t:t + P]
                    pe.matmul(hs(ps[6], h), kt, kt, start=True, stop=True)
                    last = pe.matmul(hs(ps[7], h), kt, qkv[:, h, t:t + P], start=True, stop=True)
                last.then_inc(kk_rdy[d], 1)

            first_pair(U_MI, A_MI, KD)
            for n in range(1, 28):
                if n > 1:
                    acc_wait(A_MI // 2 + n // 2, n % 2)
                    unit(U_MI + n, n % 2, KD, h_hi, h_lo, n % 2)
                if 1 <= n <= 4:
                    pe.wait_ge(q2_rdy, n)
                    if n > 1:
                        pe.wait_ge(ss_rdy, n - 1)
                    for b in range(2):
                        last = pe.matmul(sums[b], ones_t, sa[:, b * TH:b * TH + TH], start=True, stop=True)
                    last.then_inc(ssm, 1)
                if n == 11:
                    pe.wait_ge(wab_rdy, 1)
                    pe.wait_ge(ss_rdy, 4)
                    for k in range(KD):
                        for i, (w, m) in enumerate(((wab_hi, h_hi), (wab_hi, h_lo), (wab_lo, h_hi))):
                            for b in range(2):
                                last = pe.matmul(sums[b][0:NAB, :], w[:, k, :], m[:, k, b * TH:b * TH + TH],
                                                 start=k == 0 and i == 0, stop=k == KD - 1 and i == 2)
                    last.then_inc(ab_mm, 1)
                if n == 12:
                    pe.wait_ge(ab_ev, 1)
                    for t in range(NC):
                        last = pe.transpose(ps[6][:, t * NAB:(t + 1) * NAB], abt[0:NAB, t * P:t * P + P],
                                            ident[0:NAB, 0:NAB])
                    last.then_inc(ab_tr, 1)
                if n == 14:
                    pe.wait_ge(dve_g, 1)
                    pe.wait_ge(in_tri, 48)
                    for d in range(2):
                        gv = gsm["g"][:, d].rearrange("p c h -> p (c h)")
                        pe.matmul(ps[7][:, 32 * d:32 * d + 20], tri[:, d, :], gv, start=True, stop=True)
                        last = pe.matmul(ps[7][:, 64 + 32 * d:64 + 32 * d + 20], ones_t, gv, start=True, stop=True)
                    last.then_inc(gsum, 1)
                g = n - PREP0 - 1
                if 0 <= g < GROUPS_DN:
                    mask_row(*divmod(g, 2))
                    products(*divmod(g, 2))
                if 0 <= g + 1 < GROUPS_DN:
                    row(*divmod(g + 1, 2))
            for n in range(10):
                t, isv = divmod(n, 2)
                if n == 0:
                    pe.wait_ge(qs_rdy, 12)
                if n < 2:
                    acc_wait(A_MO // 2, 0)
                else:
                    pe.wait_ge((tok_evA, tok_evB)[n % 2], n // 2)
                for h in range(HEADS):
                    last = pe.transpose(ps[n % 2][:, h * P:h * P + P],
                                        qkv[:, (8 if isv else 4) + h, t * P:t * P + P], ident[:, :])
                last.then_inc(tok_tr, 1)
            acc_wait(A_MO // 2, 1)
            pe.wait_ge(tok_evA, 5)
            pe.wait_ge(tok_evB, 5)
            bank = [[ps[4 * d + i] for i in range(4)] for d in range(2)]

            def level_x(n, d, m):
                pe.wait_ge(nt_rdy[d], 3 * n + m + 1)
                pe.wait_ge(t_rdy[d], 3 * n + m + 1)
                if n > 0 or m > 0:
                    pe.wait_ge(xm_rdy[d], 3 * n + m)
                nt = (NTa, NTb)[(3 * n + m) % 2][d]
                for h in range(HEADS):
                    last = pe.matmul(hs(bank[d][3], h), nt[:, h, :], Tm[d][:, h, :], start=True, stop=True)
                last.then_inc(x_mm[d], 1)

            def level_tr(n, d, m):
                R = Rm[n % 2][d]
                pe.wait_ge(xm_rdy[d], 3 * n + m + 1)
                pe.wait_ge(rr_rdy[d], 4 * n + m + 1)
                if m == 0 and n > 1:
                    pe.wait_ge(wt_rdy[d], n - 1)
                if m == 0 and n > 0:
                    pe.wait_ge(o_read[d], n)
                for h in range(HEADS):
                    if m < LEVELS - 1:
                        pe.matmul(hs(bank[d][0], h), R[:, h, :], Xm[d][:, h, :], start=True, stop=True)
                    last = pe.matmul(hs(bank[d][2], h), Xm[d][:, h, :], R[:, h, :], start=True, stop=True)
                last.then_inc(tr_mm[d], 1)

            def w_product(n, d):
                pe.wait_ge(rr_rdy[d], 4 * n + 4)
                pe.wait_ge(ke_rdy[d], n)
                pe.wait_ge(t_rdy[d], 3 * n + 3)
                for h in range(HEADS):
                    last = pe.matmul(hs(bank[d][0], h), ke[d][:, h, :], Rm[n % 2][d][:, h, :], start=True, stop=True)
                last.then_inc(w_mm[d], 1)

            def v_product(n, d, s_in):
                c0 = chunk(n, d)
                pe.wait_ge(rr_rdy[d], 4 * n + 4)
                if n > 0:
                    pe.wait_ge(s_rdy[d], n)
                if n == 1:
                    pe.wait_ge(in_s[d], 16)
                for h in range(HEADS):
                    last = pe.matmul(hs(bank[d][1], h), Rm[n % 2][d][:, h, :], hs(vtok[:, c0, :], h),
                                     start=True, stop=n == 0)
                    if n > 0:
                        if h == 0:
                            pe.wait_ge(wt_rdy[d], n)
                        last = pe.matmul(hs(bank[d][1], h), WT[d][:, h, :], s_in[:, h, :], start=False, stop=True)
                last.then_inc(v_mm[d], 1)

            def s_product(n, d):
                pe.wait_ge(vn_rdy[d], n + 1)
                pe.wait_ge(kg_rdy[d], n + 1)
                for h in range(HEADS):
                    last = pe.matmul(hs(bank[d][1], h), kg[d][:, h, :], VN[d][:, h, :], start=True, stop=True)
                last.then_inc(s_mm[d], 1)

            def o_product(n, d, s_in):
                pe.wait_ge(vn_rdy[d], n + 1)
                pe.wait_ge(rr_rdy[d], 4 * n + 4)
                pe.wait_ge(in_qk[d], 16 * (2 * n + 1))
                for h in range(HEADS):
                    last = pe.matmul(hs(bank[d][2], h), VN[d][:, h, :], QK[d][:, h, :], start=True, stop=n == 0)
                    if n > 0:
                        last = pe.matmul(hs(bank[d][2], h), s_in[:, h, :], qg[d][:, h, :], start=False, stop=True)
                last.then_inc(o_mm[d], 1)

            s_of = lambda n, d: {0: None, 1: Sc[d], 2: Sa[d], 3: Sc[d], 4: Sa[d]}[n]
            for n in range(-1, NC):
                if n > 0:
                    for d in range(2):
                        w_product(n, d)
                if n >= 0:
                    for d in range(2):
                        v_product(n, d, s_of(n, d))
                if n < NC - 1:
                    for d in range(2):
                        level_x(n + 1, d, 0)
                if n >= 0:
                    for d in range(2):
                        if n < NC - 1:
                            s_product(n, d)
                        o_product(n, d, s_of(n, d))
                if n < NC - 1:
                    for m in range(LEVELS):
                        for d in range(2):
                            if m > 0:
                                level_x(n + 1, d, m)
                        for d in range(2):
                            level_tr(n + 1, d, m)

            for h in range(HEADS):
                pe.wait_ge(osq_rdy, h + 1)
                pe.wait_ge(oq_rdy, h + 1)
                if h > 0:
                    pe.wait_ge(ort_rdy, h)
                else:
                    pe.wait_ge(o_read[0], NC)
                    pe.wait_ge(o_read[1], NC)
                for b in range(2):
                    pe.matmul(sums[b], ones_t, oq[:, h, b * TH:b * TH + TH], start=True, stop=False)
                    last = pe.matmul(sums[b], ones_t, osq[:, b * TH:b * TH + TH], start=False, stop=True)
                last.then_inc(osum, 1)

            for j in range(KD):
                if j == 0:
                    pe.wait_ge(o_read[0], NC)
                acc_wait(A_MO // 2 + j // 2, j % 2)
                unit(U_MO + j, j % 2, KD, h_hi, h_lo, j % 2, h_wait=(lambda k: (yl_rdy, k + 1)) if j == 0 else None)
            sum_squares(2, ssq_g)

            swiglu_in(0, U_F2I, A_F2I, h_wait=2 * KD)
            with pe.Fori(1, KF) as i:
                swiglu_in(i, U_F2I, A_F2I)

            def turn_y(j):
                pe.wait_ge(xg_rdy, j + 1)
                if j > 0:
                    pe.wait_ge(y_ev, j)
                for t in range(NC):
                    last = pe.transpose(ps[6 + t // 4][:, t % 4 * P:t % 4 * P + P], xg[:, j % 2, t * P:t * P + P],
                                        ident[:, :])
                last.then_inc(y_tr, 1)

            swiglu_out(U_F2O, A_F2O, KF, after=lambda j: turn_y(j - 1) if j > 0 else None)
            turn_y(KD - 1)
            pe.wait_ge(ssq_rdy, 4 * KD)
            for t in range(NC):
                last = pe.matmul(ps[4][:, t:t + 1], ssq_h[:, t * P:t * P + P], ones[:, :], start=True, stop=True)
            last.then_inc(y_sum, 1)

        @block.scalar
        def _(act):
            def split_hi(u, slot, kt, u_half, first=False):
                act.wait_ge(w_in[slot], 16 * u_half + 16)
                if not first:
                    act.wait_ge(mm_done, u - 1)
                nc.scalar.activation(w_hi[:, slot, 0:kt * P], w_raw[:, slot, 0:kt * P], ACT.Copy
                                     ).then_inc(hi_ready, 1)

            act.dma_start(vrow[R_CTX:R_CTX + 8, :], c_ctx.rearrange("(k p) -> k p", p=P)).then_inc(in_vec, 16)
            act.dma_start(vrow[R_C:R_C + 8, :], c[0].rearrange("(k p) -> k p", p=P)).then_inc(in_vec, 16)
            for row, v in ((R_N1, norm1[0]), (R_NM, norm_mix[0]), (R_N2, norm2[0]), (R_NF, norm_f)):
                act.dma_start(vrow[row:row + 8, :], v.rearrange("(k p) -> k p", p=P)).then_inc(in_vec, 16)
            act.dma_start(vrow[R_CONV:R_CONV + 12, :],
                         conv_w[0].rearrange("w (k p) -> (w k) p", p=P)).then_inc(in_vec, 16)
            act.dma_start(vrow[R_DNC:R_DNC + 36, :],
                         dn_conv_w[0].rearrange("w (k p) -> (w k) p", p=P)).then_inc(in_vec, 16)
            act.dma_start(vrow[R_DNN:R_DNN + 1, :], dn_norm).then_inc(in_vec, 16)
            act.dma_start(brow[:, :], b_ada[0].rearrange("(k p) -> k p", p=P)).then_inc(in_vec, 16)
            act.dma_start(ident[:, :], consts[:, C_ID:C_ID + P]).then_inc(in_id, 16)
            act.wait_ge(vec_tr, 1)
            nc.scalar.activation(vec[:, :], ps[0][:, 0:NROWS], ACT.Copy).then_inc(vec_rdy, 1)
            nc.scalar.activation(bada[:, :], ps[0][:, P:P + 9 * KD], ACT.Copy).then_inc(vec_rdy, 1)
            act.wait_ge(misc_set, 4)
            act.wait_ge(vec_rdy, 2)
            nc.scalar.activation(ccol[:, :, 0:2], vec[:, 0:16].rearrange("p (i k) -> p k i", i=2), ACT.Silu
                                 ).then_inc(c_rdy, 1)
            xf = x[:, :, :].rearrange("p k t -> p (k t)")
            for n in range(0, 10, 2):
                act.wait_ge(x_tr, n + 1)
                nc.scalar.activation(xf[:, n * 512:n * 512 + 512], ps[2][:, :], ACT.Copy).then_inc(x_evA, 1)

            def square(n, k, wait, odd=sq_h):
                act.wait_ge(*wait)
                if n > 1:
                    act.wait_ge(ssq_rdy, n - 1)
                nc.scalar.activation((sa, odd)[k % 2][:, :], x[:, k, :], ACT.Square).then_inc(sq_rdy, 1)

            def ada_out(n, width):
                act.wait_ge(ada_mm, 8 * n + 8)
                if not (isinstance(n, int) and n == 0):
                    act.wait_ge(ada_tr, n)
                nc.scalar.activation(ada_r[:, 0:width], adap[:, 0:width], ACT.Copy).then_inc(ada_row, 1)

            for k in range(KD):
                act.wait_ge(x_evA, 5)
                square(k, k, (x_evB, 5))

            def norm(m, kt_next=None, n_sum=0):
                act.wait_ge(sum_mm, m + 1)
                nc.scalar.activation(halves(rinv[:, :])[:, 0, :], sums[0], ACT.Sqrt, bias=eps[:, :], scale=1.0 / D)
                nc.scalar.activation(halves(rinv[:, :])[:, 1, :], sums[1], ACT.Sqrt, bias=eps[:, :], scale=1.0 / D
                                     ).then_inc(rt_rdy, 1)
                if m == 0:
                    ada_out(0, 512)
                    for u in range(2):
                        split_hi(u, u, KD, 0, first=True)
                act.wait_ge(gain_rdy, 1 if m == 0 else 2)
                for k in range(KD):
                    act.wait_ge(*tn_wait(m, k))
                    for i, t0, t1 in GROUPS:
                        last = nc.scalar.activation(h_hi[:, k, t0:t1], tn[:, k, t0:t1], ACT.Identity,
                                                    bias=mod[:, 3 * m * KD + k, i:i + 1],
                                                    scale=gain[:, m, k, i:i + 1])
                    last.then_inc(hh_rdy, 1)

            norm(0)

            def gate_in(i, u0, i0):
                act.wait_ge(mm_done, u0 + 2 * i + 1)
                if not (isinstance(i, int) and i0 + i == 0):
                    act.wait_ge(g_rdy, i + i0)
                for b in range(2):
                    last = nc.scalar.activation(sa[:, b * TH:b * TH + TH], acc[0][b], ACT.Silu)
                last.then_inc(sa_rdy, 1)

            def swiglu_in(i, u0, i0, kt_next=KD, last=False):
                if not (isinstance(i, int) and i == 0):
                    split_hi(u0 + 2 * i + 1, 1, KD, u0 // 2 + i)
                gate_in(i, u0, i0)
                act.wait_ge(sa_rdy, i + i0 + 1)
                act_free(0)
                split_hi(u0 + 2 * i + 2, 0, kt_next, u0 // 2 + i + 1)

            def act_free(slot):
                act.sem_inc(acc_free[slot], 1)

            def slab(s, width=512):
                for half in range(2):
                    swiglu_in(2 * s + half, U_F1I, 0)
                ada_out(s + 1, width)
            slab(0)
            with act.Fori(1, 3) as s:
                slab(s)
            slab(3, 256)
            with act.Fori(8, KF - 1) as i:
                swiglu_in(i, U_F1I, 0)
            swiglu_in(KF - 1, U_F1I, 0, kt_next=KH)

            def swiglu_out(u0, n0, kt_next, x0, after=lambda j: None):
                for j in range(KD):
                    split_hi(u0 + 2 * j + 1, 1, KH, u0 // 2 + j)
                    if j > 0:
                        square(n0 + j - 1, j - 1, (x_upd, x0 + j))
                        after(j - 1)
                    if j < KD - 1:
                        split_hi(u0 + 2 * j + 2, 0, KH, u0 // 2 + j + 1)
                    elif kt_next:
                        split_hi(u0 + 2 * j + 2, 0, kt_next, u0 // 2 + j + 1)
                square(n0 + KD - 1, KD - 1, (x_upd, x0 + KD))

            swiglu_out(U_F1O, KD, KD, 0)
            split_hi(U_MI + 1, 1, KD, U_MI // 2)
            norm(1)

            flat = lambda t: t[:, :, :].rearrange("p h j -> p (h j)")
            for n in range(28):
                u = U_MI + n + 1
                if n == 8:
                    act.wait_ge(in_wab, 16)
                    nc.scalar.activation(wab_hi[:, :, :], wab[:, :, :], ACT.Copy).then_inc(wab_h, 1)
                if 0 < n < 27:
                    split_hi(u, (n + 1) % 2, KD, u // 2)
                if n == 12:
                    act.wait_ge(ab_mm, 1)
                    for b in range(2):
                        last = nc.scalar.activation(abt[0:NAB, b * TH:b * TH + TH], sums[b][0:NAB, :], ACT.Copy)
                    last.then_inc(ab_ev, 1)
                if n == 13:
                    act.wait_ge(ab_rdy, 3)
                    nc.scalar.activation(gsm["t1"][:, :, :, :], gsm["t1"][:, :, :, :], ACT.Exp).then_inc(act_g, 1)
                    nc.scalar.activation(gsm["beta"][:, :, :, :], gsm["t3"][:, :, :, :], ACT.Exp).then_inc(act_g, 1)
                    act.wait_ge(in_adt, 32)
                    nc.scalar.activation(gsm["adt"][:, 0:8], gsm["adt"][:, 0:8], ACT.Exp).then_inc(act_g, 1)
                    act.wait_ge(act_g, 3)
                    nc.scalar.activation(gsm["t1"][:, :, :, :], gsm["t1"][:, :, :, :], ACT.Ln, bias=1.0
                                         ).then_inc(act_g, 1)
                if n == 15:
                    act.wait_ge(dve_g, 2)
                    nc.scalar.activation(gsm["eg"][:, :, :, :], gsm["gc"][:, :, :, :], ACT.Exp)
                    nc.scalar.activation(gsm["gl"][:, :, :, :], gsm["gt"][:, :, :, :], ACT.Exp)
                    nc.scalar.activation(gsm["kgs"][:, :, :, :], gsm["t2"][:, :, :, :], ACT.Exp).then_inc(gates, 1)
                g = n - PREP0 - 1
                if 2 <= g < GROUPS_DN:
                    m, d = divmod(g, 2)
                    act.wait_ge(row_rdy[d], m + 1)
                    if m > 1:
                        act.wait_ge(qg_rdy[d], m - 1)
                    nc.scalar.activation(flat(Erow[d]), ps[4 + d][:, :], ACT.Exp).then_inc(erow_rdy[d], 1)
                g -= 1
                if 0 <= g < GROUPS_DN:
                    m, d = divmod(g, 2)
                    act.wait_ge(rowm[d], m + 1)
                    for h in range(HEADS):
                        last = nc.scalar.activation(DT[d][:, h, :], ps[4 + d][:, h * P:h * P + P], ACT.Exp,
                                                    bias=gsm["ngc"][:, d, chunk(m, d), h:h + 1])
                    last.then_inc(dt_rdy[d], 1)
                if 1 <= n <= 4:
                    act.wait_ge(ssm, n)
                    for b in range(2):
                        last = nc.scalar.activation(ss[:, n - 1, b * TH:b * TH + TH], sums[b], ACT.Copy)
                    last.then_inc(ss_rdy, 1)
                if n < 12:
                    act.wait_ge(mm_done, U_MI + n + 1)
                    if n > 0:
                        act.wait_ge(qs_rdy, n)
                    tile = qkv_tile(n)
                    tap = vec[:, R_DNC + 12 + tile:R_DNC + 13 + tile]
                    for b in range(2):
                        last = nc.scalar.activation(cv[:, b * TH:b * TH + TH], acc[n % 2][b], ACT.Identity, scale=tap)
                    last.then_inc(cv_rdy, 1)
                    act.wait_ge(uc_rdy, n + 1)
                    nc.scalar.activation(qkv[:, tile, :], cv[:, :], ACT.Silu).then_inc(qs_rdy, 1)
                    if n < 4:
                        act.wait_ge(qs_rdy, n + 1)
                        if n > 0:
                            act.wait_ge(ssm, n)
                        nc.scalar.activation(sa[:, :], qkv[:, tile, :], ACT.Square).then_inc(q2_rdy, 1)
                elif n < 16:
                    act.wait_ge(mm_done, U_MI + n + 1)
                    for b in range(2):
                        last = nc.scalar.activation(zs[:, n - 12, b * TH:b * TH + TH], acc[n % 2][b], ACT.Silu)
                    last.then_inc(z_rdy, 1)
                    act.wait_ge(z_rdy, n - 11)
                    act_free(n % 2)
                elif n % 3 == 1:
                    act.wait_ge(mm_done, U_MI + n + 1)
                    if n > 16:
                        act.wait_ge(u_rdy, (n - 16) // 3)
                    for b in range(2):
                        last = nc.scalar.activation(cc[:, b * TH:b * TH + TH], acc[n % 2][b], ACT.Copy)
                    last.then_inc(cc_rdy, 1)
                    act.wait_ge(cc_rdy, (n - 16) // 3 + 1)
                    act_free(n % 2)
                if n == 11:
                    act.wait_ge(ss_rdy, 4)
                    for k in range(4):
                        nc.scalar.activation(ss[:, k, :], ss[:, k, :], ACT.Sqrt, bias=eps[:, :]).then_inc(st_rdy, 1)

            def tok(t):
                act.wait_ge(tok_tr, 2 * t + 1)
                if t == 0:
                    for d in range(2):
                        act.wait_ge(st_lt[d], 16 * NC)
                        act.wait_ge(st_qk[d], 16 * (2 * NC - 1))
                nc.scalar.activation(ktok[:, t, :], ps[0][:, :], ACT.Copy).then_inc(tok_evA, 1)
            for t in range(NC):
                tok(t)

            for j in range(2):
                split_hi(U_MO + j, j, KD, U_MO // 2)

            bank = [[ps[4 * d + i] for i in range(4)] for d in range(2)]
            for n in range(-1, NC):
                if n > 0:
                    for d in range(2):
                        act.wait_ge(w_mm[d], n)
                        if n > 1:
                            act.wait_ge(v_mm[d], n)
                        nc.scalar.activation(flat(WT[d]), bank[d][0][:, :], ACT.Copy, scale=-1.0
                                             ).then_inc(wt_rdy[d], 1)
                if n < NC - 1:
                    for m in range(LEVELS):
                        for d in range(2):
                            act.wait_ge(x_mm[d], 3 * (n + 1) + m + 1)
                            if 3 * (n + 1) + m > 0:
                                act.wait_ge(tr_mm[d], 3 * (n + 1) + m)
                            nc.scalar.activation(flat(Xm[d]), bank[d][3][:, :], ACT.Copy).then_inc(xm_rdy[d], 1)
                if n == 0:
                    for d, out in enumerate((s_out_f, s_out_b)):
                        act.wait_ge(s_rdy[d], 1)
                        act.dma_start(out[0, 0].rearrange("h k v -> k h v"), Sb[d][:, :, :]).then_inc(st_done, 16)

            act.wait_ge(v_mm[0], NC)
            act.wait_ge(v_mm[1], NC)
            for h in range(HEADS):
                nc.scalar.activation(oq[:, h, :], qkv[:, h, :], ACT.Square, scale=P * EPS ** 0.5).then_inc(oq_rdy, 1)
            act.wait_ge(st_done, 32)
            for h in range(HEADS):
                if h == 0:
                    act.wait_ge(o_read[0], NC)
                    act.wait_ge(o_read[1], NC)
                else:
                    act.wait_ge(osum, h)
                nc.scalar.activation(osq[:, :], ot[:, h, :], ACT.Square).then_inc(osq_rdy, 1)
                act.wait_ge(osum, h + 1)
                for b in range(2):
                    last = nc.scalar.activation(orr[:, h, b * TH:b * TH + TH], sums[b], ACT.Sqrt, bias=eps_o[:, :],
                                                scale=1.0 / P)
                last.then_inc(ort_rdy, 1)
            act.wait_ge(o_mm[0], NC)
            act.wait_ge(o_mm[1], NC)
            for k in range(KD):
                if k < 4:
                    act.wait_ge(y_rdy, k + 1)
                    src = yc[:, k, :]
                else:
                    act.wait_ge(on_rdy, k - 3)
                    src = ot[:, k - 4, :]
                nc.scalar.activation(h_hi[:, k, :], src, ACT.Copy).then_inc(yh_rdy, 1)
            for j in range(KD):
                u = U_MO + j + 1
                if j > 0:
                    split_hi(u, u % 2, KD, u // 2)
                if j > 0:
                    square(2 * KD + j - 1, j - 1, (x_upd, KD + j), sq_g)
            square(3 * KD - 1, KD - 1, (x_upd, 2 * KD), sq_g)
            split_hi(U_F2I + 1, 1, KD, U_F2I // 2)
            norm(2)
            swiglu_in(0, U_F2I, KF)
            with act.Fori(1, KF - 1) as i:
                swiglu_in(i, U_F2I, KF)
            swiglu_in(KF - 1, U_F2I, KF, kt_next=KH)

            def scale_x(j):
                if j > 1:
                    act.wait_ge(y_tr, j - 1)
                nc.scalar.activation(xg[:, j % 2, :], x[:, j, :], ACT.Identity, scale=vec[:, R_NF + j:R_NF + j + 1]
                                     ).then_inc(xg_rdy, 1)

            def copy_y(j):
                act.wait_ge(y_tr, j + 1)
                nc.scalar.activation(yo[:, 0:4, j * P:j * P + P], ps[6][:, :].rearrange("p (t f) -> p t f", t=4), ACT.Copy)
                nc.scalar.activation(yo[:, 4, j * P:j * P + P], ps[7][:, 0:P], ACT.Copy).then_inc(y_ev, 1)

            def after(j):
                scale_x(j)
                if j > 0:
                    copy_y(j - 1)
            swiglu_out(U_F2O, 3 * KD, None, 2 * KD, after)
            after(KD - 1)
            copy_y(KD - 1)
            act.wait_ge(y_sum, 1)
            nc.scalar.activation(rfin[:, :], ps[4][:, 0:NC], ACT.Sqrt, bias=eps[:, :], scale=1.0 / D).then_inc(y_rt, 1)

        @block.vector
        def _(dve):
            link = seq(dve)

            def split_lo(u, slot, kt):
                dve.wait_ge(hi_ready, u + 1)
                nc.vector.tensor_tensor(w_lo[:, slot, 0:kt * P], w_raw[:, slot, 0:kt * P],
                                        w_hi[:, slot, 0:kt * P].bitcast(F32), ALU.subtract).then_inc(lo_ready, 1)

            nc.vector.memset(ones[:, :], 1.0).then_inc(misc_set, 1)
            nc.vector.memset(eps[:, :], EPS).then_inc(misc_set, 1)
            nc.vector.memset(eps_o[:, :], EPS * EPS * P).then_inc(misc_set, 1)
            nc.vector.memset(ccol[:, :, :], 0.0).then_inc(misc_set, 1)
            xf = x[:, :, :].rearrange("p k t -> p (k t)")
            for n in range(1, 10, 2):
                dve.wait_ge(x_tr, n + 1)
                nc.vector.tensor_copy(xf[:, n * 512:n * 512 + 512], ps[3][:, :]).then_inc(x_evB, 1)

            def ada_cols(n, blocks):
                dve.wait_ge(ada_tr, n + 1)
                if isinstance(n, int) and n == 0:
                    dve.wait_ge(vec_rdy, 2)
                for b in range(blocks):
                    src = adat[:, b * P:b * P + P].rearrange("p (g i) -> p g i", i=32)
                    for i in range(2):
                        lo = 16 * n + b
                        last = nc.vector.tensor_tensor(
                            mod[:, bass.ds(lo, 4, blocks), i], src[:, :, i], bada[:, bass.ds(lo, 4, blocks)], ALU.add)
                last.then_inc(mod_rdy, 1)

            def gains(m, first):
                for i in range(2):
                    last = nc.vector.scalar_tensor_tensor(
                        out=gain[:, m, :, i], in0=mod[:, (3 * m + 1) * KD:(3 * m + 2) * KD, i], scalar=1.0,
                        in1=vec[:, (R_N1, R_NM, R_N2)[m]:(R_N1, R_NM, R_N2)[m] + 8], op0=ALU.add, op1=ALU.mult)
                return last

            def add_squares(m, k, dst, odd=sq_h):
                dve.wait_ge(sq_rdy, KD * m + k + 1)
                src = (sa, odd)[k % 2]
                if k == 0:
                    nc.vector.tensor_copy(dst[:, :], src[:, :]).then_inc(ssq_rdy, 1)
                else:
                    dve.wait_ge(ssq_rdy, KD * m + k)
                    nc.vector.tensor_tensor(dst[:, :], dst[:, :], src[:, :], ALU.add).then_inc(ssq_rdy, 1)

            for k in range(KD):
                add_squares(0, k, ssq_h)

            def norm(m):
                dve.wait_ge(rt_rdy, m + 1)
                nc.vector.reciprocal(rinv[:, :], rinv[:, :]).then_inc(r_rdy, 1)
                dve.wait_ge(r_rdy, m + 1)
                for k in range(0, KD, 2 if m == 0 else KD):
                    nc.vector.tensor_tensor(tn[:, k, :], x[:, k, :], rinv[:, :], ALU.mult).then_inc(tn_rdy, 1)
                if m == 0:
                    ada_cols(0, 4)
                    dve.wait_ge(mod_rdy, 1)
                    gains(0, True).then_inc(gain_rdy, 1)
                    for u in range(2):
                        split_lo(u, u, KD)
                    dve.wait_ge(gain_rdy, 1)

                def low(k):
                    dve.wait_ge(hf_rdy, KD * m + k + 1)
                    dve.wait_ge(hh_rdy, KD * m + k + 1)
                    nc.vector.tensor_tensor(h_lo[:, k, :], hf[:, k, :], h_hi[:, k, :].bitcast(F32), ALU.subtract
                                            ).then_inc(h_rdy, 1)
                for k in range(KD):
                    if k > 0:
                        low(k - 1)
                    dve.wait_ge(*tn_wait(m, k))
                    for i, t0, t1 in GROUPS:
                        last = nc.vector.tensor_scalar(hf[:, k, t0:t1], tn[:, k, t0:t1], gain[:, m, k, i:i + 1],
                                                       mod[:, 3 * m * KD + k, i:i + 1], ALU.mult, ALU.add)
                    last.then_inc(hf_rdy, 1)
                low(KD - 1)

            norm(0)

            def gate_out(i, u0, i0):
                dve.wait_ge(mm_done, u0 + 2 * i + 2)
                dve.wait_ge(sa_rdy, i + i0 + 1)
                for b in range(2):
                    last = nc.vector.tensor_tensor(sa[:, b * TH:b * TH + TH], sa[:, b * TH:b * TH + TH], acc[1][b],
                                                   ALU.mult)
                last.then_inc(gp_rdy, 1)
                dve.wait_ge(gp_rdy, i + i0 + 1)
                dve.sem_inc(acc_free[1], 1)
                gh = g_hi[:, bass.ds(i, 1), :].rearrange("p a t -> p (a t)")
                gl = g_lo[:, bass.ds(i, 1), :].rearrange("p a t -> p (a t)")
                nc.vector.tensor_copy(gh, sa[:, :]).then_inc(gh_rdy, 1)
                dve.wait_ge(gh_rdy, i + i0 + 1)
                nc.vector.tensor_tensor(gl, sa[:, :], gh.bitcast(F32), ALU.subtract).then_inc(g_rdy, 1)

            def swiglu_in(i, u0, i0, kt_next=KD):
                if not (isinstance(i, int) and i == 0):
                    split_lo(u0 + 2 * i + 1, 1, KD)
                split_lo(u0 + 2 * i + 2, 0, kt_next)
                gate_out(i, u0, i0)

            def slab(s, blocks=4):
                for half in range(2):
                    swiglu_in(2 * s + half, U_F1I, 0)
                ada_cols(s + 1, blocks)
            slab(0)
            with dve.Fori(1, 3) as s:
                slab(s)
            slab(3, 2)
            dve.wait_ge(mod_rdy, 5)
            gains(1, False)
            gains(2, False)
            for m in range(3):
                last = nc.vector.tensor_scalar(gate[:, m, :, :], mod[:, (3 * m + 2) * KD:(3 * m + 3) * KD, :],
                                               1.0 if m == 1 else 0.5, None, ALU.mult)
            last.then_inc(gain_rdy, 1)
            with dve.Fori(8, KF - 1) as i:
                swiglu_in(i, U_F1I, 0)
            swiglu_in(KF - 1, U_F1I, 0, kt_next=KH)

            def residual(m, j, done, a_slot, n):
                dve.wait_ge(mm_done, done)
                if j == 0:
                    dve.wait_ge(gain_rdy, 2)
                for bnk, b0, b1, i, t0 in PIECES:
                    last = nc.vector.scalar_tensor_tensor(
                        out=x[:, j, t0:t0 + b1 - b0], in0=acc[a_slot][bnk][:, b0:b1], scalar=gate[:, m, j, i:i + 1],
                        in1=x[:, j, t0:t0 + b1 - b0], op0=ALU.mult, op1=ALU.add)
                last.then_inc(x_upd, 1)
                dve.wait_ge(x_upd, n + 1)
                dve.sem_inc(acc_free[a_slot], 1)

            def swiglu_out(u0, m, x0, kt_next, norm_m):
                for j in range(KD):
                    split_lo(u0 + 2 * j + 1, 1, KH)
                    if j < KD - 1:
                        split_lo(u0 + 2 * j + 2, 0, KH)
                    elif kt_next:
                        split_lo(u0 + 2 * j + 2, 0, kt_next)
                    if j > 0:
                        add_squares(norm_m, j - 1, ssq_h)
                    residual(m, j, u0 + 2 * j + 2, j % 2, x0 + j)
                add_squares(norm_m, KD - 1, ssq_h)

            swiglu_out(U_F1O, 0, 0, KD, 1)
            split_lo(U_MI + 1, 1, KD)
            norm(1)

            def taps(n, a_slot):
                dve.wait_ge(cv_rdy, n + 1)
                a = acc[a_slot]
                tile = qkv_tile(n)
                before, after = (vec[:, R_DNC + 12 * w + tile:R_DNC + 12 * w + tile + 1] for w in (0, 2))
                for step, (bnk, b0, b1, t0, tap) in enumerate((
                        (0, 0, TP - 1, 1, before), (0, TP, TH, TP + 1, before), (1, 0, TH - 1, TH + 1, before),
                        (0, 1, TP, 0, after), (0, TP + 1, TH, TP, after), (1, 0, TH, TH - 1, after))):
                    ins = nc.vector.scalar_tensor_tensor(out=cv[:, t0:t0 + b1 - b0], in0=a[bnk][:, b0:b1], scalar=tap,
                                                         in1=cv[:, t0:t0 + b1 - b0], op0=ALU.mult, op1=ALU.add)
                    if step in (2, 5):
                        link(ins)
                dve.sem_inc(acc_free[a_slot], 1)
                dve.sem_inc(uc_rdy, 1)

            G = gsm

            def gates_first():
                dve.wait_ge(ab_tr, 1)
                dve.wait_ge(in_adt, 32)
                ab4 = G["ab"][:, :].rearrange("p (c a h) -> p a c h", c=NC, a=4)
                link(nc.vector.tensor_copy(G["ab"][:, :], ps[6][:, 0:NC * NAB]))
                for d in range(2):
                    dtb = G["adt"][:, 8 + 4 * d:12 + 4 * d].rearrange("p (a h) -> p a h", a=1).to_broadcast([P, NC, HEADS])
                    last = nc.vector.tensor_tensor(G["g"][:, d], ab4[:, 2 * d], dtb, ALU.add)
                link(last)
                link(nc.vector.tensor_scalar(G["t2"][:, :, :, :], G["g"][:, :, :, :], -1.0, None, ALU.mult))
                nc.vector.tensor_tensor(G["t1"][:, :, :, :], G["g"][:, :, :, :], G["t2"][:, :, :, :], ALU.min
                                        ).then_inc(ab_rdy, 1)
                for d in range(2):
                    nc.vector.tensor_scalar(G["t3"][:, d], ab4[:, 2 * d + 1], -1.0, None, ALU.mult).then_inc(ab_rdy, 1)
                dve.wait_ge(ab_rdy, 3)
                link(nc.vector.tensor_scalar(G["t2"][:, :, :, :], G["g"][:, :, :, :], 0.0, None, ALU.max))

            def gates_second():
                dve.wait_ge(act_g, 4)
                link(nc.vector.tensor_tensor(G["t2"][:, :, :, :], G["t2"][:, :, :, :], G["t1"][:, :, :, :], ALU.add))
                for d in range(2):
                    A = G["adt"][:, 4 * d:4 * d + 4].rearrange("p (a h) -> p a h", a=1).to_broadcast([P, NC, HEADS])
                    last = nc.vector.tensor_tensor(G["g"][:, d], G["t2"][:, d], A, ALU.mult)
                link(last)
                nc.vector.tensor_scalar(G["g"][:, :, :, :], G["g"][:, :, :, :], -1.0, None, ALU.mult
                                        ).then_inc(dve_g, 1)
                link(nc.vector.tensor_scalar(G["t3"][:, :, :, :], G["beta"][:, :, :, :], 1.0, None, ALU.add))
                link(nc.vector.reciprocal(G["beta"][:, :, :, :], G["t3"][:, :, :, :]))

            def gates_third():
                dve.wait_ge(gsum, 1)
                flat2 = lambda t, d: t[:, d].rearrange("p c h -> p (c h)")
                for d in range(2):
                    nc.vector.tensor_copy(flat2(G["gc"], d), ps[7][:, 32 * d:32 * d + 20])
                    last = nc.vector.tensor_copy(flat2(G["gt"], d), ps[7][:, 64 + 32 * d:64 + 32 * d + 20])
                link(last)
                nc.vector.tensor_scalar(G["ngc"][:, :, :, :], G["gc"][:, :, :, :], -1.0, None, ALU.mult)
                link(nc.vector.tensor_tensor(G["t2"][:, :, :, :], G["gt"][:, :, :, :], G["gc"][:, :, :, :],
                                             ALU.subtract))
                dve.sem_inc(dve_g, 1)

            def prepare(n, d):
                dve.wait_ge(kk_rdy[d], n + 1)
                dve.wait_ge(dt_rdy[d], n + 1)
                if n > 0:
                    dve.wait_ge(st_lt[d], 16 * n)
                    dve.wait_ge(st_qk[d], 16 * (2 * n - 1))
                for h in range(HEADS):
                    last = nc.vector.scalar_tensor_tensor(
                        out=LTp[d][:, h, :], in0=ps[6][:, h * P:h * P + P], scalar=G["beta"][:, d, chunk(n, d), h:h + 1],
                        in1=DT[d][:, h, :], op0=ALU.mult, op1=ALU.mult)
                last.then_inc(lt_rdy[d], 1)
                nc.vector.tensor_tensor(flat(QKp[d]), ps[7][:, :], flat(DT[d]), ALU.mult).then_inc(qk_rdy[d], 1)

            def substitute(b):
                dve.wait_ge(pk_in, (64, 128, 160)[b])
                if b == 0:
                    dve.wait_ge(in_tri, 48)
                else:
                    dve.wait_ge(st_rt[0], 64 * b)
                    dve.wait_ge(st_rt[1], 64 * b)
                u, neg, xs, xt, tmp, mask = (sub[n] for n in ("u", "n", "x", "xt", "tmp", "mask"))
                half = P // 2
                nc.vector.tensor_tensor(neg[0:half, :, :], u[0:half, :, :], mask[0:half, :, :], ALU.mult)
                nc.vector.tensor_tensor(neg[half:P, :, :], u[half:P, :, :].rearrange("p a b -> p b a"),
                                        mask[half:P, :, :], ALU.mult)
                link(nc.vector.tensor_scalar(xs[:, :, :], mask[:, :, :], 0.0, None, ALU.max))
                for j in range(BS - 2, -1, -1):
                    w = BS - 1 - j
                    link(nc.vector.tensor_tensor(
                        tmp[:, 0:w, 0:w], neg[:, j:j + 1, j + 1:BS].to_broadcast([P, w, w]),
                        xs[:, j + 1:BS, j + 1:BS].rearrange("p k i -> p i k"), ALU.mult))
                    link(nc.vector.tensor_reduce(xs[:, j, j + 1:BS], tmp[:, 0:w, 0:w], mybir.AxisListType.X, ALU.add))
                nc.vector.tensor_copy(xt[:, :, :], xs[:, :, :].rearrange("p a b -> p b a")).then_inc(solved, 1)

            flat = lambda t: t[:, :, :].rearrange("p h j -> p (h j)")
            for n in range(28):
                u = U_MI + n + 1
                if n == 8:
                    dve.wait_ge(wab_h, 1)
                    nc.vector.tensor_tensor(wab_lo[:, :, :], wab[:, :, :], wab_hi[:, :, :].bitcast(F32), ALU.subtract
                                            ).then_inc(wab_rdy, 1)
                if 0 < n < 27:
                    split_lo(u, (n + 1) % 2, KD)
                a_slot = n % 2
                if n == 10:
                    dve.wait_ge(in_tri, 48)
                    nc.vector.tensor_copy(negb[:, :, :], negf[:, :, :])
                    link(nc.vector.tensor_copy(identb[:, :], ident[:, :]))
                if n == 13:
                    gates_first()
                if 0 <= n - PREP0 - 2 < GROUPS_DN:
                    prepare(*divmod(n - PREP0 - 2, 2))
                if n == 15:
                    gates_third()
                if n < 12:
                    taps(n, a_slot)
                elif n < 16:
                    pass
                elif n % 3 == 2:
                    m = (n - 16) // 3
                    dve.wait_ge(mm_done, U_MI + n + 1)
                    dve.wait_ge(cc_rdy, m + 1)
                    for b in range(2):
                        last = nc.vector.tensor_tensor(uu[:, b * TH:b * TH + TH], cc[:, b * TH:b * TH + TH],
                                                       acc[a_slot][b], ALU.mult)
                    last.then_inc(u_rdy, 1)
                    dve.wait_ge(u_rdy, m + 1)
                    dve.sem_inc(acc_free[a_slot], 1)
                    if m == 0:
                        dve.wait_ge(qs_rdy, 12)
                    tap = [vec[:, R_CONV + 4 * w + m:R_CONV + 4 * w + m + 1] for w in range(3)]
                    link(nc.vector.tensor_scalar(cv[:, :], uu[:, :], tap[1], None, ALU.mult))
                    for w in (0, 2):
                        for t0, t1, far in ((0, TP, 1), (TP, T, GRID_W)):
                            o = slice(t0 + far, t1) if w == 0 else slice(t0, t1 - far)
                            i = slice(t0, t1 - far) if w == 0 else slice(t0 + far, t1)
                            ins = nc.vector.scalar_tensor_tensor(out=cv[:, o], in0=uu[:, i], scalar=tap[w],
                                                                 in1=cv[:, o], op0=ALU.mult, op1=ALU.add)
                        link(ins)
                elif n % 3 == 0:
                    m = (n - 16) // 3
                    dve.wait_ge(mm_done, U_MI + n + 1)
                    for b in range(2):
                        last = nc.vector.tensor_tensor(yc[:, m, b * TH:b * TH + TH], cv[:, b * TH:b * TH + TH],
                                                       acc[a_slot][b], ALU.mult)
                    last.then_inc(y_rdy, 1)
                    dve.wait_ge(y_rdy, m + 1)
                    dve.sem_inc(acc_free[a_slot], 1)
                if 12 <= n < 16:
                    k = n - 12
                    dve.wait_ge(st_rdy, k + 1)
                    link(nc.vector.reciprocal(ss[:, k, :], ss[:, k, :]))
                    nc.vector.tensor_tensor(qkv[:, 4 + k, :], qkv[:, 4 + k, :], ss[:, k, :], ALU.mult
                                            ).then_inc(qn_rdy, 1)
                if n == 13:
                    gates_second()
                if n == PREP0 + 7:
                    substitute(0)
                if n == PREP0 + 10:
                    substitute(1)
            for t in range(NC):
                dve.wait_ge(tok_tr, 2 * t + 2)
                if t == 0:
                    for d in range(2):
                        dve.wait_ge(st_lt[d], 16 * NC)
                        dve.wait_ge(st_qk[d], 16 * (2 * NC - 1))
                nc.vector.tensor_copy(vtok[:, t, :], ps[1][:, :]).then_inc(tok_evB, 1)

            for j in range(2):
                split_lo(U_MO + j, j, KD)

            bank = [[ps[4 * d + i] for i in range(4)] for d in range(2)]
            b3 = lambda t: t[:, :].rearrange("p (h j) -> p h j", h=HEADS)
            s_of = lambda n, d: {0: None, 1: Sc[d], 2: Sa[d], 3: Sc[d], 4: Sa[d]}[n]
            for n in range(-1, NC):
                if n >= 0:
                    for d in range(2):
                        dve.wait_ge(v_mm[d], n + 1)
                        if n == 0:
                            dve.wait_ge(gates, 1)
                        beta4 = G["beta"][:, d, chunk(n, d), :].rearrange("p (h a) -> p h a", a=1).to_broadcast(
                            [P, HEADS, P])
                        nc.vector.tensor_tensor(VN[d][:, :, :], b3(bank[d][1]), beta4, ALU.mult).then_inc(vn_rdy[d], 1)
                    for d in range(2):
                        c0 = chunk(n, d)
                        if n < NC - 1:
                            dve.wait_ge(s_mm[d], n + 1)
                            s_in, s_new = s_of(n, d), (Sb if n == 0 else Sa if n in (1, 3) else Sc)[d]
                            if n == 0:
                                nc.vector.tensor_copy(flat(s_new), bank[d][1][:, :]).then_inc(s_rdy[d], 1)
                            else:
                                for h in range(HEADS):
                                    last = nc.vector.scalar_tensor_tensor(
                                        out=s_new[:, h, :], in0=s_in[:, h, :], scalar=G["gl"][:, d, c0, h:h + 1],
                                        in1=bank[d][1][:, h * P:h * P + P], op0=ALU.mult, op1=ALU.add)
                                last.then_inc(s_rdy[d], 1)
                        dve.wait_ge(o_mm[d], n + 1)
                        dst = ot[:, :, c0 * P:c0 * P + P]
                        first = d == 0 if c0 == 0 or chunk(n, 0) == chunk(n, 1) else n < (c0 if d else NC - c0)
                        if first:
                            nc.vector.tensor_copy(dst, b3(bank[d][2])).then_inc(o_read[d], 1)
                        else:
                            if c0 == 0:
                                dve.wait_ge(o_read[0], 1)
                            else:
                                dve.wait_ge(o_read[1 - d], (NC - c0 if d == 0 else c0) + 1)
                            nc.vector.tensor_tensor(dst, dst, b3(bank[d][2]), ALU.add).then_inc(o_read[d], 1)
                if n < NC - 1:
                    for m in range(LEVELS):
                        for d in range(2):
                            dve.wait_ge(tr_mm[d], 3 * (n + 1) + m + 1)
                            if m < LEVELS - 1:
                                nc.vector.tensor_tensor(flat(Tm[d]), flat(Tm[d]), bank[d][0][:, :], ALU.add
                                                        ).then_inc(t_rdy[d], 1)
                            R = Rm[(n + 1) % 2][d]
                            dve.wait_ge(rr_rdy[d], 4 * (n + 1) + m + 1)
                            nc.vector.tensor_tensor(flat(R), flat(R), bank[d][2][:, :], ALU.add).then_inc(rr_rdy[d], 1)
                if n == 0:
                    substitute(2)

            for h in range(HEADS):
                dve.wait_ge(ort_rdy, h + 1)
                dve.wait_ge(osq_rdy, h + 1)
                nc.vector.reciprocal(orr[:, h, :], orr[:, h, :]).then_inc(orr_rdy, 1)
                dve.wait_ge(orr_rdy, h + 1)
                dve.wait_ge(z_rdy, h + 1)
                link(nc.vector.scalar_tensor_tensor(out=orr[:, h, :], in0=zs[:, h, :],
                                                    scalar=vec[:, R_DNN:R_DNN + 1], in1=orr[:, h, :],
                                                    op0=ALU.mult, op1=ALU.mult))
                nc.vector.tensor_tensor(ot[:, h, :], ot[:, h, :], orr[:, h, :], ALU.mult).then_inc(on_rdy, 1)
            dve.wait_ge(o_mm[0], NC)
            dve.wait_ge(o_mm[1], NC)
            for k in range(KD):
                dve.wait_ge(yh_rdy, k + 1)
                src = yc[:, k, :] if k < 4 else ot[:, k - 4, :]
                if k >= 4:
                    dve.wait_ge(on_rdy, k - 3)
                nc.vector.tensor_tensor(h_lo[:, k, :], src, h_hi[:, k, :].bitcast(F32), ALU.subtract
                                        ).then_inc(yl_rdy, 1)
            for j in range(KD):
                u = U_MO + j + 1
                if j > 0:
                    split_lo(u, u % 2, KD)
                if j > 0:
                    add_squares(2, j - 1, ssq_g, sq_g)
                residual(1, j, U_MO + j + 1, j % 2, KD + j)
            add_squares(2, KD - 1, ssq_g, sq_g)
            split_lo(U_F2I + 1, 1, KD)
            norm(2)
            swiglu_in(0, U_F2I, KF)
            with dve.Fori(1, KF - 1) as i:
                swiglu_in(i, U_F2I, KF)
            swiglu_in(KF - 1, U_F2I, KF, kt_next=KH)
            swiglu_out(U_F2O, 2, 2 * KD, None, 3)
            dve.wait_ge(y_rt, 1)
            nc.vector.reciprocal(rfin[:, :], rfin[:, :]).then_inc(y_r, 1)
            dve.wait_ge(y_r, 1)
            dve.wait_ge(y_ev, KD)
            for t in range(NC):
                nc.vector.tensor_scalar(yo[:, t, :], yo[:, t, :], rfin[:, t:t + 1], None, ALU.mult).then_inc(y_fin, 1)

        @block.gpsimd
        def _(pool):
            def norm(m):
                pool.wait_ge(r_rdy, m + 1)
                for k in range(1, KD, 2 if m == 0 else 1):
                    nc.gpsimd.tensor_tensor(tn[:, k, :], x[:, k, :], rinv[:, :], ALU.mult).then_inc(tnp_rdy, 1)

            norm(0)
            norm(1)
            G = gsm
            bc = lambda t, d, c0: t[:, d, c0, :].rearrange("p (h a) -> p h a", a=1).to_broadcast([P, HEADS, P])
            rep = lambda m: m.rearrange("p (a j) -> p a j", a=1).to_broadcast([P, HEADS, P])
            pool.wait_ge(gates, 1)
            pool.wait_ge(in_tri, 48)

            def decayed_q(n, d):
                c0 = chunk(n, d)
                pool.wait_ge(erow_rdy[d], n)
                if n > 1:
                    pool.wait_ge(st_qk[d], 16 * (2 * n - 1))
                nc.gpsimd.tensor_tensor(qgp[d][:, :, :], qkv[:, 0:4, c0 * P:c0 * P + P], Erow[d][:, :, :], ALU.mult
                                        ).then_inc(qg_rdy[d], 1)

            for g in range(GROUPS_DN + 1):
                n, d = divmod(g, 2)
                if g < GROUPS_DN:
                    if n > 0:
                        pool.wait_ge(lt_rdy[d], n)
                        pool.wait_ge(qk_rdy[d], n)
                    nc.gpsimd.tensor_tensor(gtri[d][:, :, :], rep(tri[:, d, :]), bc(G["g"], d, chunk(n, d)), ALU.mult
                                            ).then_inc(gtri_rdy[d], 1)
                if g > 2:
                    decayed_q(*divmod(g - 1, 2))

            pool.wait_ge(in_lev, 32)
            pool.wait_ge(mm_done, U_MO)
            blk4 = blk[:, :].rearrange("p (a b c) -> p a b c", a=1, b=BPC).to_broadcast([P, HEADS, BPC, BS])

            def expand(dst, n, d, kind):
                src = rt16[d][:, n % 2, kind, :].rearrange("p (h a c) -> p h a c", h=HEADS, a=1)
                return nc.gpsimd.tensor_tensor(dst[:, :, :].rearrange("p h (b c) -> p h b c", c=BS),
                                               src.to_broadcast([P, HEADS, BPC, BS]), blk4, ALU.mult)

            def mask(n, d, m):
                i = 3 * n + m
                if m == 0:
                    pool.wait_ge(in_lt[d], 16 * (n + 1))
                if i > 1:
                    pool.wait_ge(x_mm[d], i - 1)
                nc.gpsimd.tensor_tensor((NTa, NTb)[i % 2][d][:, :, :], LT[d][:, :, :],
                                        rep(lev[:, LEVELS * d + m, :]), ALU.mult).then_inc(nt_rdy[d], 1)

            for n in range(NC):
                for d in range(2):
                    pool.wait_ge(in_rt[n % 2][d], 32 * (n // 2 + 1))
                    if n > 0:
                        pool.wait_ge(x_mm[d], 3 * n)
                    expand(Tm[d], n, d, 1).then_inc(t_rdy[d], 1)
                    mask(n, d, 0)
                for d in range(2):
                    if n > 0:
                        pool.wait_ge(rr_rdy[d], 4 * n)
                    if n > 1:
                        pool.wait_ge(v_mm[d], n - 1)
                    expand(Rm[n % 2][d], n, d, 0).then_inc(rr_rdy[d], 1)
                    mask(n, d, 1)
                if n == 0:
                    pool.wait_ge(tok_evA, NC)
                for d in range(2):
                    mask(n, d, 2)
                for d in range(2):
                    kt = ktok[:, chunk(n, d), :].rearrange("p (h j) -> p h j", h=HEADS)
                    if n > 0:
                        if n > 1:
                            pool.wait_ge(w_mm[d], n - 1)
                        nc.gpsimd.tensor_tensor(ke[d][:, :, :], kt, bc(G["eg"], d, chunk(n, d)), ALU.mult
                                                ).then_inc(ke_rdy[d], 1)
                    if n < NC - 1:
                        if n > 0:
                            pool.wait_ge(s_mm[d], n)
                        nc.gpsimd.tensor_tensor(kg[d][:, :, :], kt, bc(G["kgs"], d, chunk(n, d)), ALU.mult
                                                ).then_inc(kg_rdy[d], 1)
            norm(2)


_INS = ["x_prompt", "x_sample", "state_dn_fwd", "state_dn_bwd", "c", "c_ctx", "w_ada", "b_ada", "norm_ffn1",
        "w_ffn1_in", "w_ffn1_out", "norm_mix", "w_mix_in", "conv_w", "dn_conv_w", "dn_a_log", "dn_dt_bias", "dn_norm",
        "w_mix_out", "norm_ffn2", "w_ffn2_in", "w_ffn2_out", "norm_final"]
_OUTS = [(1, TP, D), (1, TS, D), (1, 1, HEADS, P, P), (1, 1, HEADS, P, P)]


def kernel(**inputs):
    import concourse.bacc as bacc
    from concourse.bass_utils import run_bass_kernel_spmd

    nc = bacc.Bacc("TRN2", target_bir_lowering=False, num_devices=1)
    arrays, args = {}, []
    for name in _INS:
        a = np.ascontiguousarray(inputs[name])
        arrays[f"in_{name}"] = a
        args.append(nc.dram_tensor(f"in_{name}", a.shape, mybir.dt.from_np(a.dtype), kind="ExternalInput").ap())
    arrays["in_consts"] = constants()
    args.append(nc.dram_tensor("in_consts", (P, NCONST), F32, kind="ExternalInput").ap())
    for i, shape in enumerate(_OUTS):
        args.append(nc.dram_tensor(f"out_{i}", shape, F32, kind="ExternalOutput").ap())
    hybrid_layer(nc, *args)
    r = run_bass_kernel_spmd(nc, [arrays], core_ids=[0])
    return tuple(r.results[0][f"out_{i}"] for i in range(len(_OUTS)))
```

```python
from contextlib import ExitStack

import numpy as np

import concourse.bass as bass
from concourse import mybir

F32 = mybir.dt.float32
F32R = mybir.dt.float32r
BF16 = mybir.dt.bfloat16
ALU = mybir.AluOpType
ACT = mybir.ActivationFunctionType

P = 128
D = 1024
KD = D // P
TP, TS = 128, 512
T = TP + TS
TH = T // 2
NC = T // P
FF = 2816
KF = FF // P
KH = KF // 2
HEADS = 4
CW = D // 2
QKV0 = 3 * CW
Z0 = QKV0 + 3 * CW
AB0 = Z0 + CW
NAB = 4 * HEADS
BS = 16
LEV0 = 4
LEVELS = 3
BPC = P // BS
GROUPS_DN = 2 * NC
HPL = BPC * (BS * P + BS)
PREP0 = 15
GRID_W = 64
EPS = 1e-6
NEG = -1e30

U_F1I = 0
U_F1O = U_F1I + 2 * KF
U_MI = U_F1O + 2 * KD
U_MO = U_MI + 28
U_F2I = U_MO + KD
U_F2O = U_F2I + 2 * KF
U_END = U_F2O + 2 * KD
A_F1I = 0
A_F1O = A_F1I + 2 * KF
A_MI = A_F1O + KD
A_MO = A_MI + 28
A_F2I = A_MO + KD
A_F2O = A_F2I + 2 * KF

R_CTX, R_C, R_N1, R_NM, R_N2, R_NF, R_CONV, R_DNC, R_DNN = 0, 8, 16, 24, 32, 40, 48, 60, 96
NROWS = 97
C_ID, C_TRI, C_LEV, C_BLK = 0, P, 3 * P, 3 * P + 2 * LEVELS * P
C_NEG = C_BLK + P
C_SUB = C_NEG + 2 * P
NCONST = C_SUB + BS * BS


def constants():
    j, i = np.meshgrid(np.arange(P), np.arange(P), indexing="ij")
    out = np.zeros((P, NCONST), np.float32)
    out[:, C_ID:C_ID + P] = i == j
    for d in range(2):
        a, b = (j, i) if d == 0 else (i, j)
        out[:, C_TRI + d * P:C_TRI + (d + 1) * P] = a <= b
        for m in range(LEVELS):
            s = LEV0 + m
            joined = (a >> s) + 1 == (b >> s)
            c = C_LEV + (d * LEVELS + m) * P
            out[:, c:c + P] = -1.0 * (joined & ((b >> s) % 2 == 1))
        out[:, C_NEG + d * P:C_NEG + (d + 1) * P] = np.where(a <= b, 0.0, NEG)
    out[:, C_BLK:C_BLK + P] = j // BS == i // BS
    out[:, C_SUB:] = (np.eye(BS) - np.triu(np.ones((BS, BS)), 1)).reshape(1, -1)
    return out


def hybrid_layer(nc, x_prompt, x_sample, state_f, state_b, c, c_ctx, w_ada, b_ada, norm1, w1i, w1o, norm_mix,
                 w_mi, conv_w, dn_conv_w, a_log, dt_bias, dn_norm, w_mo, norm2, w2i, w2o, norm_f, consts,
                 y_prompt, y_sample, s_out_f, s_out_b):
    ctx = ExitStack()
    with ctx:
        sem = lambda name: ctx.enter_context(nc.semaphore(name))
        place = {"at": 16512}

        def sb(name, shape, dt, at=None):
            size = int(np.prod(shape[1:])) * (2 if dt == BF16 else 4)
            if at is None:
                at = place["at"]
                place["at"] += (size + 31) // 32 * 32
            return nc.alloc_sbuf_tensor_at(name, shape, dt, offset=at)

        x = sb("x", [P, KD, T], F32)
        at_h = place["at"]
        h_hi = sb("h_hi", [P, KD, T], F32R)
        h_lo = sb("h_lo", [P, KD, T], F32R)
        at_g = place["at"]
        g_hi = sb("g_hi", [P, KF, T], F32R)
        g_lo = sb("g_lo", [P, KF, T], F32R)
        w_raw = sb("w_raw", [P, 2, KH * P], F32)
        w_hi = sb("w_hi", [P, 2, KH * P], F32R)
        w_lo = sb("w_lo", [P, 2, KH * P], F32R)
        at_sa = place["at"]
        sa = sb("sa", [P, T], F32)
        mod = sb("mod", [P, 9 * KD, 2], F32)
        gain = sb("gain", [P, 3, KD, 2], F32)
        gate = sb("gate", [P, 3, KD, 2], F32)
        vec = sb("vec", [P, NROWS], F32)
        bada = sb("bada", [P, 9 * KD], F32)
        ident = sb("ident", [P, P], F32)
        ones = sb("ones", [P, 1], F32)
        eps = sb("eps", [P, 1], F32)
        eps_o = sb("eps_o", [P, 1], F32)
        rms = sb("rms", [P, NC], F32)
        assert place["at"] <= 229344, place["at"]
        ones_t = ones[:, 0:1].to_broadcast([P, P])

        KB = 1024
        xin = sb("xin", [P, NC, D], F32, at=at_g)
        vrow = sb("vrow", [NROWS, P], F32, at=at_g + 20 * KB)
        brow = sb("brow", [9 * KD, P], F32, at=at_g + 20 * KB + 512)
        at_ada = at_g + (KF + 8) * 4 * T
        ADA = 4
        ada_w = sb("ada_w", [P, ADA, 2048], F32, at=at_ada)
        ada_r = sb("ada_r", [P, 512], F32, at=at_ada + ADA * 8 * KB)
        ccol = sb("ccol", [P, KD, 32], F32, at=at_ada + ADA * 8 * KB + 2048)
        assert at_ada + ADA * 8 * KB + 2048 + 1024 <= at_g + 2 * KF * 4 * T
        rinv = sb("rinv", [P, T], F32, at=at_g + 20 * KB)
        tn = sb("tn", [P, KD, T], F32, at=at_g)
        hf = sb("hf", [P, KD, T], F32, at=at_g + 24 * KB)
        B = 4 * T
        qkv = sb("qkv", [P, 12, T], F32, at=at_g)
        zs = sb("zs", [P, 4, T], F32, at=at_g + 12 * B)
        yc = sb("yc", [P, 4, T], F32, at=at_g + 16 * B)
        ot = sb("ot", [P, HEADS, T], F32, at=at_g + 20 * B)
        wab = sb("wab", [P, KD, NAB], F32, at=at_g + 20 * B)
        wab_2 = sb("wab_2", [P, KD, 2, NAB], F32R, at=at_g + 20 * B + 512)
        abt = sb("abt", [2 * NAB, T], F32, at=at_g + 20 * B + 1536)
        negf = sb("negf", [P, 2, P], F32, at=at_g + 22 * B)
        ktok = sb("ktok", [P, NC, CW], F32, at=at_g + 24 * B)
        vtok = sb("vtok", [P, NC, CW], F32, at=at_g + 28 * B)
        ss = sb("ss", [P, 4, T], F32, at=at_g + 36 * B)
        cc = sb("cc", [P, T], F32, at=at_g + 40 * B)
        uu = sb("uu", [P, T], F32, at=at_g + 41 * B)
        cv = sb("cv", [P, T], F32, at=at_g + 42 * B)
        tri = sb("tri", [P, 2, P], F32, at=at_g + 43 * B)
        negb = sb("negb", [P, 2, P], BF16, at=at_g + 43 * B + 1024)
        identb = sb("identb", [P, P], BF16, at=at_g + 43 * B + 1536)
        lev = sb("lev", [P, 2 * LEVELS, P], F32, at=at_g + 40 * B)
        blk = sb("blk", [P, P], F32, at=at_g + 40 * B + 3072)
        rt16 = [sb(f"rt16_{d}", [P, 2, 2, HEADS * BS], F32, at=at_g + 40 * B + 3584 + 1024 * d) for d in range(2)]
        gsm = {}
        off = at_sa
        for name in ("g", "beta", "gc", "ngc", "gt", "gl", "kgs", "t1", "t2", "t3"):
            gsm[name] = sb("s_" + name, [P, 2, NC, HEADS], F32, at=off)
            off += 160
        off = at_g + 22 * B + 1024
        for name, width in (("ab", NC * NAB), ("adt", 16)):
            gsm[name] = sb(name, [P, width], F32, at=off)
            off += 4 * width
        spots = [at_g + 24 * B + 2048 * i for i in range(10)]
        per = lambda name: [sb(f"{name}{d}", [P, HEADS, P], F32, at=spots.pop(0)) for d in range(2)]
        DT = per("DT")
        gtri = DT
        Erow, LTp, QKp, qgp = per("Erow"), per("LTp"), per("QKp"), per("qgp")
        spots = [at_g + 20 * B + 2048 * i for i in range(2)]
        kep = per("kep")
        sub = {name: sb("sub_" + name, [P, BS, BS], F32, at=at_g + 32 * B + 1024 * i)
               for i, name in enumerate(("u", "n", "x", "xt", "tmp", "mask"))}
        spots = [at_h + 2048 * i for i in range(20)] + [at_g + 36 * B + 2048 * i for i in range(5)] + \
                [at_g + 32 * B + 6144 + 2048 * i for i in range(2)] + [at_g + 8 * B + 2048 * i for i in range(5)]
        NTa, NTb, Tm, QK, qg, Xm, LT, ke = (per(n) for n in ("NTa", "NTb", "Tm", "QK", "qg", "Xm", "LT", "ke"))
        Rm = [per("Rm0_"), per("Rm1_")]
        kg, VN, VD, Sa, Sb, Sc = (per(n) for n in ("kg", "VN", "VD", "Sa", "Sb", "Sc"))
        keep = lambda name, n: nc.dram_tensor(name, [NC, 2, n], F32).ap()
        d_lt = keep("d_lt", HEADS * HPL)
        d_qk, d_qg, d_ke = keep("d_qk", P * CW), keep("d_qg", P * CW), keep("d_ke", P * CW)
        d_rt = nc.dram_tensor("d_rt", [NC, 2, 2, P * HEADS * BS], F32).ap()

        def view(t, dims):
            return bass.AP(tensor=t.tensor, offset=t.offset, ap=dims)

        osq = [sb(f"osq{i}", [P, HEADS, P], F32, at=at_g + 32 * B + 2048 * i) for i in range(3)]
        rc = sb("rc", [P, NC * HEADS], F32, at=at_g + 40 * B + 5632)

        ssq_h = sb("ssq_h", [P, T], F32, at=at_h)
        ssq_g = sb("ssq_g", [P, T], F32, at=at_g + 38 * B)
        sq_h = sb("sq_h", [P, T], F32, at=at_h + B)
        sq_g = sb("sq_g", [P, T], F32, at=at_g + 39 * B)
        xg = sb("xg", [P, 2, T], F32, at=at_h + 2 * B)
        rfin = sb("rfin", [P, NC], F32, at=at_h + 5 * B)
        yo = sb("yo", [P, NC, D], F32, at=at_h + 8 * B)

        ps = [ctx.enter_context(nc.psum_tensor(f"ps{i}", [P, 512], F32)) for i in range(8)]
        acc = [[ps[2 * s][:, 0:TH], ps[2 * s + 1][:, 0:TH]] for s in (0, 1, 3)]
        sums = [ps[4][:, 0:TH], ps[5][:, 0:TH]]
        adap, adat = ps[6], ps[7]

        in_x, in_vec, in_wab, in_adt, in_tri, in_lev = (sem(n) for n in (
            "in_x", "in_vec", "in_wab", "in_adt", "in_tri", "in_lev"))
        pk_in, solved = sem("pk_in"), sem("solved")
        in_s = [sem(f"in_s{d}") for d in range(2)]
        w_in = [sem(f"w_in{s}") for s in range(2)]
        hi_ready, lo_ready, mm_done = sem("hi_ready"), sem("lo_ready"), sem("mm_done")
        acc_free = [sem(f"acc_free{s}") for s in range(2)]
        ada_in = [sem(f"ada_in{s}") for s in range(ADA)]
        ada_mm, ada_row, ada_tr, mod_rdy = sem("ada_mm"), sem("ada_row"), sem("ada_tr"), sem("mod_rdy")
        misc_set, vec_tr, vec_rdy, c_rdy = sem("misc_set"), sem("vec_tr"), sem("vec_rdy"), sem("c_rdy")
        x_tr, x_evA, x_evB = sem("x_tr"), sem("x_evA"), sem("x_evB")
        sq_rdy, ssq_rdy, sum_mm, rt_rdy, r_rdy = (sem(n) for n in ("sq_rdy", "ssq_rdy", "sum_mm", "rt_rdy", "r_rdy"))
        tn_rdy, tnp_rdy, hh_rdy, hf_rdy, h_rdy = (sem(n) for n in ("tn_rdy", "tnp_rdy", "hh_rdy", "hf_rdy", "h_rdy"))
        sa_rdy, gp_rdy, gh_rdy, g_rdy = sem("sa_rdy"), sem("gp_rdy"), sem("gh_rdy"), sem("g_rdy")
        x_upd = sem("x_upd")
        dve_step = sem("dve_step")
        gain_rdy = sem("gain_rdy")

        def seq(engine):
            count = [0]

            def link(instruction):
                count[0] += 1
                instruction.then_inc(dve_step, 1)
                engine.wait_ge(dve_step, count[0])
            return link

        cv_rdy, qs_rdy, q2_rdy, ssm, ss_rdy, st_rdy, qn_rdy = (sem(n) for n in (
            "cv_rdy", "qs_rdy", "q2_rdy", "ssm", "ss_rdy", "st_rdy", "qn_rdy"))
        cc_rdy, u_rdy, uc_rdy, y_rdy, z_rdy = (sem(n) for n in ("cc_rdy", "u_rdy", "uc_rdy", "y_rdy", "z_rdy"))
        wab_h, wab_rdy, ab_mm, ab_ev, ab_tr, ab_rdy = (sem(n) for n in (
            "wab_h", "wab_rdy", "ab_mm", "ab_ev", "ab_tr", "ab_rdy"))
        tok_tr, tok_evA, tok_evB = sem("tok_tr"), sem("tok_evA"), sem("tok_evB")
        act_g, dve_g, gsum, gates = sem("act_g"), sem("dve_g"), sem("gsum"), sem("gates")
        pair = lambda n: [sem(f"{n}{d}") for d in range(2)]
        gtri_rdy, row_rdy, erow_rdy, rowm, kk_rdy, dt_rdy, lt_rdy, qk_rdy = (pair(n) for n in (
            "gtri_rdy", "row_rdy", "erow_rdy", "rowm", "kk_rdy", "dt_rdy", "lt_rdy", "qk_rdy"))
        nt_rdy, x_mm, xm_rdy, tr_mm, t_rdy, rr_rdy = (pair(n) for n in (
            "nt_rdy", "x_mm", "xm_rdy", "tr_mm", "t_rdy", "rr_rdy"))
        in_rt = [pair("in_rt_even"), pair("in_rt_odd")]
        st_lt, st_qk, st_rt, in_lt, in_qk = (pair(n) for n in (
            "st_lt", "st_qk", "st_rt", "in_lt", "in_qk"))
        kg_rdy, qg_rdy, w_mm, wt_rdy, v_mm, vn_rdy, o_mm, o_read, s_mm, s_rdy = (pair(n) for n in (
            "kg_rdy", "qg_rdy", "w_mm", "wt_rdy", "v_mm", "vn_rdy", "o_mm", "o_read", "s_mm", "s_rdy"))
        osq_rdy, oq_rdy, osum, ort_rdy, orr_rdy, oz_rdy, ob_mm, on_rdy, yh_rdy, yl_rdy = (sem(n) for n in (
            "osq_rdy", "oq_rdy", "osum", "ort_rdy", "orr_rdy", "oz_rdy", "ob_mm", "on_rdy", "yh_rdy", "yl_rdy"))
        xg_rdy, y_tr, y_ev, y_sum, y_rt, y_fin, out_done, st_done = (sem(n) for n in (
            "xg_rdy", "y_tr", "y_ev", "y_sum", "y_rt", "y_fin", "out_done", "st_done"))

        GROUPS = ((0, 0, TP), (1, TP, T))
        PIECES = ((0, 0, TP, 0, 0), (0, TP, TH, 1, TP), (1, 0, TH, 1, TH))

        def strip_col(n):
            if n < 16:
                return QKV0 + P * qkv_tile(n)
            return (CW, 2 * CW, 0)[(n - 16) % 3] + P * ((n - 16) // 3)

        def qkv_tile(n):
            return n + 4 if n < 4 else n - 4 if n < 8 else n

        def chunk(n, d):
            return n if n == 0 or d == 0 else NC - n

        ODONE, EARLY = (0, 2, 3, 1, 4), 3

        def tn_wait(m, k):
            return (tn_rdy, m + 1) if k == 0 else (tnp_rdy, (KD - 1) * m + k)

        block = ctx.enter_context(nc.Block())

        @block.sync
        def _(sp):
            sp.dma_start(xin[:, 0, :], x_prompt[0]).then_inc(in_x, 16)
            for t in range(1, NC):
                sp.dma_start(xin[:, t, :], x_sample[0, (t - 1) * P:t * P, :]).then_inc(in_x, 16)

            def load_w(u, slot, src, kt, wait=True):
                if wait:
                    sp.wait_ge(lo_ready, u - 1)
                sp.dma_start(w_raw[:, slot, 0:kt * P].rearrange("p (k f) -> p k f", k=kt),
                             src).then_inc(w_in[slot], 16)

            ada_v = w_ada[0].rearrange("(k p) f -> p k f", p=P)

            def load_ada(n, s, k, col, width):
                if not (isinstance(n, int) and n < ADA):
                    sp.wait_ge(ada_mm, n - ADA + 1)
                sp.dma_start(ada_w[:, s, 0:width], ada_v[:, k, bass.ds(col, width)]).then_inc(ada_in[s], 16)

            w_in_v = [w[0].rearrange("(k p) f -> p k f", p=P) for w in (w1i, w2i)]
            w_out_v = [w[0].rearrange("(k p) f -> p k f", p=P) for w in (w1o, w2o)]
            sp.wait_ge(in_vec, 11 * 16)
            for k in range(KD):
                load_ada(k, k % ADA, k, 0, 2048)
            for u in range(2):
                load_w(u, u, w_in_v[0][:, :, u * FF:u * FF + P], KD, wait=False)

            with sp.Fori(0, 3) as s:
                for half in range(2):
                    for k in range(4):
                        load_ada(8 * s + (8 + 4 * half + k), k, 4 * half + k, 2048 * s + 2048, 2048)
                    i = 2 * s + half + 1
                    for b in range(2):
                        load_w(2 * i + b, b, w_in_v[0][:, :, bass.ds(P * i + b * FF, P)], KD)
            for half in range(2):
                for k in range(4):
                    load_ada(32 + 4 * half + k, k, 4 * half + k, 8192, 1024)
                i = 7 + half
                for b in range(2):
                    load_w(2 * i + b, b, w_in_v[0][:, :, P * i + b * FF:P * i + b * FF + P], KD)
            with sp.Fori(9, KF) as i:
                for b in range(2):
                    load_w(2 * i + b, b, w_in_v[0][:, :, bass.ds(P * i + b * FF, P)], KD)
            with sp.Fori(0, KD) as j:
                for b in range(2):
                    load_w(U_F1O + 2 * j + b, b, w_out_v[0][:, KH * b:KH * b + KH, bass.ds(P * j, P)], KH)

            w_mi_v = w_mi[0].rearrange("(k p) f -> p k f", p=P)

            def prep_store(g):
                n, d = divmod(g, 2)
                sp.wait_ge(lt_rdy[d], n + 1)
                sp.dma_start(view(d_lt[n, d], [[P, P], [HPL, HEADS], [1, P]]), LTp[d][:, :, :]).then_inc(st_lt[d], 16)
                sp.wait_ge(qk_rdy[d], n + 1)
                sp.dma_start(view(d_qk[n, d], [[CW, P], [1, CW]]), QKp[d][:, :, :]).then_inc(st_qk[d], 16)
                if n > 0:
                    sp.wait_ge(qg_rdy[d], n)
                    sp.dma_start(view(d_qg[n, d], [[CW, P], [1, CW]]), qgp[d][:, :, :]).then_inc(st_qk[d], 16)
                    sp.dma_start(view(d_ke[n, d], [[CW, P], [1, CW]]), kep[d][:, :, :]).then_inc(st_qk[d], 16)

            def batch(b):
                return [(n, d, 64 * d + 32 * (n % 2)) for n in range(2 * b, min(2 * b + 2, NC)) for d in range(2)]

            def pack(b):
                if b > 0:
                    sp.wait_ge(solved, b)
                for n, d, p0 in batch(b):
                    sp.wait_ge(st_lt[d], 16 * (n + 1))
                    sp.dma_start(sub["u"][p0:p0 + 32, :, :], view(d_lt[n, d], [[BS * P + BS, 32], [P, BS], [1, BS]])
                                 ).then_inc(pk_in, 16)

            def unpack(b):
                sp.wait_ge(solved, b + 1)
                for n, d, p0 in batch(b):
                    for kind in range(2):
                        src = sub["x" if kind == d else "xt"]
                        sp.dma_start(view(d_rt[n, d, kind], [[BS * BS, 32], [1, BS * BS]]), src[p0:p0 + 32, :, :]
                                     ).then_inc(st_rt[d], 16)

            for n in range(28):
                col = strip_col(n)
                load_w(U_MI + n, n % 2, w_mi_v[:, :, col:col + P], KD)
                if n == 1:
                    sp.wait_ge(mm_done, U_MI)
                    sp.dma_start(wab[:, :, :], w_mi_v[:, :, AB0:AB0 + NAB]).then_inc(in_wab, 16)
                    sp.dma_start(tri[:, :, :], consts[:, C_TRI:C_TRI + 2 * P].rearrange("p (a b) -> p a b", a=2)
                                 ).then_inc(in_tri, 16)
                    sp.dma_start(negf[:, :, :], consts[:, C_NEG:C_NEG + 2 * P].rearrange("p (a b) -> p a b", a=2)
                                 ).then_inc(in_tri, 16)
                    sp.dma_start(sub["mask"][:, :, :], consts[:, C_SUB:C_SUB + BS * BS].rearrange(
                        "p (a b) -> p a b", a=BS)).then_inc(in_tri, 16)
                    sp.dma_start(gsm["adt"][:, 0:8], a_log.rearrange("a b h -> a (b h)").to_broadcast([P, 8])
                                 ).then_inc(in_adt, 16)
                    sp.dma_start(gsm["adt"][:, 8:16], dt_bias.rearrange("a b h -> a (b h)").to_broadcast([P, 8])
                                 ).then_inc(in_adt, 16)
                g = n - PREP0 - 4
                if g >= 0:
                    prep_store(g)
                if g == 3:
                    pack(0)
                if g == 6:
                    unpack(0)
                if g == 7:
                    pack(1)
            prep_store(9)
            w_mo_v = w_mo[0].rearrange("(k p) f -> p k f", p=P)
            for j in range(2):
                load_w(U_MO + j, j % 2, w_mo_v[:, :, P * j:P * j + P], KD)
            unpack(1)
            pack(2)
            sp.wait_ge(y_rdy, 4)
            sp.dma_start(lev[:, :, :], consts[:, C_LEV:C_LEV + 2 * LEVELS * P].rearrange("p (a b) -> p a b", b=P)
                         ).then_inc(in_lev, 16)
            sp.dma_start(blk[:, :], consts[:, C_BLK:C_BLK + P]).then_inc(in_lev, 16)
            sp.wait_ge(mm_done, U_MO)

            def dn_load_t(n):
                for d in range(2):
                    if n > 1:
                        sp.wait_ge(t_rdy[d], 3 * (n - 2) + 1)
                        sp.wait_ge(rr_rdy[d], 4 * (n - 2) + 1)
                    sp.wait_ge(st_rt[d], 32 * (n + 1))
                    for kind in range(2):
                        sp.dma_start(rt16[d][:, n % 2, kind, :].rearrange("p (h c) -> p h c", h=HEADS),
                                     view(d_rt[n, d, kind], [[BS, P], [P * BS, HEADS], [1, BS]])
                                     ).then_inc(in_rt[n % 2][d], 16)
                    if n > 0:
                        sp.wait_ge(nt_rdy[d], 3 * n)
                    if n > 1:
                        sp.wait_ge(w_mm[d], n - 1)
                    sp.wait_ge(st_lt[d], 16 * (n + 1))
                    sp.dma_start(LT[d][:, :, :], view(d_lt[n, d], [[P, P], [HPL, HEADS], [1, P]])
                                 ).then_inc(in_lt[d], 16)
                    if n > 0:
                        sp.wait_ge(st_qk[d], 16 * (3 * n + 1))
                        sp.dma_start(ke[d][:, :, :], view(d_ke[n, d], [[CW, P], [1, CW]])).then_inc(in_lt[d], 16)

            def dn_load_o(n):
                for d in range(2):
                    if n > 0:
                        sp.wait_ge(o_mm[d], n)
                    sp.wait_ge(st_qk[d], 16 * (3 * n + 1))
                    sp.dma_start(QK[d][:, :, :], view(d_qk[n, d], [[CW, P], [1, CW]])).then_inc(in_qk[d], 16)
                    if n > 0:
                        sp.dma_start(qg[d][:, :, :], view(d_qg[n, d], [[CW, P], [1, CW]])).then_inc(in_qk[d], 16)

            dn_load_t(0)
            dn_load_o(0)
            sp.wait_ge(tok_tr, 10)
            for d, state in enumerate((state_f, state_b)):
                sp.dma_start(Sc[d][:, :, :], state[0, 0].rearrange("h k v -> k h v")).then_inc(in_s[d], 16)
            for n in range(1, NC):
                dn_load_t(n)
                if n == NC - 2:
                    unpack(2)
                dn_load_o(n)
            for j in range(2, KD):
                load_w(U_MO + j, j % 2, w_mo_v[:, :, P * j:P * j + P], KD)
            with sp.Fori(0, KF) as i:
                for b in range(2):
                    load_w(U_F2I + 2 * i + b, b, w_in_v[1][:, :, bass.ds(P * i + b * FF, P)], KD)
            with sp.Fori(0, KD) as j:
                for b in range(2):
                    load_w(U_F2O + 2 * j + b, b, w_out_v[1][:, KH * b:KH * b + KH, bass.ds(P * j, P)], KH)
            for t in range(NC):
                sp.wait_ge(*((y_fin, t // 2 + 1) if t % 2 == 0 else (y_ev, KD + t // 2 + 1)))
                dst = y_prompt[0] if t == 0 else y_sample[0, (t - 1) * P:t * P, :]
                sp.dma_start(dst, yo[:, t, :]).then_inc(out_done, 16)
            sp.wait_ge(out_done, 16 * NC)
            sp.wait_ge(st_done, 32)

        @block.tensor
        def _(pe):
            def unit(u, slot, kt, hi, lo, a_slot, start=True, stop=True, k0=0, h_wait=None, ready=True):
                pe.wait_ge(lo_ready, u + 1)
                for k in range(kt):
                    if h_wait is not None:
                        pe.wait_ge(*h_wait(k))
                    wh = w_hi[:, slot, k * P:k * P + P]
                    wl = w_lo[:, slot, k * P:k * P + P]
                    for n, (w, m) in enumerate(((wh, hi), (wh, lo), (wl, hi))):
                        for b in range(2):
                            last = pe.matmul(acc[a_slot][b], w, m[:, k0 + k, b * TH:b * TH + TH],
                                             start=start and k == 0 and n == 0,
                                             stop=stop and k == kt - 1 and n == 2)
                last.then_inc(mm_done, 1)

            def acc_wait(a_half, slot):
                if not (isinstance(a_half, int) and a_half == 0):
                    pe.wait_ge(acc_free[slot], a_half)

            def sum_squares(m, src):
                pe.wait_ge(ssq_rdy, KD * (m + 1))
                for t in range(NC):
                    last = pe.matmul(ps[5][:, 2 * P + t:2 * P + t + 1], src[:, t * P:t * P + P], ones[:, :],
                                     start=True, stop=True)
                last.then_inc(sum_mm, 1)

            def spread(m):
                pe.wait_ge(r_rdy, 2 * m + 1)
                for t in range(NC):
                    last = pe.matmul(ps[4 + t // 4][:, t % 4 * P:t % 4 * P + P], rms[:, t:t + 1].to_broadcast([P, P]),
                                     ident[:, :], start=True, stop=True)
                last.then_inc(sum_mm, 1)

            pe.wait_ge(in_vec, 11 * 16)
            pe.transpose(ps[0][:, 0:NROWS], vrow[:, :], ident[0:NROWS, 0:NROWS])
            pe.transpose(ps[0][:, P:P + 9 * KD], brow[:, :], ident[0:9 * KD, 0:9 * KD]).then_inc(vec_tr, 1)
            pe.wait_ge(in_x, 16 * NC)
            for n in range(10):
                if n >= 2:
                    pe.wait_ge((x_evA, x_evB)[n % 2], n // 2)
                for m in range(4):
                    k, t = divmod(4 * n + m, NC)
                    last = pe.transpose(ps[2 + n % 2][:, m * P:m * P + P], xin[:, t, k * P:k * P + P], ident[:, :])
                last.then_inc(x_tr, 1)

            def ada_step(n, s, k, width):
                pe.wait_ge(ada_in[s], 16 * (n // ADA + 1) if isinstance(n, int) else n)
                for g in range(4):
                    last = pe.matmul(adap[32 * g:32 * g + 32, 0:width], ccol[:, k, :],
                                     ada_w[:, s, g * width:(g + 1) * width], start=k == 0, stop=k == KD - 1)
                last.then_inc(ada_mm, 1)

            def ada_turn(n, blocks):
                pe.wait_ge(ada_row, n + 1)
                if not (isinstance(n, int) and n == 0):
                    pe.wait_ge(mod_rdy, n)
                for b in range(blocks):
                    last = pe.transpose(adat[:, b * P:b * P + P], ada_r[:, b * P:b * P + P], ident[:, :])
                last.then_inc(ada_tr, 1)

            pe.wait_ge(c_rdy, 1)
            for k in range(KD):
                ada_step(k, k % ADA, k, 512)
                if k == 4:
                    sum_squares(0, ssq_h)
                if k == 6:
                    spread(0)
            ada_turn(0, 4)

            def first_pair(u0, a0, h0):
                for b in range(2):
                    acc_wait(a0 // 2, b)
                    pe.wait_ge(lo_ready, u0 + b + 1)
                for k in range(KD):
                    pe.wait_ge(h_rdy, h0 + k + 1)
                    for s in range(2):
                        wh, wl = (w[:, s, k * P:k * P + P] for w in (w_hi, w_lo))
                        for n, (w, m) in enumerate(((wh, h_hi), (wh, h_lo), (wl, h_hi))):
                            for b in range(2):
                                last = pe.matmul(acc[s][b], w, m[:, k, b * TH:b * TH + TH],
                                                 start=k == 0 and n == 0, stop=k == KD - 1 and n == 2)
                        if k == KD - 1:
                            last.then_inc(mm_done, 1)

            def swiglu_in(i, u0, a0, kt_next=None, extra=(), h_wait=None):
                if h_wait is not None:
                    first_pair(u0, a0, h_wait)
                    for step in extra:
                        step()
                    return
                for b in range(2):
                    acc_wait(a0 // 2 + i, b)
                    unit(u0 + 2 * i + b, b, KD, h_hi, h_lo, b)
                    for step in extra[2 * b:2 * b + 2]:
                        step()

            def with_ada(i, s, half, n_of, width, first_wait=None):
                steps = []
                for k in range(4):
                    kk = 4 * half + k
                    steps.append(lambda kk=kk, k=k: ada_step(n_of(kk), k, kk, width))
                swiglu_in(i, U_F1I, A_F1I, extra=steps, h_wait=first_wait)

            def slab(s, first=False):
                for half in range(2):
                    with_ada(2 * s + half, s, half,
                             (lambda kk: 8 * (s + 1) + kk) if isinstance(s, int) else
                             (lambda kk: 16 * (2 * s + 3 + kk // 4)), 512 if not isinstance(s, int) or s < 3 else 256,
                             0 if first and half == 0 else None)
            slab(0, first=True)
            ada_turn(1, 4)
            with pe.Fori(1, 3) as s:
                slab(s)
                ada_turn(s + 1, 4)
            slab(3)
            ada_turn(4, 2)
            with pe.Fori(8, KF) as i:
                swiglu_in(i, U_F1I, A_F1I)

            def swiglu_out(u0, a0, g0, after=lambda j: None):
                for j in range(KD):
                    s = j % 2
                    acc_wait(a0 // 2 + j // 2, s)
                    for b in range(2):
                        unit(u0 + 2 * j + b, b, KH, g_hi, g_lo, s, start=b == 0, stop=b == 1, k0=KH * b,
                             h_wait=(lambda k, b=b: (g_rdy, g0 + KH * b + k + 1)) if j == 0 else None)
                    after(j)

            swiglu_out(U_F1O, A_F1O, 0)
            sum_squares(1, ssq_h)
            spread(1)

            hs = lambda t, h: t[:, h * P:h * P + P]

            def row(n, d):
                pe.wait_ge(gtri_rdy[d], n + 1)
                if n > 0:
                    pe.wait_ge(dt_rdy[d], n)
                pe.matmul(ps[4 + d][:, :], ones_t, gtri[d][:, :, :], start=True, stop=True).then_inc(row_rdy[d], 1)

            def mask_row(n, d):
                if n > 0:
                    pe.wait_ge(erow_rdy[d], n)
                pe.matmul(ps[4 + d][:, :], identb[:, :], negb[:, d:d + 1, :].to_broadcast([P, HEADS, P]),
                          start=False, stop=True, skip_group_check=True).then_inc(rowm[d], 1)

            def products(n, d):
                t = chunk(n, d) * P
                if n == 0 and d == 0:
                    pe.wait_ge(qn_rdy, 4)
                else:
                    pe.wait_ge(lt_rdy[1 - d], n + d)
                    pe.wait_ge(qk_rdy[1 - d], n + d)
                for h in range(HEADS):
                    kt = qkv[:, 4 + h, t:t + P]
                    pe.matmul(hs(ps[6], h), kt, kt, start=True, stop=True)
                    last = pe.matmul(hs(ps[7], h), kt, qkv[:, h, t:t + P], start=True, stop=True)
                last.then_inc(kk_rdy[d], 1)

            first_pair(U_MI, A_MI, KD)
            for n in range(1, 28):
                if n == 2:
                    unit(U_MI + n, 0, KD, h_hi, h_lo, 2)
                elif n > 1:
                    acc_wait(A_MI // 2 + n // 2, n % 2)
                    unit(U_MI + n, n % 2, KD, h_hi, h_lo, n % 2)
                if 2 <= n <= 5:
                    pe.wait_ge(q2_rdy, n - 1)
                    if n > 2:
                        pe.wait_ge(ss_rdy, n - 2)
                    for b in range(2):
                        last = pe.matmul(sums[b], ones_t, (sa, uu)[n % 2][:, b * TH:b * TH + TH], start=True, stop=True)
                    last.then_inc(ssm, 1)
                if n == 11:
                    pe.wait_ge(wab_rdy, 1)
                    pe.wait_ge(ss_rdy, 4)
                    for k in range(KD):
                        for i, m in enumerate((h_hi, h_lo)):
                            for b in range(2):
                                last = pe.matmul(sums[b][0:2 * NAB, :], wab_2[:, k, :, :], m[:, k, b * TH:b * TH + TH],
                                                 start=k == 0 and i == 0, stop=k == KD - 1 and i == 1)
                    last.then_inc(ab_mm, 1)
                if n == 12:
                    pe.wait_ge(ab_ev, 1)
                    for t in range(NC):
                        for i in range(2):
                            last = pe.matmul(ps[6][:, t * NAB:(t + 1) * NAB], abt[:, t * P:t * P + P],
                                             ident[0:2 * NAB, i * NAB:(i + 1) * NAB], start=i == 0, stop=i == 1)
                    last.then_inc(ab_tr, 1)
                if n == 14:
                    pe.wait_ge(dve_g, 1)
                    pe.wait_ge(in_tri, 48)
                    for d in range(2):
                        gv = gsm["g"][:, d].rearrange("p c h -> p (c h)")
                        pe.matmul(ps[7][:, 32 * d:32 * d + 20], tri[:, d, :], gv, start=True, stop=True)
                        last = pe.matmul(ps[7][:, 64 + 32 * d:64 + 32 * d + 20], ones_t, gv, start=True, stop=True)
                    last.then_inc(gsum, 1)
                g = n - PREP0 - 1
                if 0 <= g < GROUPS_DN:
                    mask_row(*divmod(g, 2))
                    products(*divmod(g, 2))
                if 0 <= g + 1 < GROUPS_DN:
                    row(*divmod(g + 1, 2))
            for n in range(10):
                t, isv = divmod(n, 2)
                if n == 0:
                    pe.wait_ge(qs_rdy, 12)
                if n < 2:
                    acc_wait(A_MO // 2, 0)
                else:
                    pe.wait_ge((tok_evA, tok_evB)[n % 2], n // 2)
                for h in range(HEADS):
                    last = pe.transpose(ps[n % 2][:, h * P:h * P + P],
                                        qkv[:, (8 if isv else 4) + h, t * P:t * P + P], ident[:, :])
                last.then_inc(tok_tr, 1)
            acc_wait(A_MO // 2, 1)
            pe.wait_ge(tok_evA, 5)
            pe.wait_ge(tok_evB, 5)
            bank = [[ps[4 * d + i] for i in range(4)] for d in range(2)]

            def level_x(n, d, m):
                pe.wait_ge(nt_rdy[d], 3 * n + m + 1)
                pe.wait_ge(t_rdy[d], 3 * n + m + 1)
                if n > 0 or m > 0:
                    pe.wait_ge(xm_rdy[d], 3 * n + m)
                nt = (NTa, NTb)[(3 * n + m) % 2][d]
                for h in range(HEADS):
                    last = pe.matmul(hs(bank[d][3], h), nt[:, h, :], Tm[d][:, h, :], start=True, stop=True)
                last.then_inc(x_mm[d], 1)

            def level_tr(n, d, m):
                R = Rm[n % 2][d]
                pe.wait_ge(xm_rdy[d], 3 * n + m + 1)
                pe.wait_ge(rr_rdy[d], 4 * n + m + 1)
                if m == 0 and n > 0:
                    pe.wait_ge(o_read[d], n)
                for h in range(HEADS):
                    if m < LEVELS - 1:
                        pe.matmul(hs(bank[d][0], h), R[:, h, :], Xm[d][:, h, :], start=True, stop=True)
                    last = pe.matmul(hs(bank[d][2], h), Xm[d][:, h, :], R[:, h, :], start=True, stop=True)
                last.then_inc(tr_mm[d], 1)

            def w_product(n, d, s_in):
                pe.wait_ge(in_lt[d], 16 * (2 * n + 1))
                pe.wait_ge(s_rdy[d], n)
                if n == 1:
                    pe.wait_ge(in_s[d], 16)
                for h in range(HEADS):
                    last = pe.matmul(hs(bank[d][1], h), ke[d][:, h, :], s_in[:, h, :], start=True, stop=True)
                last.then_inc(w_mm[d], 1)

            def v_product(n, d):
                pe.wait_ge(rr_rdy[d], 4 * n + 4)
                if n > 0:
                    pe.wait_ge(wt_rdy[d], n)
                for h in range(HEADS):
                    rhs = VD[d][:, h, :] if n > 0 else hs(vtok[:, chunk(n, d), :], h)
                    last = pe.matmul(hs(bank[d][1], h), Rm[n % 2][d][:, h, :], rhs, start=True, stop=True)
                last.then_inc(v_mm[d], 1)

            def s_product(n, d):
                pe.wait_ge(vn_rdy[d], n + 1)
                pe.wait_ge(kg_rdy[d], n + 1)
                for h in range(HEADS):
                    last = pe.matmul(hs(bank[d][1], h), kg[d][:, h, :], VN[d][:, h, :], start=True, stop=True)
                last.then_inc(s_mm[d], 1)

            def o_product(n, d, s_in):
                pe.wait_ge(vn_rdy[d], n + 1)
                pe.wait_ge(rr_rdy[d], 4 * n + 4)
                pe.wait_ge(in_qk[d], 16 * (2 * n + 1))
                for h in range(HEADS):
                    last = pe.matmul(hs(bank[d][2], h), VN[d][:, h, :], QK[d][:, h, :], start=True, stop=n == 0)
                    if n > 0:
                        last = pe.matmul(hs(bank[d][2], h), s_in[:, h, :], qg[d][:, h, :], start=False, stop=True)
                last.then_inc(o_mm[d], 1)

            def o_squares(i):
                pe.wait_ge(oq_rdy, HEADS + i + 1)
                if i == 0:
                    pe.wait_ge(xm_rdy[1], 3 * NC)
                for h in range(HEADS):
                    last = pe.matmul(ps[7][:, HEADS * i + h:HEADS * i + h + 1], osq[i % 3][:, h, :], ones[:, :],
                                     start=True, stop=True)
                last.then_inc(osum, 1)

            def o_spread(i):
                pe.wait_ge(orr_rdy, 1 if i < EARLY else 2)
                if i == 0:
                    pe.wait_ge(t_rdy[1], 3 * NC)
                    pe.wait_ge(vn_rdy[1], NC)
                elif i == 2:
                    pe.wait_ge(o_read[1], NC)
                elif i > 2:
                    pe.wait_ge(on_rdy, i - 2)
                for h in range(HEADS):
                    last = pe.matmul(hs(ps[4 + i % 3], h), rc[:, HEADS * i + h:HEADS * i + h + 1].to_broadcast([P, P]),
                                     ident[:, :], start=True, stop=True)
                last.then_inc(ob_mm, 1)

            s_of = lambda n, d: {0: None, 1: Sc[d], 2: Sa[d], 3: Sc[d], 4: Sa[d]}[n]
            for n in range(-1, NC):
                if n >= 0:
                    for d in range(2):
                        v_product(n, d)
                if n == NC - 1:
                    for i in range(EARLY):
                        o_squares(i)
                if n < NC - 1:
                    for d in range(2):
                        level_x(n + 1, d, 0)
                if n >= 0:
                    for d in range(2):
                        if n < NC - 1:
                            s_product(n, d)
                        o_product(n, d, s_of(n, d))
                if n < NC - 1:
                    for m in range(LEVELS):
                        for d in range(2):
                            if m > 0:
                                level_x(n + 1, d, m)
                        for d in range(2):
                            level_tr(n + 1, d, m)
                        if m == 1 and n >= 0:
                            for d in range(2):
                                w_product(n + 1, d, s_of(n + 1, d))

            def pair_tile(k, wait=None):
                if wait is not None:
                    pe.wait_ge(yl_rdy, wait)
                for s in range(2):
                    wh, wl = (w[:, s, k * P:k * P + P] for w in (w_hi, w_lo))
                    for n, (w, m) in enumerate(((wh, h_hi), (wh, h_lo), (wl, h_hi))):
                        for b in range(2):
                            last = pe.matmul(acc[s][b], w, m[:, k, b * TH:b * TH + TH],
                                             start=k == 0 and n == 0, stop=k == KD - 1 and n == 2)
                    if k == KD - 1:
                        last.then_inc(mm_done, 1)

            pe.wait_ge(lo_ready, U_MO + 2)
            for i in range(EARLY):
                o_spread(i)
            pe.wait_ge(o_read[0], NC)
            pair_tile(0, 1)
            for i in range(EARLY, NC):
                o_squares(i)
            pair_tile(1, 2)
            pair_tile(2, 3)
            for i in range(EARLY, NC):
                o_spread(i)
            pair_tile(3, 4)
            for k in range(4, KD):
                pair_tile(k, 4 + NC if k == 4 else None)
            for j in range(2, KD):
                acc_wait(A_MO // 2 + j // 2, j % 2)
                unit(U_MO + j, j % 2, KD, h_hi, h_lo, j % 2)
            sum_squares(2, ssq_g)
            spread(2)

            swiglu_in(0, U_F2I, A_F2I, h_wait=2 * KD)
            with pe.Fori(1, KF) as i:
                swiglu_in(i, U_F2I, A_F2I)

            def turn_y(j):
                pe.wait_ge(xg_rdy, j + 1)
                if j > 0:
                    pe.wait_ge(y_ev, j)
                for t in range(NC):
                    last = pe.transpose(ps[6 + t // 4][:, t % 4 * P:t % 4 * P + P], xg[:, j % 2, t * P:t * P + P],
                                        ident[:, :])
                last.then_inc(y_tr, 1)

            swiglu_out(U_F2O, A_F2O, KF, after=lambda j: turn_y(j - 1) if j > 0 else None)
            turn_y(KD - 1)
            pe.wait_ge(ssq_rdy, 4 * KD)
            for t in range(NC):
                last = pe.matmul(ps[4][:, t:t + 1], ssq_h[:, t * P:t * P + P], ones[:, :], start=True, stop=True)
            last.then_inc(y_sum, 1)

        @block.scalar
        def _(act):
            def split_hi(u, slot, kt, u_half, first=False):
                act.wait_ge(w_in[slot], 16 * u_half + 16)
                if not first:
                    act.wait_ge(mm_done, u - 1)
                nc.scalar.activation(w_hi[:, slot, 0:kt * P], w_raw[:, slot, 0:kt * P], ACT.Copy
                                     ).then_inc(hi_ready, 1)

            act.dma_start(vrow[R_CTX:R_CTX + 8, :], c_ctx.rearrange("(k p) -> k p", p=P)).then_inc(in_vec, 16)
            act.dma_start(vrow[R_C:R_C + 8, :], c[0].rearrange("(k p) -> k p", p=P)).then_inc(in_vec, 16)
            for row, v in ((R_N1, norm1[0]), (R_NM, norm_mix[0]), (R_N2, norm2[0]), (R_NF, norm_f)):
                act.dma_start(vrow[row:row + 8, :], v.rearrange("(k p) -> k p", p=P)).then_inc(in_vec, 16)
            act.dma_start(vrow[R_CONV:R_CONV + 12, :],
                         conv_w[0].rearrange("w (k p) -> (w k) p", p=P)).then_inc(in_vec, 16)
            act.dma_start(vrow[R_DNC:R_DNC + 36, :],
                         dn_conv_w[0].rearrange("w (k p) -> (w k) p", p=P)).then_inc(in_vec, 16)
            act.dma_start(vrow[R_DNN:R_DNN + 1, :], dn_norm).then_inc(in_vec, 16)
            act.dma_start(brow[:, :], b_ada[0].rearrange("(k p) -> k p", p=P)).then_inc(in_vec, 16)
            act.dma_start(ident[:, :], consts[:, C_ID:C_ID + P]).then_inc(in_vec, 16)
            act.wait_ge(vec_tr, 1)
            nc.scalar.activation(vec[:, :], ps[0][:, 0:NROWS], ACT.Copy).then_inc(vec_rdy, 1)
            nc.scalar.activation(bada[:, :], ps[0][:, P:P + 9 * KD], ACT.Copy).then_inc(vec_rdy, 1)
            act.wait_ge(misc_set, 4)
            act.wait_ge(vec_rdy, 2)
            nc.scalar.activation(ccol[:, :, 0:2], vec[:, 0:16].rearrange("p (i k) -> p k i", i=2), ACT.Silu
                                 ).then_inc(c_rdy, 1)
            xf = x[:, :, :].rearrange("p k t -> p (k t)")
            for n in range(0, 10, 2):
                act.wait_ge(x_tr, n + 1)
                nc.scalar.activation(xf[:, n * 512:n * 512 + 512], ps[2][:, :], ACT.Copy).then_inc(x_evA, 1)

            def square(n, k, wait, odd=sq_h):
                act.wait_ge(*wait)
                if n > 1:
                    act.wait_ge(ssq_rdy, n - 1)
                nc.scalar.activation((sa, odd)[k % 2][:, :], x[:, k, :], ACT.Square).then_inc(sq_rdy, 1)

            def ada_out(n, width):
                act.wait_ge(ada_mm, 8 * n + 8)
                if not (isinstance(n, int) and n == 0):
                    act.wait_ge(ada_tr, n)
                nc.scalar.activation(ada_r[:, 0:width], adap[:, 0:width], ACT.Copy).then_inc(ada_row, 1)

            for k in range(KD):
                act.wait_ge(x_evA, 5)
                square(k, k, (x_evB, 5))

            def norm(m, kt_next=None, n_sum=0):
                act.wait_ge(sum_mm, 2 * m + 1)
                nc.scalar.activation(rms[:, :], ps[5][:, 2 * P:2 * P + NC], ACT.Sqrt, bias=eps[:, :], scale=1.0 / D
                                     ).then_inc(rt_rdy, 1)
                if m > 0:
                    u = (U_MI, U_F2I)[m - 1] + 1
                    split_hi(u, 1, KD, u // 2)
                act.wait_ge(sum_mm, 2 * m + 2)
                nc.scalar.activation(rinv[:, 0:4 * P], ps[4][:, :], ACT.Copy)
                nc.scalar.activation(rinv[:, 4 * P:T], ps[5][:, 0:P], ACT.Copy).then_inc(r_rdy, 1)
                if m == 0:
                    ada_out(0, 512)
                    for u in range(2):
                        split_hi(u, u, KD, 0, first=True)
                act.wait_ge(gain_rdy, 1 if m == 0 else 2)
                for k in range(KD):
                    act.wait_ge(*tn_wait(m, k))
                    for i, t0, t1 in GROUPS:
                        last = nc.scalar.activation(h_hi[:, k, t0:t1], tn[:, k, t0:t1], ACT.Identity,
                                                    bias=mod[:, 3 * m * KD + k, i:i + 1],
                                                    scale=gain[:, m, k, i:i + 1])
                    last.then_inc(hh_rdy, 1)

            norm(0)

            def gate_in(i, u0, i0):
                act.wait_ge(mm_done, u0 + 2 * i + 1)
                if not (isinstance(i, int) and i0 + i == 0):
                    act.wait_ge(g_rdy, i + i0)
                for b in range(2):
                    last = nc.scalar.activation(sa[:, b * TH:b * TH + TH], acc[0][b], ACT.Silu)
                last.then_inc(sa_rdy, 1)

            def swiglu_in(i, u0, i0, kt_next=KD, last=False):
                if not (isinstance(i, int) and i == 0):
                    split_hi(u0 + 2 * i + 1, 1, KD, u0 // 2 + i)
                else:
                    split_hi(u0 + 2, 0, kt_next, u0 // 2 + 1)
                gate_in(i, u0, i0)
                act.wait_ge(sa_rdy, i + i0 + 1)
                act_free(0)
                if not (isinstance(i, int) and i == 0):
                    split_hi(u0 + 2 * i + 2, 0, kt_next, u0 // 2 + i + 1)

            def act_free(slot):
                act.sem_inc(acc_free[slot], 1)

            def slab(s, width=512):
                for half in range(2):
                    swiglu_in(2 * s + half, U_F1I, 0)
                ada_out(s + 1, width)
            slab(0)
            with act.Fori(1, 3) as s:
                slab(s)
            slab(3, 256)
            with act.Fori(8, KF - 1) as i:
                swiglu_in(i, U_F1I, 0)
            swiglu_in(KF - 1, U_F1I, 0, kt_next=KH)

            def swiglu_out(u0, n0, kt_next, x0, after=lambda j: None):
                for j in range(KD):
                    split_hi(u0 + 2 * j + 1, 1, KH, u0 // 2 + j)
                    if j > 0:
                        square(n0 + j - 1, j - 1, (x_upd, x0 + j))
                        after(j - 1)
                    if j < KD - 1:
                        split_hi(u0 + 2 * j + 2, 0, KH, u0 // 2 + j + 1)
                    elif kt_next:
                        split_hi(u0 + 2 * j + 2, 0, kt_next, u0 // 2 + j + 1)
                square(n0 + KD - 1, KD - 1, (x_upd, x0 + KD))

            swiglu_out(U_F1O, KD, KD, 0)
            norm(1)

            flat = lambda t: t[:, :, :].rearrange("p h j -> p (h j)")
            for n in range(28):
                u = U_MI + n + 1
                if n == 8:
                    act.wait_ge(in_wab, 16)
                    nc.scalar.activation(wab_2[:, :, 0, :], wab[:, :, :], ACT.Copy).then_inc(wab_h, 1)
                if n == 1:
                    split_hi(u + 1, 1, KD, (u + 1) // 2)
                elif 2 < n < 27:
                    split_hi(u, (n + 1) % 2, KD, u // 2)
                if n == 12:
                    act.wait_ge(ab_mm, 1)
                    for b in range(2):
                        last = nc.scalar.activation(abt[:, b * TH:b * TH + TH], sums[b][0:2 * NAB, :], ACT.Copy)
                    last.then_inc(ab_ev, 1)
                if n == 13:
                    act.wait_ge(ab_rdy, 3)
                    nc.scalar.activation(gsm["t1"][:, :, :, :], gsm["t1"][:, :, :, :], ACT.Exp).then_inc(act_g, 1)
                    nc.scalar.activation(gsm["beta"][:, :, :, :], gsm["t3"][:, :, :, :], ACT.Exp).then_inc(act_g, 1)
                    act.wait_ge(in_adt, 32)
                    nc.scalar.activation(gsm["adt"][:, 0:8], gsm["adt"][:, 0:8], ACT.Exp).then_inc(act_g, 1)
                    act.wait_ge(act_g, 3)
                    nc.scalar.activation(gsm["t1"][:, :, :, :], gsm["t1"][:, :, :, :], ACT.Ln, bias=1.0
                                         ).then_inc(act_g, 1)
                if n == 15:
                    act.wait_ge(dve_g, 2)
                    nc.scalar.activation(gsm["gl"][:, :, :, :], gsm["gt"][:, :, :, :], ACT.Exp)
                    nc.scalar.activation(gsm["kgs"][:, :, :, :], gsm["t2"][:, :, :, :], ACT.Exp).then_inc(gates, 1)
                g = n - PREP0 - 1
                if 2 <= g < GROUPS_DN:
                    m, d = divmod(g, 2)
                    act.wait_ge(row_rdy[d], m + 1)
                    if m > 1:
                        act.wait_ge(qg_rdy[d], m - 1)
                    nc.scalar.activation(flat(Erow[d]), ps[4 + d][:, :], ACT.Exp).then_inc(erow_rdy[d], 1)
                g -= 1
                if 0 <= g < GROUPS_DN:
                    m, d = divmod(g, 2)
                    act.wait_ge(rowm[d], m + 1)
                    for h in range(HEADS):
                        last = nc.scalar.activation(DT[d][:, h, :], ps[4 + d][:, h * P:h * P + P], ACT.Exp,
                                                    bias=gsm["ngc"][:, d, chunk(m, d), h:h + 1])
                    last.then_inc(dt_rdy[d], 1)
                if 3 <= n <= 6:
                    act.wait_ge(ssm, n - 2)
                    for b in range(2):
                        last = nc.scalar.activation(ss[:, n - 3, b * TH:b * TH + TH], sums[b], ACT.Copy)
                    last.then_inc(ss_rdy, 1)
                if n < 12:
                    act.wait_ge(mm_done, U_MI + n + 1)
                    if n == 0:
                        split_hi(u + 1, 0, KD, (u + 1) // 2)
                    if n > 0:
                        act.wait_ge(qs_rdy, n)
                    tile = qkv_tile(n)
                    tap = vec[:, R_DNC + 12 + tile:R_DNC + 13 + tile]
                    for b in range(2):
                        last = nc.scalar.activation(cv[:, b * TH:b * TH + TH], acc[2 if n == 2 else n % 2][b],
                                                    ACT.Identity, scale=tap)
                    last.then_inc(cv_rdy, 1)
                    act.wait_ge(uc_rdy, n + 1)
                    nc.scalar.activation(qkv[:, tile, :], cv[:, :], ACT.Silu).then_inc(qs_rdy, 1)
                    if n < 4:
                        act.wait_ge(qs_rdy, n + 1)
                        if n > 1:
                            act.wait_ge(ssm, n - 1)
                        nc.scalar.activation((sa, uu)[n % 2][:, :], qkv[:, tile, :], ACT.Square).then_inc(q2_rdy, 1)
                elif n < 16:
                    act.wait_ge(mm_done, U_MI + n + 1)
                    for b in range(2):
                        last = nc.scalar.activation(zs[:, n - 12, b * TH:b * TH + TH], acc[n % 2][b], ACT.Silu)
                    last.then_inc(z_rdy, 1)
                    act.wait_ge(z_rdy, n - 11)
                    act_free(n % 2)
                elif n % 3 == 1:
                    act.wait_ge(mm_done, U_MI + n + 1)
                    if n > 16:
                        act.wait_ge(u_rdy, (n - 16) // 3)
                    for b in range(2):
                        last = nc.scalar.activation(cc[:, b * TH:b * TH + TH], acc[n % 2][b], ACT.Copy)
                    last.then_inc(cc_rdy, 1)
                    act.wait_ge(cc_rdy, (n - 16) // 3 + 1)
                    act_free(n % 2)
                if n == 11:
                    act.wait_ge(ss_rdy, 4)
                    for k in range(4):
                        nc.scalar.activation(ss[:, k, :], ss[:, k, :], ACT.Sqrt, bias=eps[:, :]).then_inc(st_rdy, 1)

            def tok(t):
                act.wait_ge(tok_tr, 2 * t + 1)
                if t == 0:
                    for d in range(2):
                        act.wait_ge(st_lt[d], 16 * NC)
                        act.wait_ge(st_qk[d], 16 * (3 * NC - 2))
                nc.scalar.activation(ktok[:, t, :], ps[0][:, :], ACT.Copy).then_inc(tok_evA, 1)
            for t in range(NC):
                tok(t)

            for j in range(2):
                split_hi(U_MO + j, j, KD, U_MO // 2)

            bank = [[ps[4 * d + i] for i in range(4)] for d in range(2)]
            for n in range(-1, NC):
                if n < NC - 1:
                    for m in range(LEVELS):
                        for d in range(2):
                            act.wait_ge(x_mm[d], 3 * (n + 1) + m + 1)
                            if 3 * (n + 1) + m > 0:
                                act.wait_ge(tr_mm[d], 3 * (n + 1) + m)
                            nc.scalar.activation(flat(Xm[d]), bank[d][3][:, :], ACT.Copy).then_inc(xm_rdy[d], 1)
                if n == 0:
                    for h in range(HEADS):
                        nc.scalar.activation(qkv[:, h, :], qkv[:, h, :], ACT.Square, scale=P * EPS ** 0.5
                                             ).then_inc(oq_rdy, 1)
                    for d, out in enumerate((s_out_f, s_out_b)):
                        act.wait_ge(s_rdy[d], 1)
                        act.dma_start(out[0, 0].rearrange("h k v -> k h v"), Sb[d][:, :, :]).then_inc(st_done, 16)

            def o_square(i):
                c0 = ODONE[i]
                if i >= 3:
                    act.wait_ge(osum, i - 2)
                nc.scalar.activation(osq[i % 3][:, :, :], ot[:, :, c0 * P:c0 * P + P], ACT.Square).then_inc(osq_rdy, 1)

            def o_root(i0, i1):
                act.wait_ge(osum, i1)
                nc.scalar.activation(rc[:, HEADS * i0:HEADS * i1], ps[7][:, HEADS * i0:HEADS * i1], ACT.Sqrt,
                                     bias=eps_o[:, :], scale=1.0 / P).then_inc(ort_rdy, 1)

            for d in range(2):
                act.wait_ge(o_read[d], NC - 1)
                act.wait_ge(st_rt[d], 32 * NC)
            for i in range(EARLY):
                o_square(i)
            act.wait_ge(y_rdy, 4)
            for k in range(4):
                nc.scalar.activation(h_hi[:, k, :], yc[:, k, :], ACT.Copy).then_inc(yh_rdy, 1)
            o_root(0, EARLY)
            act.wait_ge(o_read[0], NC)
            act.wait_ge(o_read[1], NC)
            for i in range(EARLY, NC):
                o_square(i)
            o_root(EARLY, NC)
            for i in range(NC):
                c0 = ODONE[i]
                act.wait_ge(on_rdy, i + 1)
                nc.scalar.activation(h_hi[:, 4:8, c0 * P:c0 * P + P], ot[:, :, c0 * P:c0 * P + P], ACT.Copy
                                     ).then_inc(yh_rdy, 1)
            act.wait_ge(st_done, 32)
            for j in range(KD):
                u = U_MO + j + 1
                if j > 0:
                    split_hi(u, u % 2, KD, u // 2)
                if j > 0:
                    square(2 * KD + j - 1, j - 1, (x_upd, KD + j), sq_g)
            square(3 * KD - 1, KD - 1, (x_upd, 2 * KD), sq_g)
            norm(2)
            swiglu_in(0, U_F2I, KF)
            with act.Fori(1, KF - 1) as i:
                swiglu_in(i, U_F2I, KF)
            swiglu_in(KF - 1, U_F2I, KF, kt_next=KH)

            def scale_x(j):
                if j > 1:
                    act.wait_ge(y_tr, j - 1)
                nc.scalar.activation(xg[:, j % 2, :], x[:, j, :], ACT.Identity, scale=vec[:, R_NF + j:R_NF + j + 1]
                                     ).then_inc(xg_rdy, 1)

            def copy_y(j):
                act.wait_ge(y_tr, j + 1)
                nc.scalar.activation(yo[:, 0:4, j * P:j * P + P], ps[6][:, :].rearrange("p (t f) -> p t f", t=4), ACT.Copy)
                nc.scalar.activation(yo[:, 4, j * P:j * P + P], ps[7][:, 0:P], ACT.Copy).then_inc(y_ev, 1)

            def after(j):
                scale_x(j)
                if j > 0:
                    copy_y(j - 1)
            swiglu_out(U_F2O, 3 * KD, None, 2 * KD, after)
            after(KD - 1)
            copy_y(KD - 1)
            act.wait_ge(y_sum, 1)
            nc.scalar.activation(rfin[:, :], ps[4][:, 0:NC], ACT.Sqrt, bias=eps[:, :], scale=1.0 / D).then_inc(y_rt, 1)
            act.wait_ge(y_rt, 2)
            act.wait_ge(y_ev, KD)
            for t in range(1, NC, 2):
                nc.scalar.activation(yo[:, t, :], yo[:, t, :], ACT.Copy, scale=rfin[:, t:t + 1]).then_inc(y_ev, 1)

        @block.vector
        def _(dve):
            link = seq(dve)

            def split_lo(u, slot, kt):
                dve.wait_ge(hi_ready, u + 1)
                nc.vector.tensor_tensor(w_lo[:, slot, 0:kt * P], w_raw[:, slot, 0:kt * P],
                                        w_hi[:, slot, 0:kt * P].bitcast(F32), ALU.subtract).then_inc(lo_ready, 1)

            nc.vector.memset(ones[:, :], 1.0).then_inc(misc_set, 1)
            nc.vector.memset(eps[:, :], EPS).then_inc(misc_set, 1)
            nc.vector.memset(eps_o[:, :], EPS * EPS * P).then_inc(misc_set, 1)
            nc.vector.memset(ccol[:, :, :], 0.0).then_inc(misc_set, 1)
            xf = x[:, :, :].rearrange("p k t -> p (k t)")
            for n in range(1, 10, 2):
                dve.wait_ge(x_tr, n + 1)
                nc.vector.tensor_copy(xf[:, n * 512:n * 512 + 512], ps[3][:, :]).then_inc(x_evB, 1)

            def ada_cols(n, blocks):
                dve.wait_ge(ada_tr, n + 1)
                if isinstance(n, int) and n == 0:
                    dve.wait_ge(vec_rdy, 2)
                for b in range(blocks):
                    src = adat[:, b * P:b * P + P].rearrange("p (g i) -> p g i", i=32)
                    for i in range(2):
                        lo = 16 * n + b
                        last = nc.vector.tensor_tensor(
                            mod[:, bass.ds(lo, 4, blocks), i], src[:, :, i], bada[:, bass.ds(lo, 4, blocks)], ALU.add)
                last.then_inc(mod_rdy, 1)

            def gains(m, first):
                for i in range(2):
                    last = nc.vector.scalar_tensor_tensor(
                        out=gain[:, m, :, i], in0=mod[:, (3 * m + 1) * KD:(3 * m + 2) * KD, i], scalar=1.0,
                        in1=vec[:, (R_N1, R_NM, R_N2)[m]:(R_N1, R_NM, R_N2)[m] + 8], op0=ALU.add, op1=ALU.mult)
                return last

            def add_squares(m, k, dst, odd=sq_h):
                dve.wait_ge(sq_rdy, KD * m + k + 1)
                src = (sa, odd)[k % 2]
                if k == 0:
                    nc.vector.tensor_copy(dst[:, :], src[:, :]).then_inc(ssq_rdy, 1)
                else:
                    dve.wait_ge(ssq_rdy, KD * m + k)
                    nc.vector.tensor_tensor(dst[:, :], dst[:, :], src[:, :], ALU.add).then_inc(ssq_rdy, 1)

            for k in range(KD):
                add_squares(0, k, ssq_h)

            def norm(m):
                dve.wait_ge(rt_rdy, m + 1)
                nc.vector.reciprocal(rms[:, :], rms[:, :]).then_inc(r_rdy, 1)
                if m > 0:
                    split_lo((U_MI, U_F2I)[m - 1] + 1, 1, KD)
                dve.wait_ge(r_rdy, 2 * m + 2)
                nc.vector.tensor_tensor(tn[:, 0, :], x[:, 0, :], rinv[:, :], ALU.mult).then_inc(tn_rdy, 1)
                if m == 0:
                    ada_cols(0, 4)
                    dve.wait_ge(mod_rdy, 1)
                    gains(0, True).then_inc(gain_rdy, 1)
                    dve.wait_ge(gain_rdy, 1)

                def full(k):
                    dve.wait_ge(*tn_wait(m, k))
                    for i, t0, t1 in GROUPS:
                        last = nc.vector.tensor_scalar(hf[:, k, t0:t1], tn[:, k, t0:t1], gain[:, m, k, i:i + 1],
                                                       mod[:, 3 * m * KD + k, i:i + 1], ALU.mult, ALU.add)
                    last.then_inc(hf_rdy, 1)

                def low(k):
                    dve.wait_ge(hf_rdy, KD * m + k + 1)
                    dve.wait_ge(hh_rdy, KD * m + k + 1)
                    nc.vector.tensor_tensor(h_lo[:, k, :], hf[:, k, :], h_hi[:, k, :].bitcast(F32), ALU.subtract
                                            ).then_inc(h_rdy, 1)
                full(0)
                if m == 0:
                    for u in range(2):
                        split_lo(u, u, KD)
                for k in range(1, KD):
                    low(k - 1)
                    full(k)
                low(KD - 1)

            norm(0)

            def gate_out(i, u0, i0):
                dve.wait_ge(mm_done, u0 + 2 * i + 2)
                dve.wait_ge(sa_rdy, i + i0 + 1)
                for b in range(2):
                    last = nc.vector.tensor_tensor(sa[:, b * TH:b * TH + TH], sa[:, b * TH:b * TH + TH], acc[1][b],
                                                   ALU.mult)
                last.then_inc(gp_rdy, 1)
                dve.wait_ge(gp_rdy, i + i0 + 1)
                dve.sem_inc(acc_free[1], 1)
                gh = g_hi[:, bass.ds(i, 1), :].rearrange("p a t -> p (a t)")
                gl = g_lo[:, bass.ds(i, 1), :].rearrange("p a t -> p (a t)")
                nc.vector.tensor_copy(gh, sa[:, :]).then_inc(gh_rdy, 1)
                dve.wait_ge(gh_rdy, i + i0 + 1)
                nc.vector.tensor_tensor(gl, sa[:, :], gh.bitcast(F32), ALU.subtract).then_inc(g_rdy, 1)

            def swiglu_in(i, u0, i0, kt_next=KD):
                if not (isinstance(i, int) and i == 0):
                    split_lo(u0 + 2 * i + 1, 1, KD)
                split_lo(u0 + 2 * i + 2, 0, kt_next)
                gate_out(i, u0, i0)

            def slab(s, blocks=4):
                for half in range(2):
                    swiglu_in(2 * s + half, U_F1I, 0)
                ada_cols(s + 1, blocks)
            slab(0)
            with dve.Fori(1, 3) as s:
                slab(s)
            slab(3, 2)
            dve.wait_ge(mod_rdy, 5)
            gains(1, False)
            gains(2, False)
            for m in range(3):
                last = nc.vector.tensor_scalar(gate[:, m, :, :], mod[:, (3 * m + 2) * KD:(3 * m + 3) * KD, :],
                                               1.0 if m == 1 else 0.5, None, ALU.mult)
            last.then_inc(gain_rdy, 1)
            with dve.Fori(8, KF - 1) as i:
                swiglu_in(i, U_F1I, 0)
            swiglu_in(KF - 1, U_F1I, 0, kt_next=KH)

            def residual(m, j, done, a_slot, n):
                dve.wait_ge(mm_done, done)
                if j == 0:
                    dve.wait_ge(gain_rdy, 2)
                for bnk, b0, b1, i, t0 in PIECES:
                    last = nc.vector.scalar_tensor_tensor(
                        out=x[:, j, t0:t0 + b1 - b0], in0=acc[a_slot][bnk][:, b0:b1], scalar=gate[:, m, j, i:i + 1],
                        in1=x[:, j, t0:t0 + b1 - b0], op0=ALU.mult, op1=ALU.add)
                last.then_inc(x_upd, 1)
                dve.wait_ge(x_upd, n + 1)
                dve.sem_inc(acc_free[a_slot], 1)

            def swiglu_out(u0, m, x0, kt_next, norm_m):
                for j in range(KD):
                    split_lo(u0 + 2 * j + 1, 1, KH)
                    if j < KD - 1:
                        split_lo(u0 + 2 * j + 2, 0, KH)
                    elif kt_next:
                        split_lo(u0 + 2 * j + 2, 0, kt_next)
                    if j > 0:
                        add_squares(norm_m, j - 1, ssq_h)
                    residual(m, j, u0 + 2 * j + 2, j % 2, x0 + j)
                add_squares(norm_m, KD - 1, ssq_h)

            swiglu_out(U_F1O, 0, 0, KD, 1)
            norm(1)

            def taps(n, a_slot):
                dve.wait_ge(cv_rdy, n + 1)
                a = acc[2 if n == 2 else a_slot]
                tile = qkv_tile(n)
                before, after = (vec[:, R_DNC + 12 * w + tile:R_DNC + 12 * w + tile + 1] for w in (0, 2))
                for step, (bnk, b0, b1, t0, tap) in enumerate((
                        (0, 0, TP - 1, 1, before), (0, TP, TH, TP + 1, before), (1, 0, TH - 1, TH + 1, before),
                        (0, 1, TP, 0, after), (0, TP + 1, TH, TP, after), (1, 0, TH, TH - 1, after))):
                    ins = nc.vector.scalar_tensor_tensor(out=cv[:, t0:t0 + b1 - b0], in0=a[bnk][:, b0:b1], scalar=tap,
                                                         in1=cv[:, t0:t0 + b1 - b0], op0=ALU.mult, op1=ALU.add)
                    if step in (2, 5):
                        link(ins)
                dve.sem_inc(acc_free[a_slot], 1)
                dve.sem_inc(uc_rdy, 1)

            G = gsm

            def gates_first():
                dve.wait_ge(ab_tr, 1)
                dve.wait_ge(in_adt, 32)
                ab4 = G["ab"][:, :].rearrange("p (c a h) -> p a c h", c=NC, a=4)
                link(nc.vector.tensor_copy(G["ab"][:, :], ps[6][:, 0:NC * NAB]))
                for d in range(2):
                    dtb = G["adt"][:, 8 + 4 * d:12 + 4 * d].rearrange("p (a h) -> p a h", a=1).to_broadcast([P, NC, HEADS])
                    last = nc.vector.tensor_tensor(G["g"][:, d], ab4[:, 2 * d], dtb, ALU.add)
                link(last)
                link(nc.vector.tensor_scalar(G["t2"][:, :, :, :], G["g"][:, :, :, :], -1.0, None, ALU.mult))
                nc.vector.tensor_tensor(G["t1"][:, :, :, :], G["g"][:, :, :, :], G["t2"][:, :, :, :], ALU.min
                                        ).then_inc(ab_rdy, 1)
                for d in range(2):
                    nc.vector.tensor_scalar(G["t3"][:, d], ab4[:, 2 * d + 1], -1.0, None, ALU.mult).then_inc(ab_rdy, 1)
                dve.wait_ge(ab_rdy, 3)
                link(nc.vector.tensor_scalar(G["t2"][:, :, :, :], G["g"][:, :, :, :], 0.0, None, ALU.max))

            def gates_second():
                dve.wait_ge(act_g, 4)
                link(nc.vector.tensor_tensor(G["t2"][:, :, :, :], G["t2"][:, :, :, :], G["t1"][:, :, :, :], ALU.add))
                for d in range(2):
                    A = G["adt"][:, 4 * d:4 * d + 4].rearrange("p (a h) -> p a h", a=1).to_broadcast([P, NC, HEADS])
                    last = nc.vector.tensor_tensor(G["g"][:, d], G["t2"][:, d], A, ALU.mult)
                link(last)
                nc.vector.tensor_scalar(G["g"][:, :, :, :], G["g"][:, :, :, :], -1.0, None, ALU.mult
                                        ).then_inc(dve_g, 1)
                link(nc.vector.tensor_scalar(G["t3"][:, :, :, :], G["beta"][:, :, :, :], 1.0, None, ALU.add))
                link(nc.vector.reciprocal(G["beta"][:, :, :, :], G["t3"][:, :, :, :]))

            def gates_third():
                dve.wait_ge(gsum, 1)
                flat2 = lambda t, d: t[:, d].rearrange("p c h -> p (c h)")
                for d in range(2):
                    nc.vector.tensor_copy(flat2(G["gc"], d), ps[7][:, 32 * d:32 * d + 20])
                    last = nc.vector.tensor_copy(flat2(G["gt"], d), ps[7][:, 64 + 32 * d:64 + 32 * d + 20])
                link(last)
                nc.vector.tensor_scalar(G["ngc"][:, :, :, :], G["gc"][:, :, :, :], -1.0, None, ALU.mult)
                link(nc.vector.tensor_tensor(G["t2"][:, :, :, :], G["gt"][:, :, :, :], G["gc"][:, :, :, :],
                                             ALU.subtract))
                dve.sem_inc(dve_g, 1)

            def prepare(n, d):
                dve.wait_ge(kk_rdy[d], n + 1)
                dve.wait_ge(dt_rdy[d], n + 1)
                if n > 0:
                    dve.wait_ge(st_lt[d], 16 * n)
                    dve.wait_ge(st_qk[d], 16 * (3 * n - 2))
                for h in range(HEADS):
                    last = nc.vector.scalar_tensor_tensor(
                        out=LTp[d][:, h, :], in0=ps[6][:, h * P:h * P + P], scalar=G["beta"][:, d, chunk(n, d), h:h + 1],
                        in1=DT[d][:, h, :], op0=ALU.mult, op1=ALU.mult)
                last.then_inc(lt_rdy[d], 1)
                nc.vector.tensor_tensor(flat(QKp[d]), ps[7][:, :], flat(DT[d]), ALU.mult).then_inc(qk_rdy[d], 1)

            def sub_start(b):
                dve.wait_ge(pk_in, (64, 128, 160)[b])
                if b == 0:
                    dve.wait_ge(in_tri, 48)
                else:
                    dve.wait_ge(st_rt[0], 64 * b)
                    dve.wait_ge(st_rt[1], 64 * b)
                u, neg, xs, mask = (sub[n] for n in ("u", "n", "x", "mask"))
                half = P // 2
                nc.vector.tensor_tensor(neg[0:half, :, :], u[0:half, :, :], mask[0:half, :, :], ALU.mult)
                nc.vector.tensor_tensor(neg[half:P, :, :], u[half:P, :, :].rearrange("p a b -> p b a"),
                                        mask[half:P, :, :], ALU.mult)
                link(nc.vector.tensor_scalar(xs[:, :, :], mask[:, :, :], 0.0, None, ALU.max))

            def sub_rows(j1, j0):
                neg, xs, tmp = (sub[n] for n in ("n", "x", "tmp"))
                for j in range(j1, j0 - 1, -1):
                    w = BS - 1 - j
                    link(nc.vector.tensor_tensor(
                        tmp[:, 0:w, 0:w], neg[:, j:j + 1, j + 1:BS].to_broadcast([P, w, w]),
                        xs[:, j + 1:BS, j + 1:BS].rearrange("p k i -> p i k"), ALU.mult))
                    link(nc.vector.tensor_reduce(xs[:, j, j + 1:BS], tmp[:, 0:w, 0:w], mybir.AxisListType.X, ALU.add))

            def sub_end():
                nc.vector.tensor_copy(sub["xt"][:, :, :], sub["x"][:, :, :].rearrange("p a b -> p b a")
                                      ).then_inc(solved, 1)

            flat = lambda t: t[:, :, :].rearrange("p h j -> p (h j)")
            for n in range(28):
                u = U_MI + n + 1
                if n == 8:
                    dve.wait_ge(wab_h, 1)
                    nc.vector.tensor_tensor(wab_2[:, :, 1, :], wab[:, :, :], wab_2[:, :, 0, :].bitcast(F32), ALU.subtract
                                            ).then_inc(wab_rdy, 1)
                if n < 2:
                    split_lo(u + 1, n % 2, KD)
                elif 2 < n < 27:
                    split_lo(u, (n + 1) % 2, KD)
                a_slot = n % 2
                if n == 10:
                    dve.wait_ge(in_tri, 48)
                    nc.vector.tensor_copy(negb[:, :, :], negf[:, :, :])
                    link(nc.vector.tensor_copy(identb[:, :], ident[:, :]))
                if n == 13:
                    gates_first()
                if 0 <= n - PREP0 - 2 < GROUPS_DN:
                    prepare(*divmod(n - PREP0 - 2, 2))
                if n == 15:
                    gates_third()
                if n < 12:
                    taps(n, a_slot)
                elif n < 16:
                    pass
                elif n % 3 == 2:
                    m = (n - 16) // 3
                    dve.wait_ge(mm_done, U_MI + n + 1)
                    dve.wait_ge(cc_rdy, m + 1)
                    for b in range(2):
                        last = nc.vector.tensor_tensor(uu[:, b * TH:b * TH + TH], cc[:, b * TH:b * TH + TH],
                                                       acc[a_slot][b], ALU.mult)
                    last.then_inc(u_rdy, 1)
                    dve.wait_ge(u_rdy, m + 1)
                    dve.sem_inc(acc_free[a_slot], 1)
                    if m == 0:
                        dve.wait_ge(qs_rdy, 12)
                    tap = [vec[:, R_CONV + 4 * w + m:R_CONV + 4 * w + m + 1] for w in range(3)]
                    link(nc.vector.tensor_scalar(cv[:, :], uu[:, :], tap[1], None, ALU.mult))
                    for w in (0, 2):
                        for t0, t1, far in ((0, TP, 1), (TP, T, GRID_W)):
                            o = slice(t0 + far, t1) if w == 0 else slice(t0, t1 - far)
                            i = slice(t0, t1 - far) if w == 0 else slice(t0 + far, t1)
                            ins = nc.vector.scalar_tensor_tensor(out=cv[:, o], in0=uu[:, i], scalar=tap[w],
                                                                 in1=cv[:, o], op0=ALU.mult, op1=ALU.add)
                        link(ins)
                elif n % 3 == 0:
                    m = (n - 16) // 3
                    dve.wait_ge(mm_done, U_MI + n + 1)
                    for b in range(2):
                        last = nc.vector.tensor_tensor(yc[:, m, b * TH:b * TH + TH], cv[:, b * TH:b * TH + TH],
                                                       acc[a_slot][b], ALU.mult)
                    last.then_inc(y_rdy, 1)
                    dve.wait_ge(y_rdy, m + 1)
                    dve.sem_inc(acc_free[a_slot], 1)
                if 12 <= n < 16:
                    k = n - 12
                    dve.wait_ge(st_rdy, k + 1)
                    link(nc.vector.reciprocal(ss[:, k, :], ss[:, k, :]))
                    nc.vector.tensor_tensor(qkv[:, 4 + k, :], qkv[:, 4 + k, :], ss[:, k, :], ALU.mult
                                            ).then_inc(qn_rdy, 1)
                if n == 13:
                    gates_second()
                if n == PREP0 + 7:
                    sub_start(0)
                    sub_rows(BS - 2, 0)
                    sub_end()
                if n == PREP0 + 10:
                    sub_start(1)
                    sub_rows(BS - 2, 0)
                    sub_end()
            for t in range(NC):
                dve.wait_ge(tok_tr, 2 * t + 2)
                if t == 0:
                    for d in range(2):
                        dve.wait_ge(st_lt[d], 16 * NC)
                        dve.wait_ge(st_qk[d], 16 * (3 * NC - 2))
                nc.vector.tensor_copy(vtok[:, t, :], ps[1][:, :]).then_inc(tok_evB, 1)

            for j in range(2):
                split_lo(U_MO + j, j, KD)

            bank = [[ps[4 * d + i] for i in range(4)] for d in range(2)]
            b3 = lambda t: t[:, :].rearrange("p (h j) -> p h j", h=HEADS)
            s_of = lambda n, d: {0: None, 1: Sc[d], 2: Sa[d], 3: Sc[d], 4: Sa[d]}[n]

            def o_add(i):
                c0 = ODONE[i]
                dve.wait_ge(osq_rdy, i + 1)
                if i == 0:
                    dve.wait_ge(oq_rdy, HEADS)
                nc.vector.tensor_tensor(osq[i % 3][:, :, :], osq[i % 3][:, :, :], qkv[:, 0:4, c0 * P:c0 * P + P], ALU.add
                                        ).then_inc(oq_rdy, 1)

            for n in range(-1, NC):
                if n >= 0:
                    for d in range(2):
                        dve.wait_ge(v_mm[d], n + 1)
                        if n == 0:
                            dve.wait_ge(gates, 1)
                        beta4 = G["beta"][:, d, chunk(n, d), :].rearrange("p (h a) -> p h a", a=1).to_broadcast(
                            [P, HEADS, P])
                        nc.vector.tensor_tensor(VN[d][:, :, :], b3(bank[d][1]), beta4, ALU.mult).then_inc(vn_rdy[d], 1)
                    if n == NC - 1:
                        for i in range(EARLY):
                            o_add(i)
                        dve.wait_ge(nt_rdy[0], 3 * NC)
                        dve.wait_ge(nt_rdy[1], 3 * NC)
                        dve.wait_ge(w_mm[0], NC - 1)
                        for k in range(4):
                            dve.wait_ge(yh_rdy, k + 1)
                            nc.vector.tensor_tensor(h_lo[:, k, :], yc[:, k, :], h_hi[:, k, :].bitcast(F32),
                                                    ALU.subtract).then_inc(yl_rdy, 1)
                        dve.wait_ge(ort_rdy, 1)
                        nc.vector.reciprocal(rc[:, 0:HEADS * EARLY], rc[:, 0:HEADS * EARLY]).then_inc(orr_rdy, 1)
                    for d in range(2):
                        c0 = chunk(n, d)
                        if n < NC - 1:
                            dve.wait_ge(s_mm[d], n + 1)
                            s_in, s_new = s_of(n, d), (Sb if n == 0 else Sa if n in (1, 3) else Sc)[d]
                            if n == 0:
                                nc.vector.tensor_copy(flat(s_new), bank[d][1][:, :]).then_inc(s_rdy[d], 1)
                            else:
                                for h in range(HEADS):
                                    last = nc.vector.scalar_tensor_tensor(
                                        out=s_new[:, h, :], in0=s_in[:, h, :], scalar=G["gl"][:, d, c0, h:h + 1],
                                        in1=bank[d][1][:, h * P:h * P + P], op0=ALU.mult, op1=ALU.add)
                                last.then_inc(s_rdy[d], 1)
                        dve.wait_ge(o_mm[d], n + 1)
                        dst = ot[:, :, c0 * P:c0 * P + P]
                        first = d == 0 if c0 == 0 or chunk(n, 0) == chunk(n, 1) else n < (c0 if d else NC - c0)
                        if first:
                            nc.vector.tensor_copy(dst, b3(bank[d][2])).then_inc(o_read[d], 1)
                        else:
                            if c0 == 0:
                                dve.wait_ge(o_read[0], 1)
                            else:
                                dve.wait_ge(o_read[1 - d], (NC - c0 if d == 0 else c0) + 1)
                            nc.vector.tensor_tensor(dst, dst, b3(bank[d][2]), ALU.add).then_inc(o_read[d], 1)
                if n < NC - 1:
                    for m in range(LEVELS):
                        for d in range(2):
                            dve.wait_ge(tr_mm[d], 3 * (n + 1) + m + 1)
                            if m < LEVELS - 1:
                                nc.vector.tensor_tensor(flat(Tm[d]), flat(Tm[d]), bank[d][0][:, :], ALU.add
                                                        ).then_inc(t_rdy[d], 1)
                            R = Rm[(n + 1) % 2][d]
                            dve.wait_ge(rr_rdy[d], 4 * (n + 1) + m + 1)
                            nc.vector.tensor_tensor(flat(R), flat(R), bank[d][2][:, :], ALU.add).then_inc(rr_rdy[d], 1)
                        if m == 1 and n >= 0:
                            for d in range(2):
                                c0 = chunk(n + 1, d)
                                dve.wait_ge(w_mm[d], n + 1)
                                if n > 0:
                                    dve.wait_ge(v_mm[d], n + 1)
                                nc.vector.tensor_tensor(flat(VD[d]), vtok[:, c0, :], bank[d][1][:, :], ALU.subtract
                                                        ).then_inc(wt_rdy[d], 1)
                        i = 3 * n + m
                        if i == 0:
                            sub_start(2)
                        if 0 <= i < 5:
                            sub_rows(BS - 2 - 3 * i, BS - 4 - 3 * i)
                        if i == 5:
                            sub_end()

            def o_low(i):
                c0 = ODONE[i]
                dve.wait_ge(yh_rdy, 4 + i + 1)
                nc.vector.tensor_tensor(h_lo[:, 4:8, c0 * P:c0 * P + P], ot[:, :, c0 * P:c0 * P + P],
                                        h_hi[:, 4:8, c0 * P:c0 * P + P].bitcast(F32), ALU.subtract).then_inc(yl_rdy, 1)

            def o_scale(i):
                c0 = ODONE[i]
                oc = ot[:, :, c0 * P:c0 * P + P]
                if i < EARLY:
                    dve.wait_ge(oz_rdy, i + 2)
                dve.wait_ge(ob_mm, i + 1)
                nc.vector.tensor_tensor(oc, oc, b3(ps[4 + i % 3]), ALU.mult).then_inc(on_rdy, 1)

            dve.wait_ge(oz_rdy, 1)
            for i in range(EARLY, NC):
                o_add(i)
            for i in range(EARLY, NC):
                c0 = ODONE[i]
                oc = ot[:, :, c0 * P:c0 * P + P]
                dve.wait_ge(osq_rdy, i + 1)
                last = nc.vector.tensor_tensor(oc, oc, zs[:, :, c0 * P:c0 * P + P], ALU.mult)
            link(last)
            for i in range(EARLY):
                o_scale(i)
            dve.wait_ge(ort_rdy, 2)
            nc.vector.reciprocal(rc[:, HEADS * EARLY:], rc[:, HEADS * EARLY:]).then_inc(orr_rdy, 1)
            for i in range(EARLY):
                o_low(i)
            for i in range(EARLY, NC):
                o_scale(i)
            for i in range(EARLY, NC):
                o_low(i)
            for j in range(KD):
                u = U_MO + j + 1
                if j > 0:
                    split_lo(u, u % 2, KD)
                if j > 0:
                    add_squares(2, j - 1, ssq_g, sq_g)
                residual(1, j, U_MO + j + 1, j % 2, KD + j)
            add_squares(2, KD - 1, ssq_g, sq_g)
            norm(2)
            swiglu_in(0, U_F2I, KF)
            with dve.Fori(1, KF - 1) as i:
                swiglu_in(i, U_F2I, KF)
            swiglu_in(KF - 1, U_F2I, KF, kt_next=KH)
            swiglu_out(U_F2O, 2, 2 * KD, None, 3)
            dve.wait_ge(y_rt, 1)
            nc.vector.reciprocal(rfin[:, :], rfin[:, :]).then_inc(y_rt, 1)
            dve.wait_ge(y_rt, 2)
            dve.wait_ge(y_ev, KD)
            for t in range(0, NC, 2):
                nc.vector.tensor_scalar(yo[:, t, :], yo[:, t, :], rfin[:, t:t + 1], None, ALU.mult).then_inc(y_fin, 1)

        @block.gpsimd
        def _(pool):
            def norm(m):
                pool.wait_ge(r_rdy, 2 * m + 2)
                for k in range(1, KD):
                    nc.gpsimd.tensor_tensor(tn[:, k, :], x[:, k, :], rinv[:, :], ALU.mult).then_inc(tnp_rdy, 1)

            norm(0)
            norm(1)
            G = gsm
            bc = lambda t, d, c0: t[:, d, c0, :].rearrange("p (h a) -> p h a", a=1).to_broadcast([P, HEADS, P])
            rep = lambda m: m.rearrange("p (a j) -> p a j", a=1).to_broadcast([P, HEADS, P])
            pool.wait_ge(gates, 1)
            pool.wait_ge(in_tri, 48)

            def decayed_qk(n, d):
                c0 = chunk(n, d)
                pool.wait_ge(erow_rdy[d], n)
                pool.wait_ge(qn_rdy, 4)
                if n > 1:
                    pool.wait_ge(st_qk[d], 16 * (3 * n - 2))
                nc.gpsimd.tensor_tensor(qgp[d][:, :, :], qkv[:, 0:4, c0 * P:c0 * P + P], Erow[d][:, :, :], ALU.mult)
                nc.gpsimd.tensor_tensor(kep[d][:, :, :], qkv[:, 4:8, c0 * P:c0 * P + P], Erow[d][:, :, :], ALU.mult
                                        ).then_inc(qg_rdy[d], 1)

            for g in range(GROUPS_DN + 1):
                n, d = divmod(g, 2)
                if g < GROUPS_DN:
                    if n > 0:
                        pool.wait_ge(lt_rdy[d], n)
                        pool.wait_ge(qk_rdy[d], n)
                    nc.gpsimd.tensor_tensor(gtri[d][:, :, :], rep(tri[:, d, :]), bc(G["g"], d, chunk(n, d)), ALU.mult
                                            ).then_inc(gtri_rdy[d], 1)
                if g > 2:
                    decayed_qk(*divmod(g - 1, 2))

            pool.wait_ge(z_rdy, 4)
            nc.gpsimd.tensor_tensor(zs[:, :, :], zs[:, :, :], vec[:, R_DNN:R_DNN + 1].rearrange(
                "p (a b) -> p a b", a=1).to_broadcast([P, HEADS, T]), ALU.mult).then_inc(oz_rdy, 1)

            pool.wait_ge(in_lev, 32)
            pool.wait_ge(mm_done, U_MO)
            blk4 = blk[:, :].rearrange("p (a b c) -> p a b c", a=1, b=BPC).to_broadcast([P, HEADS, BPC, BS])

            def expand(dst, n, d, kind):
                src = rt16[d][:, n % 2, kind, :].rearrange("p (h a c) -> p h a c", h=HEADS, a=1)
                return nc.gpsimd.tensor_tensor(dst[:, :, :].rearrange("p h (b c) -> p h b c", c=BS),
                                               src.to_broadcast([P, HEADS, BPC, BS]), blk4, ALU.mult)

            def mask(n, d, m):
                i = 3 * n + m
                if m == 0:
                    pool.wait_ge(in_lt[d], 16 * (2 * n + 1))
                if i > 1:
                    pool.wait_ge(x_mm[d], i - 1)
                nc.gpsimd.tensor_tensor((NTa, NTb)[i % 2][d][:, :, :], LT[d][:, :, :],
                                        rep(lev[:, LEVELS * d + m, :]), ALU.mult).then_inc(nt_rdy[d], 1)

            for n in range(NC):
                for d in range(2):
                    pool.wait_ge(in_rt[n % 2][d], 32 * (n // 2 + 1))
                    if n > 0:
                        pool.wait_ge(x_mm[d], 3 * n)
                    expand(Tm[d], n, d, 1).then_inc(t_rdy[d], 1)
                    mask(n, d, 0)
                for d in range(2):
                    if n > 0:
                        pool.wait_ge(rr_rdy[d], 4 * n)
                    if n > 1:
                        pool.wait_ge(v_mm[d], n - 1)
                    expand(Rm[n % 2][d], n, d, 0).then_inc(rr_rdy[d], 1)
                    mask(n, d, 1)
                if n == 0:
                    pool.wait_ge(tok_evA, NC)
                for d in range(2):
                    mask(n, d, 2)
                for d in range(2):
                    kt = ktok[:, chunk(n, d), :].rearrange("p (h j) -> p h j", h=HEADS)
                    if n < NC - 1:
                        if n > 0:
                            pool.wait_ge(s_mm[d], n)
                        nc.gpsimd.tensor_tensor(kg[d][:, :, :], kt, bc(G["kgs"], d, chunk(n, d)), ALU.mult
                                                ).then_inc(kg_rdy[d], 1)
            pool.wait_ge(o_read[0], NC - 1)
            pool.wait_ge(o_read[1], NC - 1)
            for i in range(EARLY):
                oc = ot[:, :, ODONE[i] * P:ODONE[i] * P + P]
                pool.wait_ge(osq_rdy, i + 1)
                nc.gpsimd.tensor_tensor(oc, oc, zs[:, :, ODONE[i] * P:ODONE[i] * P + P], ALU.mult).then_inc(oz_rdy, 1)
            norm(2)


_INS = ["x_prompt", "x_sample", "state_dn_fwd", "state_dn_bwd", "c", "c_ctx", "w_ada", "b_ada", "norm_ffn1",
        "w_ffn1_in", "w_ffn1_out", "norm_mix", "w_mix_in", "conv_w", "dn_conv_w", "dn_a_log", "dn_dt_bias", "dn_norm",
        "w_mix_out", "norm_ffn2", "w_ffn2_in", "w_ffn2_out", "norm_final"]
_OUTS = [(1, TP, D), (1, TS, D), (1, 1, HEADS, P, P), (1, 1, HEADS, P, P)]


def kernel(**inputs):
    import concourse.bacc as bacc
    from concourse.bass_utils import run_bass_kernel_spmd

    nc = bacc.Bacc("TRN2", target_bir_lowering=False, num_devices=1)
    arrays, args = {}, []
    for name in _INS:
        a = np.ascontiguousarray(inputs[name])
        arrays[f"in_{name}"] = a
        args.append(nc.dram_tensor(f"in_{name}", a.shape, mybir.dt.from_np(a.dtype), kind="ExternalInput").ap())
    arrays["in_consts"] = constants()
    args.append(nc.dram_tensor("in_consts", (P, NCONST), F32, kind="ExternalInput").ap())
    for i, shape in enumerate(_OUTS):
        args.append(nc.dram_tensor(f"out_{i}", shape, F32, kind="ExternalOutput").ap())
    hybrid_layer(nc, *args)
    r = run_bass_kernel_spmd(nc, [arrays], core_ids=[0])
    return tuple(r.results[0][f"out_{i}"] for i in range(len(_OUTS)))
```
